# Optimizing a Trainium2 kernel written in Bass

```python
import math
import jax, jax.numpy as jnp
from jax import lax
import numpy as np

D_MODEL = 1024
BATCH = 1
SEQ = 256
DEPTH = 1

HEAD_DIM = 64
ATTN_SCALE = HEAD_DIM ** -0.5
SWA_Q_HEADS = 8
SWA_KV_HEADS = 2
SWA_GROUP = SWA_Q_HEADS // SWA_KV_HEADS
SWA_WINDOW = 128
SWA_BLOCK = 128
MOBA_HEADS = 8
MOBA_BLOCK = 256
MOBA_TOPK = 3
MOBA_Q_CHUNK = 32
NUM_BUCKETS = 32
MAX_EXACT = NUM_BUCKETS // 2
MAX_DISTANCE = 2048
N_ATTN_HEADS = SWA_Q_HEADS + MOBA_HEADS
SWA_Q_W = SWA_Q_HEADS * HEAD_DIM
SWA_KV_W = SWA_KV_HEADS * HEAD_DIM
MOBA_W = MOBA_HEADS * HEAD_DIM
N_BRANCHES = 2
IN_WIDTHS = (SWA_Q_W, SWA_KV_W, SWA_KV_W, MOBA_W, MOBA_W, MOBA_W, D_MODEL, D_MODEL)
IN_TOTAL = SWA_Q_W + 2 * SWA_KV_W + 3 * MOBA_W + N_BRANCHES * D_MODEL
D_FF = 4 * D_MODEL
N_MOD = 6
RMS_EPS = 1e-6


def rmsnorm(x, g):
    xf = x.astype(jnp.float32)
    y = xf * lax.rsqrt(jnp.mean(xf * xf, axis=-1, keepdims=True) + RMS_EPS)
    return (y * g.astype(jnp.float32)).astype(x.dtype)

def modulate(h, shift, scale):
    return h * (1.0 + scale[:, None, :]) + shift[:, None, :]

def t5_bucket(dist):
    n = jnp.maximum(dist, 0)
    nf = jnp.maximum(n, 1).astype(jnp.float32)
    large = MAX_EXACT + (jnp.log(nf / MAX_EXACT) / math.log(MAX_DISTANCE / MAX_EXACT)
                         * (NUM_BUCKETS - MAX_EXACT)).astype(jnp.int32)
    large = jnp.minimum(large, NUM_BUCKETS - 1)
    return jnp.where(n < MAX_EXACT, n, large)

def swa_attention(q, k, v, sinks, rel_bias):
    B, S = q.shape[0], q.shape[1]
    L = SWA_BLOCK
    nb = S // L
    qb = q.reshape(B, nb, L, SWA_KV_HEADS, SWA_GROUP, HEAD_DIM)
    kb = k.reshape(B, nb, L, SWA_KV_HEADS, HEAD_DIM)
    vb = v.reshape(B, nb, L, SWA_KV_HEADS, HEAD_DIM)
    pad = ((0, 0), (1, 0), (0, 0), (0, 0), (0, 0))
    kk = jnp.concatenate([jnp.pad(kb, pad)[:, :-1], kb], axis=2)
    vv = jnp.concatenate([jnp.pad(vb, pad)[:, :-1], vb], axis=2)
    s = jnp.einsum('bnqhgd,bnkhd->bnhgqk', qb, kk).astype(jnp.float32) * ATTN_SCALE
    i = jnp.arange(L)[:, None] + L
    j = jnp.arange(2 * L)[None, :]
    dist = i - j
    bias = rel_bias[t5_bucket(dist)][..., :SWA_Q_HEADS].astype(jnp.float32)
    bias = bias.transpose(2, 0, 1).reshape(SWA_KV_HEADS, SWA_GROUP, L, 2 * L)
    kabs = jnp.arange(nb)[:, None, None] * L - L + j[None]
    mask = ((dist >= 0) & (dist < SWA_WINDOW))[None] & (kabs >= 0)
    s = jnp.where(mask[None, :, None, None], s + bias, -jnp.inf)
    sink = sinks.astype(jnp.float32).reshape(SWA_KV_HEADS, SWA_GROUP)[None, None, :, :, None, None]
    m = jnp.maximum(jnp.max(s, axis=-1, keepdims=True), sink)
    p = jnp.exp(s - m)
    p = p / (jnp.sum(p, axis=-1, keepdims=True) + jnp.exp(sink - m))
    o = jnp.einsum('bnhgqk,bnkhd->bnqhgd', p.astype(v.dtype), vv)
    return o.reshape(B, S, SWA_Q_HEADS * HEAD_DIM)

def moba_attention(q, k, v, rel_bias):
    B, S = q.shape[0], q.shape[1]
    H = MOBA_HEADS
    MB = MOBA_BLOCK
    nblk = (S + MB - 1) // MB
    Sp = nblk * MB
    k_eff = max(1, min(MOBA_TOPK, nblk - 1))
    padw = ((0, 0), (0, Sp - S), (0, 0), (0, 0))
    q = jnp.pad(q, padw)
    k = jnp.pad(k, padw)
    v = jnp.pad(v, padw)
    qh = q.transpose(0, 2, 1, 3)
    kb = k.reshape(B, nblk, MB, H, HEAD_DIM).transpose(0, 3, 1, 2, 4)
    vb = v.reshape(B, nblk, MB, H, HEAD_DIM).transpose(0, 3, 1, 2, 4)
    kmean = jnp.mean(kb.astype(jnp.float32), axis=3)
    gate = jnp.einsum('bhsd,bhnd->bhsn', qh.astype(jnp.float32), kmean)
    qblk = jnp.arange(Sp) // MB
    past = jnp.arange(nblk)[None, :] < qblk[:, None]
    gate = jnp.where(past, gate, -jnp.inf)
    _, idx = lax.top_k(gate, k_eff)
    valid = jnp.arange(k_eff)[None, :] < qblk[:, None]
    table_b = rel_bias[:, SWA_Q_HEADS:].T.astype(jnp.float32)
    bi = jnp.arange(B)[:, None, None, None]
    hi = jnp.arange(H)[None, :, None, None]
    hi5 = hi[..., None]
    n_chunks = Sp // MOBA_Q_CHUNK

    def chunk_fn(ci):
        start = ci * MOBA_Q_CHUNK
        q_c = lax.dynamic_slice_in_dim(qh, start, MOBA_Q_CHUNK, axis=2)
        idx_c = lax.dynamic_slice_in_dim(idx, start, MOBA_Q_CHUNK, axis=2)
        valid_c = lax.dynamic_slice_in_dim(valid, start, MOBA_Q_CHUNK, axis=0)
        qpos = start + jnp.arange(MOBA_Q_CHUNK)
        own = start // MB
        k_sel = kb[bi, hi, idx_c]
        v_sel = vb[bi, hi, idx_c]
        s_past = jnp.einsum('bhqd,bhqrkd->bhqrk', q_c, k_sel).astype(jnp.float32) * ATTN_SCALE
        kpos_past = idx_c[..., None] * MB + jnp.arange(MB)
        bias_past = table_b[hi5, t5_bucket(qpos[:, None, None] - kpos_past)]
        s_past = jnp.where(valid_c[None, None, :, :, None], s_past + bias_past, -jnp.inf)
        s_past = s_past.reshape(B, H, MOBA_Q_CHUNK, k_eff * MB)
        k_own = lax.dynamic_index_in_dim(kb, own, axis=2, keepdims=False)
        v_own = lax.dynamic_index_in_dim(vb, own, axis=2, keepdims=False)
        s_own = jnp.einsum('bhqd,bhkd->bhqk', q_c, k_own).astype(jnp.float32) * ATTN_SCALE
        dist_own = qpos[:, None] - (own * MB + jnp.arange(MB))[None, :]
        bias_own = table_b[:, t5_bucket(dist_own)]
        s_own = jnp.where(dist_own >= 0, s_own + bias_own, -jnp.inf)
        p = jax.nn.softmax(jnp.concatenate([s_past, s_own], axis=-1), axis=-1)
        p_past = p[..., :k_eff * MB].reshape(B, H, MOBA_Q_CHUNK, k_eff, MB)
        p_own = p[..., k_eff * MB:]
        o = (jnp.einsum('bhqrk,bhqrkd->bhqd', p_past.astype(v_sel.dtype), v_sel)
             + jnp.einsum('bhqk,bhkd->bhqd', p_own.astype(v_own.dtype), v_own))
        return o

    out = lax.map(chunk_fn, jnp.arange(n_chunks))
    out = out.transpose(1, 0, 3, 2, 4).reshape(B, Sp, H * HEAD_DIM)
    return out[:, :S]

def first_inputs(seed: int = 0) -> dict:
    key = jax.random.key(seed)
    ks = jax.random.split(key, 16)
    f32 = jnp.float32
    nrm = lambda k, shape, s: jax.random.normal(k, shape, f32) * s
    return {
        "x": nrm(ks[0], (BATCH, SEQ, D_MODEL), 1.0),
        "c": nrm(ks[1], (BATCH, D_MODEL), 1.0),
        "ada_w": nrm(ks[2], (DEPTH, D_MODEL, N_MOD * D_MODEL), D_MODEL ** -0.5),
        "ada_b": nrm(ks[3], (DEPTH, N_MOD * D_MODEL), 0.02),
        "norm1_g": 1.0 + nrm(ks[4], (DEPTH, D_MODEL), 0.02),
        "norm2_g": 1.0 + nrm(ks[5], (DEPTH, D_MODEL), 0.02),
        "w_in": nrm(ks[6], (DEPTH, D_MODEL, IN_TOTAL), D_MODEL ** -0.5),
        "attn_sinks": nrm(ks[7], (DEPTH, SWA_Q_HEADS), 0.5),
        "rel_bias": nrm(ks[8], (NUM_BUCKETS, N_ATTN_HEADS), 0.5),
        "w_branch_a": nrm(ks[9], (DEPTH, SWA_Q_W, D_MODEL), SWA_Q_W ** -0.5),
        "w_branch_b": nrm(ks[10], (DEPTH, MOBA_W, D_MODEL), MOBA_W ** -0.5),
        "w_out": nrm(ks[11], (DEPTH, D_MODEL, D_MODEL), D_MODEL ** -0.5),
        "w_mlp_in": nrm(ks[12], (DEPTH, D_MODEL, D_FF), D_MODEL ** -0.5),
        "w_mlp_out": nrm(ks[13], (DEPTH, D_FF, D_MODEL), D_FF ** -0.5),
        "final_g": 1.0 + nrm(ks[14], (D_MODEL,), 0.02),
    }

def first_block(x, c, ada_w, ada_b, norm1_g, norm2_g, w_in, attn_sinks, rel_bias,
              w_branch_a, w_branch_b, w_out, w_mlp_in, w_mlp_out, final_g):
    B, S = x.shape[0], x.shape[1]
    offsets = []
    acc = 0
    for w in IN_WIDTHS[:-1]:
        acc += w
        offsets.append(acc)
    cs = jax.nn.silu(c)
    for l in range(DEPTH):
        mod = cs @ ada_w[l] + ada_b[l]
        shift1, scale1, gate1, shift2, scale2, gate2 = jnp.split(mod, N_MOD, axis=-1)
        h = modulate(rmsnorm(x, norm1_g[l]), shift1, scale1)
        proj = h @ w_in[l]
        qa, ka, va, qb, kb, vb, ga, gb = jnp.split(proj, offsets, axis=-1)
        ya = swa_attention(qa.reshape(B, S, SWA_Q_HEADS, HEAD_DIM),
                           ka.reshape(B, S, SWA_KV_HEADS, HEAD_DIM),
                           va.reshape(B, S, SWA_KV_HEADS, HEAD_DIM),
                           attn_sinks[l], rel_bias) @ w_branch_a[l]
        yb = moba_attention(qb.reshape(B, S, MOBA_HEADS, HEAD_DIM),
                            kb.reshape(B, S, MOBA_HEADS, HEAD_DIM),
                            vb.reshape(B, S, MOBA_HEADS, HEAD_DIM),
                            rel_bias) @ w_branch_b[l]
        merged = jax.nn.sigmoid(ga) * ya + jax.nn.sigmoid(gb) * yb
        x = x + gate1[:, None, :] * (merged @ w_out[l])
        h2 = modulate(rmsnorm(x, norm2_g[l]), shift2, scale2)
        y = jnp.square(jax.nn.relu(h2 @ w_mlp_in[l])) @ w_mlp_out[l]
        x = x + gate2[:, None, :] * y
    return rmsnorm(x, final_g)


DEPTH_2 = 2

CHUNK = 64
N_META = 16
N_A = DEPTH_2 // 2
N_B = DEPTH_2 - N_A
D_FF_2 = 2816
POOL_WINDOWS = (2, 4, 8, 16)
N_POOL_GROUPS = len(POOL_WINDOWS)
POOL_GROUP = D_MODEL // N_POOL_GROUPS
N_HEADS = 8
QK_NOPE = 64
QK_ROPE = 32
V_HEAD = 64
KV_RANK = 256
Q_RANK = 384
ROPE_THETA = 10000.0
Q_BLOCK = 128
EPS = 1e-6


def rmsnorm_2(x, g):
    xf = x.astype(jnp.float32)
    xf = xf * lax.rsqrt(jnp.mean(xf * xf, axis=-1, keepdims=True) + EPS)
    return xf.astype(x.dtype) * g

def swiglu(h, w_gate, w_up, w_down):
    return (jax.nn.silu(h @ w_gate) * (h @ w_up)) @ w_down

def chunk_ids(n):
    pos = jnp.arange(n)
    return jnp.where(pos < N_META, 0, (pos - N_META) // CHUNK + 1)

def rope_tables(n):
    inv = 1.0 / (ROPE_THETA ** (jnp.arange(0, QK_ROPE, 2, dtype=jnp.float32) / QK_ROPE))
    ang = jnp.arange(n, dtype=jnp.float32)[:, None] * inv[None, :]
    return jnp.cos(ang), jnp.sin(ang)

def apply_rope(x, cos, sin):
    xf = x.astype(jnp.float32)
    x1, x2 = xf[..., : QK_ROPE // 2], xf[..., QK_ROPE // 2:]
    out = jnp.concatenate([x1 * cos - x2 * sin, x2 * cos + x1 * sin], axis=-1)
    return out.astype(x.dtype)

def pool_mixer(h, w_group, scale):
    L = h.shape[1]
    hf = h.astype(jnp.float32)
    cs = jnp.concatenate([jnp.zeros_like(hf[:, :1]), jnp.cumsum(hf, axis=1)], axis=1)
    hi = jnp.arange(1, L + 1)
    outs = []
    for g, w in enumerate(POOL_WINDOWS):
        sl = slice(g * POOL_GROUP, (g + 1) * POOL_GROUP)
        lo = jnp.maximum(hi - w, 0)
        c = cs[..., sl]
        count = (hi - lo).astype(jnp.float32)[None, :, None]
        mean = (jnp.take(c, hi, axis=1) - jnp.take(c, lo, axis=1)) / count
        outs.append(mean - hf[..., sl])
    pooled = jnp.stack(outs, axis=2).astype(h.dtype)
    y = jnp.einsum('blgc,gcd->blgd', pooled, w_group)
    return y.reshape(h.shape) * scale

def mla_shared_kv(h, w_dkv, kv_latent_norm, w_uk, w_uv, cos, sin):
    B, L, _ = h.shape
    ckr = h @ w_dkv
    c_kv = rmsnorm_2(ckr[..., :KV_RANK], kv_latent_norm)
    k_rope = apply_rope(ckr[..., KV_RANK:], cos, sin)
    k_nope = (c_kv @ w_uk).reshape(B, L, N_HEADS, QK_NOPE)
    v = (c_kv @ w_uv).reshape(B, L, N_HEADS, V_HEAD)
    return k_nope, k_rope, v

def mla_attention(h, w_dq, q_latent_norm, w_uq, w_o, k_nope, k_rope, v, cos, sin):
    B, L, _ = h.shape
    cq = rmsnorm_2(h @ w_dq, q_latent_norm)
    q = (cq @ w_uq).reshape(B, L, N_HEADS, QK_NOPE + QK_ROPE)
    q_nope = q[..., :QK_NOPE]
    q_rope = apply_rope(q[..., QK_NOPE:], cos[:, None, :], sin[:, None, :])
    n_blk = -(-L // Q_BLOCK)
    Lp = n_blk * Q_BLOCK
    pad = ((0, 0), (0, Lp - L), (0, 0), (0, 0))
    qn_b = jnp.pad(q_nope, pad).reshape(B, n_blk, Q_BLOCK, N_HEADS, QK_NOPE).transpose(1, 0, 2, 3, 4)
    qr_b = jnp.pad(q_rope, pad).reshape(B, n_blk, Q_BLOCK, N_HEADS, QK_ROPE).transpose(1, 0, 2, 3, 4)
    qid_b = chunk_ids(Lp).reshape(n_blk, Q_BLOCK)
    kid = chunk_ids(L)
    sm_scale = 1.0 / math.sqrt(QK_NOPE + QK_ROPE)

    def block(args):
        qn, qr, qid = args
        s = (jnp.einsum('bqhd,bkhd->bhqk', qn, k_nope)
             + jnp.einsum('bqhr,bkr->bhqk', qr, k_rope)).astype(jnp.float32) * sm_scale
        mask = kid[None, :] <= qid[:, None]
        s = jnp.where(mask[None, None], s, jnp.finfo(jnp.float32).min)
        p = jax.nn.softmax(s, axis=-1).astype(v.dtype)
        return jnp.einsum('bhqk,bkhd->bqhd', p, v)

    o = lax.map(block, (qn_b, qr_b, qid_b))
    o = o.transpose(1, 0, 2, 3, 4).reshape(B, Lp, N_HEADS * V_HEAD)[:, :L]
    return o @ w_o

def second_inputs(seed: int = 0) -> dict:
    key = jax.random.key(seed)
    ks = iter(jax.random.split(key, 40))
    f32 = jnp.float32

    def nrm(shape, fan_in):
        return jax.random.normal(next(ks), shape, f32) * (fan_in ** -0.5)

    def gain(shape):
        return 1.0 + 0.1 * jax.random.normal(next(ks), shape, f32)

    return {
        "x": jax.random.normal(next(ks), (BATCH, SEQ, D_MODEL), f32),
        "meta_tokens": jax.random.normal(next(ks), (N_META, D_MODEL), f32),
        "ffn1_norm": gain((DEPTH_2, D_MODEL)),
        "ffn1_w_gate": nrm((DEPTH_2, D_MODEL, D_FF_2), D_MODEL),
        "ffn1_w_up": nrm((DEPTH_2, D_MODEL, D_FF_2), D_MODEL),
        "ffn1_w_down": nrm((DEPTH_2, D_FF_2, D_MODEL), D_FF_2),
        "mix_norm": gain((DEPTH_2, D_MODEL)),
        "ffn2_norm": gain((DEPTH_2, D_MODEL)),
        "ffn2_w_gate": nrm((DEPTH_2, D_MODEL, D_FF_2), D_MODEL),
        "ffn2_w_up": nrm((DEPTH_2, D_MODEL, D_FF_2), D_MODEL),
        "ffn2_w_down": nrm((DEPTH_2, D_FF_2, D_MODEL), D_FF_2),
        "pool_w": nrm((N_A, N_POOL_GROUPS, POOL_GROUP, POOL_GROUP), POOL_GROUP),
        "pool_scale": gain((N_A, D_MODEL)),
        "kv_in_norm": gain((D_MODEL,)),
        "w_dkv": nrm((D_MODEL, KV_RANK + QK_ROPE), D_MODEL),
        "kv_latent_norm": gain((KV_RANK,)),
        "w_uk": nrm((KV_RANK, N_HEADS * QK_NOPE), KV_RANK),
        "w_uv": nrm((KV_RANK, N_HEADS * V_HEAD), KV_RANK),
        "w_dq": nrm((N_B, D_MODEL, Q_RANK), D_MODEL),
        "q_latent_norm": gain((N_B, Q_RANK)),
        "w_uq": nrm((N_B, Q_RANK, N_HEADS * (QK_NOPE + QK_ROPE)), Q_RANK),
        "w_o": nrm((N_B, N_HEADS * V_HEAD, D_MODEL), N_HEADS * V_HEAD),
        "final_norm": gain((D_MODEL,)),
    }

def second_block(x, meta_tokens, ffn1_norm, ffn1_w_gate, ffn1_w_up, ffn1_w_down, mix_norm,
              ffn2_norm, ffn2_w_gate, ffn2_w_up, ffn2_w_down, pool_w, pool_scale,
              kv_in_norm, w_dkv, kv_latent_norm, w_uk, w_uv, w_dq, q_latent_norm, w_uq, w_o,
              final_norm):
    B = x.shape[0]
    meta = jnp.broadcast_to(meta_tokens[None].astype(x.dtype), (B, N_META, D_MODEL))
    h = jnp.concatenate([meta, x], axis=1)
    L = h.shape[1]
    cos, sin = rope_tables(L)
    shared = None
    for l in range(DEPTH_2):
        h = h + 0.5 * swiglu(rmsnorm_2(h, ffn1_norm[l]), ffn1_w_gate[l], ffn1_w_up[l], ffn1_w_down[l])
        u = rmsnorm_2(h, mix_norm[l])
        if l < N_A:
            h = h + pool_mixer(u, pool_w[l], pool_scale[l])
        else:
            j = l - N_A
            k_nope, k_rope, v = shared
            h = h + mla_attention(u, w_dq[j], q_latent_norm[j], w_uq[j], w_o[j],
                                  k_nope, k_rope, v, cos, sin)
        h = h + 0.5 * swiglu(rmsnorm_2(h, ffn2_norm[l]), ffn2_w_gate[l], ffn2_w_up[l], ffn2_w_down[l])
        if l == N_A - 1:
            shared = mla_shared_kv(rmsnorm_2(h, kv_in_norm), w_dkv, kv_latent_norm, w_uk, w_uv, cos, sin)
    out = rmsnorm_2(h, final_norm)
    return out[:, N_META:]


def setup_inputs(seed=0):
    out = dict(first_inputs(seed))
    for name, value in second_inputs(seed + 1).items():
        if name != "x":
            out[name + "_2"] = value
    return out


def reference(
    x, c, ada_w, ada_b, norm1_g, norm2_g, w_in, attn_sinks, rel_bias, w_branch_a, w_branch_b,
    w_out, w_mlp_in, w_mlp_out, final_g, meta_tokens_2, ffn1_norm_2, ffn1_w_gate_2, ffn1_w_up_2,
    ffn1_w_down_2, mix_norm_2, ffn2_norm_2, ffn2_w_gate_2, ffn2_w_up_2, ffn2_w_down_2, pool_w_2,
    pool_scale_2, kv_in_norm_2, w_dkv_2, kv_latent_norm_2, w_uk_2, w_uv_2, w_dq_2,
    q_latent_norm_2, w_uq_2, w_o_2, final_norm_2,
):
    x = first_block(
        x, c, ada_w, ada_b, norm1_g, norm2_g, w_in, attn_sinks, rel_bias, w_branch_a,
        w_branch_b, w_out, w_mlp_in, w_mlp_out, final_g,
    )
    return second_block(
        x, meta_tokens_2, ffn1_norm_2, ffn1_w_gate_2, ffn1_w_up_2, ffn1_w_down_2, mix_norm_2,
        ffn2_norm_2, ffn2_w_gate_2, ffn2_w_up_2, ffn2_w_down_2, pool_w_2, pool_scale_2,
        kv_in_norm_2, w_dkv_2, kv_latent_norm_2, w_uk_2, w_uv_2, w_dq_2, q_latent_norm_2,
        w_uq_2, w_o_2, final_norm_2,
    )


_drawn_inputs = setup_inputs


def setup_inputs(seed=0):
    import zlib

    import numpy as np

    out = dict(_drawn_inputs(seed))
    spreads = {}
    factors = {'norm1_g': 7.175,
     'norm2_g': 2.995,
     'attn_sinks': 64.0,
     'final_g': 2.682,
     'q_latent_norm_2': 5.942}
    for name, (base, spread) in spreads.items():
        noise = np.random.default_rng([zlib.crc32(name.encode()), seed]).standard_normal(out[name].shape)
        drawn = base * np.exp(spread * noise) if base else spread * noise
        out[name] = __import__('jax').numpy.asarray(drawn.astype(out[name].dtype))
    for name, factor in factors.items():
        out[name] = (out[name] * factor).astype(out[name].dtype)
    return out
```

```python
from contextlib import ExitStack
import math

import numpy as np

import concourse.bass as bass
from concourse import mybir

F32 = mybir.dt.float32
F32R = mybir.dt.float32r
ALU = mybir.AluOpType
ACT = mybir.ActivationFunctionType
AX_X = mybir.AxisListType.X

P = 128
D = 1024
KT = D // P
META = 16
SEQ = 256
T = META + SEQ
HD = 64
SWA_HEADS, SWA_KV, MOBA_HEADS = 8, 2, 8
HEADS1 = SWA_HEADS + MOBA_HEADS
WINDOW = 128
NB = 32
MAX_DISTANCE = 2048
FF1 = 4 * D // P
FF2 = 2816 // P
KVR = 256 // P
QR = 384 // P
MH, ROPE = 8, 32
QK = HD + ROPE
POOL_W = (2, 4, 8, 16)
PADC = 16
EPS = 1e-6
MASKED = -3.0e38
BIASC = 384

CH = 16
NRAW, NSPLIT = 3, 3
AHEAD = 2

W_IN_OFF = dict(qa=0, ka=512, va=640, qb=768, kb=1280, vb=1792, ga=2304, gb=3328)


def _r(a, n=P):
    return np.arange(a, a + n)


def weight_plan():
    groups = []

    def group(name, blocks, flush=False):
        groups.append((name, blocks, flush))

    def dense(name, arr, layer, tiles, nk, rows=None):
        rows = rows or (lambda kt: _r(kt * P))
        group(name, [(arr, layer, rows(kt), c) for kt in range(nk) for c in tiles])

    def ada(name, t0):
        group(name, [("ada_w", 0, _r(kt * P), _r(t * P)) for t in (t0, t0 + 1) for kt in range(KT)])

    for i in range(8):
        ada(f"ada{i}", 2 * i)
    o = W_IN_OFF
    tiles = [_r(o["ka"])]
    tiles += [np.concatenate([_r(o["qa"] + j * HD, HD), _r(o["qa"] + (j + 4) * HD, HD)]) for j in range(4)]
    tiles += [_r(o["kb"] + j * P) for j in range(4)] + [_r(o["qb"] + j * P) for j in range(4)]
    for i in range(0, 13, 2):
        dense(f"qk{i // 2}", "w_in", 0, tiles[i:i + 2], KT)
    group("va", [("w_in", 0, _r(kt * P), _r(o["va"])) for kt in range(KT)], True)
    group("vb", [("w_in", 0, _r(kt * P), _r(o["vb"] + j * P)) for kt in range(KT) for j in range(4)], True)
    for i in range(HEADS1):
        if i % 2 == 0:
            t = i
            dense(f"gate{i // 2}", "w_in", 0, [_r(o["ga"] + (t + n) * P) for n in range(2)], KT)
        ada(f"ada{8 + i}", 16 + 2 * i)
    rows_a = lambda kt: np.concatenate([_r(kt * HD, HD), _r((kt + 4) * HD, HD)])
    for i in range(4):
        t2 = [_r((2 * i + n) * P) for n in range(2)]
        dense(f"bra{i}", "w_branch_a", 0, t2, 4, rows_a)
        dense(f"brb{i}", "w_branch_b", 0, t2, 4)
    for i in range(4):
        dense(f"wout{i}", "w_out", 0, [_r((2 * i + n) * P) for n in range(2)], KT)
    for i in range(FF1 // 2):
        dense(f"mlp_in{i}", "w_mlp_in", 0, [_r((2 * i + n) * P) for n in range(2)], KT)
    for i in range(4):
        dense(f"mlp_out{i}", "w_mlp_out", 0, [_r((2 * i + n) * P) for n in range(2)], FF1)

    def gate_up(f, layer, j):
        blocks = []
        for kt in range(KT):
            blocks += [(f"{f}_w_gate_2", layer, _r(kt * P), _r(j * P)), (f"{f}_w_up_2", layer, _r(kt * P), _r(j * P))]
        group(f"{f}_{layer}_gu{j}", blocks)

    def down(f, layer):
        for i in range(4):
            dense(f"{f}_{layer}_down{i}", f"{f}_w_down_2", layer, [_r((2 * i + n) * P) for n in range(2)], FF2)

    for j in range(FF2):
        gate_up("ffn1", 0, j)
    down("ffn1", 0)
    for g in range(4):
        group(f"pool{g}", [("pool_w_2", g, _r(kt * P), _r(n * P)) for kt in range(2) for n in range(2)])
    for j in range(FF2):
        gate_up("ffn2", 0, j)
    down("ffn2", 0)
    dense("ckv", "w_dkv_2", None, [_r(0), _r(P)], KT)
    rope = _r(KVR * P, ROPE)
    swap = np.concatenate([rope[ROPE // 2:], rope[:ROPE // 2]])
    dense("krope", "w_dkv_2", None, [np.concatenate([rope, swap, rope, swap])], KT)
    for j in range(FF2):
        gate_up("ffn1", 1, j)
        if j == 3:
            for i in range(2):
                dense(f"uk{i}", "w_uk_2", None, [_r((2 * i + n) * P) for n in range(2)], KVR)
            group("uv", [("w_uv_2", None, _r(kt * P), _r(j4 * P)) for kt in range(KVR) for j4 in range(4)], True)
    down("ffn1", 1)
    dense("dq0", "w_dq_2", 0, [_r(0), _r(P)], KT)
    dense("dq1", "w_dq_2", 0, [_r(2 * P)], KT)
    head = lambda h: h * QK
    nope = [np.concatenate([_r(head(2 * j + n), HD) for n in range(2)]) for j in range(4)]
    for i in range(2):
        dense(f"uqn{i}", "w_uq_2", 0, nope[2 * i:2 * i + 2], QR)
    for i in range(2):
        rp = [_r(head(4 * i + n) + HD, ROPE) for n in range(4)]
        sw = [np.concatenate([r[ROPE // 2:], r[:ROPE // 2]]) for r in rp]
        dense(f"uqr{i}", "w_uq_2", 0, [np.concatenate(rp), np.concatenate(sw)], QR)
    for i in range(4):
        dense(f"wo{i}", "w_o_2", 0, [_r((2 * i + n) * P) for n in range(2)], 4)
    for j in range(FF2):
        gate_up("ffn2", 1, j)
    down("ffn2", 1)

    chunks, where = [[]], {}
    for name, blocks, flush in groups:
        if flush and chunks[-1]:
            chunks.append([])
        where[name] = []
        for b in blocks:
            if len(chunks[-1]) == CH:
                chunks.append([])
            where[name].append((len(chunks) - 1, len(chunks[-1])))
            chunks[-1].append(b)
    return chunks, where


def vector_plan():
    at, n = {}, 0
    for name, w in (("c", KT), ("ada_b", 6 * KT), ("norm1_g", KT), ("norm2_g", KT), ("final_g", KT),
                    ("ffn1_norm0", KT), ("ffn1_norm1", KT), ("mix_norm0", KT), ("mix_norm1", KT),
                    ("ffn2_norm0", KT), ("ffn2_norm1", KT), ("pool_scale", KT), ("kv_in_norm", KT),
                    ("final_norm", KT), ("kv_latent_norm", KVR), ("q_latent_norm", QR), ("sinks", SWA_HEADS)):
        at[name] = n
        n += w
    return at, n


def constant_plan():
    at, n = {}, 0
    for name, w in (("ident", P), ("cos", T), ("sin", T), ("mla_mask", T), ("count_fix", 4 * PADC)):
        at[name] = n
        n += w
    return at, n


def constants():
    at, n = constant_plan()
    out = np.zeros((P, n), np.float32)
    out[:, at["ident"]:at["ident"] + P] = np.eye(P, dtype=np.float32)
    inv = (1.0 / (np.float32(10000.0) ** (np.arange(0, ROPE, 2, dtype=np.float32) / ROPE))).astype(np.float32)
    ang = np.arange(T, dtype=np.float32)[None, :] * inv[:, None]
    cos, sin = np.cos(ang).astype(np.float32), np.sin(ang).astype(np.float32)
    for g in range(P // ROPE):
        r = g * ROPE
        out[r:r + ROPE, at["cos"]:at["cos"] + T] = np.concatenate([cos, cos])
        out[r:r + ROPE, at["sin"]:at["sin"] + T] = np.concatenate([-sin, sin])
    out[0:64, at["mla_mask"] + T - 64:at["mla_mask"] + T] = MASKED
    for g, w in enumerate(POOL_W):
        t = np.arange(PADC)
        out[:, at["count_fix"] + g * PADC:at["count_fix"] + (g + 1) * PADC] = w / np.minimum(t + 1, w)
    return out


def bias_constants():
    dist = 255 - np.arange(BIASC)
    n = np.maximum(dist, 0)
    half = NB // 2
    large = half + (np.log(np.maximum(n, 1).astype(np.float32) / half) / math.log(MAX_DISTANCE / half)
                    * (NB - half)).astype(np.int32)
    bucket = np.where(n < half, n, np.minimum(large, NB - 1))
    out = np.zeros((NB + 2, BIASC), np.float32)
    out[bucket, np.arange(BIASC)] = 1.0
    out[NB, (dist < 0) | (dist >= WINDOW)] = MASKED
    out[NB + 1, dist < 0] = MASKED
    sel = np.zeros((2, HEADS1), np.float32)
    sel[0, :SWA_HEADS] = 1.0
    sel[1, SWA_HEADS:] = 1.0
    return out, sel


class Counter:

    def __init__(self, sem):
        self.sem, self.value = sem, 0

    def add(self, n=1):
        self.value += n
        return (self, self.value)


class Queue:

    def __init__(self, engine, counter=None):
        self.engine, self.counter, self.passed = engine, counter, {}

    def do(self, make, after=(), signal=None):
        for token in after:
            if token is None:
                continue
            counter, value = token
            if self.passed.get(counter, 0) < value:
                self.passed[counter] = value
                self.engine.wait_ge(counter.sem, value)
        made = make(self.engine)
        if signal is False:
            return None
        counter, n = (self.counter, 1) if signal is None else signal
        made.then_inc(counter.sem, n)
        return counter.add(n)


def build_program(nc, xT, metaT, vecs, consts, bias_oh, bias_rows, wstream, scratch, outT):
    chunks, where = weight_plan()
    last_use = {}
    for name, places in where.items():
        for c, off in places:
            last_use[c] = max(last_use.get(c, 0), off)
    vat, vn = vector_plan()
    cat, cn = constant_plan()

    ctx = ExitStack()
    with ctx:
        def sb(name, shape, dt=F32, to=ctx):
            return to.enter_context(nc.sbuf_tensor("sb_" + name, shape, dt))

        def counter(name):
            return Counter(ctx.enter_context(nc.semaphore(name)))

        X = sb("X", [P, KT, T])
        xh, xl = sb("xh", [P, KT, T], F32R), sb("xl", [P, KT, T], F32R)
        raw = sb("raw", [P, NRAW, CH * P])
        whi, wlo = sb("whi", [P, NSPLIT, CH * P], F32R), sb("wlo", [P, NSPLIT, CH * P], F32R)
        vec = sb("vec", [P, vn])
        con = sb("con", [P, cn])
        mean_ones = sb("mean_ones", [P, 3, P])
        sumsq, sq = sb("sumsq", [P, T]), sb("sq", [P, 2, T])
        root, rstd, rstd2 = sb("root", [P, T]), sb("rstd", [P, T]), sb("rstd2", [P, T])
        mod, csil, g1m = sb("mod", [P, 6 * KT]), sb("csil", [P, KT]), sb("g1m", [P, 2 * KT])
        gu, hidf, tmp = sb("gu", [P, 2, 2, T]), sb("hidf", [P, 2, 2 * SEQ]), sb("tmp", [P, 2, T])
        eps_c = sb("eps_c", [P, 2])
        stat = sb("stat", [P, 4, 8])
        with ExitStack() as s:
            qk = sb("qk", [P, 13, SEQ], to=s)
            vtok = sb("vtok", [P, 2, 640], to=s)
            sig = sb("sig", [P, 16, SEQ], to=s)
            bias = sb("bias", [P, HEADS1, SEQ], to=s)
            sc1, p1, pT1 = (sb(n, [P, 2, 384], to=s) for n in ("sc1", "p1", "pT1"))
        with ExitStack() as s:
            U, SA, SB_ = (sb(n, [P, KT, PADC + T], to=s) for n in ("U", "SA", "SB"))
        with ExitStack() as s:
            qhead = sb("qhead", [QK, MH, SEQ], to=s)
            sc2, p2 = (sb(n, [P, 2, 416], to=s) for n in ("sc2", "p2"))
            pT2, pT2m = sb("pT2", [P, 2, 384], to=s), sb("pT2m", [META, 2, 256], to=s)
            cqf = sb("cqf", [P, QR, SEQ], to=s)
            cqh, cql = sb("cqh", [P, QR, SEQ], F32R, to=s), sb("cql", [P, QR, SEQ], F32R, to=s)
            o2h, o2l = sb("o2h", [P, 4, SEQ], F32R, to=s), sb("o2l", [P, 4, SEQ], F32R, to=s)
        hh, hl = sb("hh", [P, FF1 * SEQ], F32R), sb("hl", [P, FF1 * SEQ], F32R)
        with ExitStack() as s:
            boh, brow, brows = sb("boh", [NB + 2, BIASC], to=s), sb("brow", [NB + 2, HEADS1], to=s), sb("brows", [HEADS1, BIASC], to=s)
        with ExitStack() as s:
            khead = sb("khead", [QK, MH, T], to=s)
            v2 = sb("v2", [P, 3, MH * HD], to=s)
            krot = sb("krot", [ROPE, T], to=s)
        oh, ol = sb("oh", [P, 8, SEQ], F32R), sb("ol", [P, 8, SEQ], F32R)
        ckvf = sb("ckvf", [P, KVR, T])
        kvx = FF2 * T
        G = [ctx.enter_context(nc.psum_tensor(f"G{i}", [P, 2, 512], F32)) for i in range(2)]
        A = [ctx.enter_context(nc.psum_tensor(f"A{i}", [P, 512], F32)) for i in range(4)]

        pe_done, act_done, dve_done = counter("pe_done"), counter("act_done"), counter("dve_done")
        pool_done, hi_done, lo_done = counter("pool_done"), counter("hi_done"), counter("lo_done")
        loaded = [counter(f"loaded{i}") for i in range(NRAW)]
        small_in, x_in, con_in, meta_in = counter("small_in"), counter("x_in"), counter("con_in"), counter("meta_in")
        rows_in, rows_out, bias_in, stored = counter("rows_in"), counter("rows_out"), counter("bias_in"), counter("stored")
        pe, act, dve = Queue(nc.tensor, pe_done), Queue(nc.scalar, act_done), Queue(nc.vector, dve_done)
        pool, sp = Queue(nc.gpsimd, pool_done), Queue(nc.sync)

        def V(name, k=0, n=1):
            return vec[:, vat[name] + k:vat[name] + k + n]

        ident = con[:, cat["ident"]:cat["ident"] + P]
        f = lambda ap: ap.bitcast(F32)
        COLS1 = slice(META, T)

        vec_ok = sp.do(lambda e: e.dma_start(vec[:, :], vecs), signal=(small_in, 16))
        x_ok = sp.do(lambda e: e.dma_start(X[:, :, META:T], xT), signal=(x_in, 16))

        load_of, hi_of, lo_of, free_of = {}, {}, {}, {}
        plain = {c for n in where if n.startswith("ada") for c, _ in where[n]}

        def load_chunk(c):
            if c >= len(chunks) or c in load_of:
                return
            slot, w = c % NRAW, len(chunks[c]) * P
            before = [] if c < NRAW else [free_of[c - NRAW] if c - NRAW in plain else lo_of[c - NRAW]]
            load_of[c] = sp.do(lambda e: e.dma_start(raw[:, slot, 0:w], wstream[c, :, 0:w]), before, (loaded[slot], 16))

        split_at, split_order = {}, [c for c in range(len(chunks)) if c not in plain]
        for i, c in enumerate(split_order):
            split_at[c] = i
        plain_ready = [-1]

        def load_upto(c):
            for k in range(c + 1):
                if k not in load_of:
                    ok = k < NRAW or ((free_of if k - NRAW in plain else lo_of).get(k - NRAW) is not None)
                    if not ok:
                        return
                    load_chunk(k)

        def split_chunk(c):
            if c in lo_of:
                return
            load_upto(c)
            i, w, slot = split_at[c], len(chunks[c]) * P, c % NRAW
            s = i % NSPLIT
            before = free_of[split_order[i - NSPLIT]] if i >= NSPLIT else None
            hi_of[c] = act.do(lambda e: e.activation(whi[:, s, 0:w], raw[:, slot, 0:w], ACT.Copy), [load_of[c], before], (hi_done, 1))
            lo_of[c] = dve.do(lambda e: e.tensor_tensor(wlo[:, s, 0:w], raw[:, slot, 0:w], f(whi[:, s, 0:w]), ALU.subtract),
                              [hi_of[c], before], (lo_done, 1))
            load_upto(c + NRAW)

        def need(c):
            for k in range(c, min(c + AHEAD, len(chunks) - 1) + 1):
                if k in plain:
                    load_upto(k)
                    continue
                i = split_at[k]
                if i >= NSPLIT and split_order[i - NSPLIT] not in free_of:
                    break
                if k - NRAW >= 0 and k not in load_of and (free_of if k - NRAW in plain else lo_of).get(k - NRAW) is None:
                    break
                split_chunk(k)

        def used(c, off, token_wanted):
            return token_wanted or off == last_use[c]

        def mark(c, off, token):
            if off == last_use[c]:
                free_of[c] = token
                load_upto(c + NRAW)

        def weights(c, off, n=1):
            s = split_at[c] % NSPLIT
            return whi[:, s, off * P:(off + n) * P], wlo[:, s, off * P:(off + n) * P]

        gnext, gfree = [0], [[], []]

        def gemm(name, ntiles, nk, src, n, ready=None):
            g = gnext[0] % 2
            gnext[0] += 1
            before = list(gfree[g])
            gfree[g] = []
            places, i, token = where[name], 0, None
            for kt in range(nk):
                for t in range(ntiles):
                    c, off = places[i]
                    i += 1
                    need(c)
                    xs, xr = src(kt)
                    w_h, w_l = weights(c, off)
                    waits = before + [hi_of[c], lo_of[c]] + (ready(kt) if ready else [])
                    out = G[g][:, t, 0:n]
                    first = lambda e: e.matmul(out, w_h, xs, start=kt == 0, stop=False)
                    pe.do(first, waits, signal=False)
                    pe.do(lambda e: e.matmul(out, w_h, xr, start=False, stop=False), signal=False)
                    end = i == nk * ntiles
                    last = lambda e: e.matmul(out, w_l, xs, start=False, stop=kt == nk - 1)
                    tok = pe.do(last, signal=None if used(c, off, end) else False)
                    mark(c, off, tok)
                    if end:
                        token = tok
            return g, token

        def token_major(name, width, nk, src, rows, tile0, ready=None):
            g = gnext[0] % 2
            gnext[0] += 1
            before, gfree[g] = list(gfree[g]), []
            places, nb, token = where[name], width // P, None
            for kt in range(nk):
                c, off = places[kt * nb]
                need(c)
                w_h, w_l = weights(c, off, nb)
                for i, (a, m) in enumerate(rows):
                    xs, xr = src(kt, a, m)
                    out = G[g][0:m, i, 0:width]
                    waits = before + [hi_of[c], lo_of[c]] + (ready(kt) if ready else [])
                    for j, (s_, m_) in enumerate(((xs, w_h), (xr, w_h), (xs, w_l))):
                        end = i == len(rows) - 1 and j == 2
                        fn = lambda e: e.matmul(out, s_, m_, start=kt == 0 and j == 0, stop=kt == nk - 1 and j == 2)
                        tok = pe.do(fn, waits, None if end else False)
                    if i == len(rows) - 1:
                        if tile0:
                            mark(c, off + nb - 1, tok)
                        token = tok
            return g, token

        def split_out(hi, lo, src, after, scale=None, bias_=None, in1=None):
            kw = {}
            if scale is not None:
                kw["scale"] = scale
            if bias_ is not None:
                kw["bias"] = bias_
            fn = ACT.Copy if bias_ is None and scale is None else ACT.Identity
            th = act.do(lambda e: e.activation(hi, src, fn, **kw), after)
            if scale is not None:
                tl = dve.do(lambda e: e.scalar_tensor_tensor(lo, src, scale, f(hi), ALU.mult, ALU.subtract), [th] + after)
            elif bias_ is not None:
                tl = dve.do(lambda e: e.scalar_tensor_tensor(lo, src, bias_, f(hi), ALU.add, ALU.subtract), [th] + after)
            else:
                tl = dve.do(lambda e: e.tensor_tensor(lo, src, f(hi), ALU.subtract), [th] + after)
            return [th, tl]

        sq_state = dict(n=0, tok=None, used=None)

        def square_in(src, first, cols, after):
            dst = sumsq[:, cols]
            if first:
                sq_state["tok"] = pool.do(lambda e: e.tensor_tensor(dst, src, src, ALU.mult), after + [sq_state["used"]])
            else:
                s = sq[:, sq_state["n"] % 2, cols]
                sq_state["n"] += 1
                a = pool.do(lambda e: e.tensor_tensor(s, src, src, ALU.mult), after)
                sq_state["tok"] = pool.do(lambda e: e.tensor_tensor(dst, dst, s, ALU.add), [a, sq_state["tok"]])

        afree = [[], [], [], []]

        def rstd_of(which, dst, cols):
            n = cols.stop - cols.start
            t = pe.do(lambda e: e.matmul(A[0][:, 0:n], mean_ones[:, which, :], sumsq[:, cols], start=True, stop=True),
                      [sq_state["tok"]] + afree[0])
            sq_state["used"] = t
            r = act.do(lambda e: e.activation(root[:, cols], A[0][:, 0:n], ACT.Sqrt, bias=eps_c[:, 0:1]), [t])
            afree[0] = [r]
            return dve.do(lambda e: e.reciprocal(dst[:, cols], root[:, cols]), [r])

        def norm_input(hi, lo, gain, cols):
            ready = {}

            def tile(kt, tok):
                ready[kt] = split_out(hi(kt), lo(kt), X[:, kt, cols], [tok], scale=V(gain, kt))
            return ready, tile

        dve.do(lambda e: e.memset(eps_c[:, :], EPS))
        for i, n in enumerate((D, KVR * P, QR * P)):
            ones_t = dve.do(lambda e: e.memset(mean_ones[:, i, :], 1.0 / n))
        load_upto(NRAW - 1)
        for kt in range(KT):
            square_in(X[:, kt, COLS1], kt == 0, COLS1, [x_ok])
        cs = act.do(lambda e: e.activation(csil[:, :], V("c", 0, KT), ACT.Silu), [vec_ok])
        afree[0] = [ones_t]
        r1 = rstd_of(0, rstd, COLS1)

        def ada_tiles(i):
            g = gnext[0] % 2
            gnext[0] += 1
            before, gfree[g] = list(gfree[g]), []
            tok = None
            for j, (c, off) in enumerate(where[f"ada{i}"]):
                need(c)
                t, kt = divmod(j, KT)
                a = raw[:, c % NRAW, off * P:(off + 1) * P]
                fn = lambda e: e.matmul(G[g][:, t, 0:1], a, csil[:, kt:kt + 1], start=kt == 0, stop=kt == KT - 1)
                tok = pe.do(fn, before + [load_of[c], cs], None if used(c, off, j == 2 * KT - 1) else False)
                mark(c, off, tok)
            m = dve.do(lambda e: e.tensor_tensor(mod[:, 2 * i:2 * i + 2], G[g][:, :, 0], V("ada_b", 2 * i, 2), ALU.add), [tok, vec_ok])
            gfree[g] = [m]
            return m

        for i in range(8):
            m = ada_tiles(i)
            if i == 0:
                con_ok = sp.do(lambda e: e.dma_start(con[:, :], consts), signal=(con_in, 16))
                sp.do(lambda e: e.dma_start(boh[:, :], bias_oh), signal=(rows_in, 16))
                rin = sp.do(lambda e: e.dma_start(brow[:, :], bias_rows), signal=(rows_in, 16))
        bt = pe.do(lambda e: e.matmul(A[1][0:HEADS1, 0:BIASC], brow[:, :], boh[:, :], start=True, stop=True), [rin])
        bt = dve.do(lambda e: e.tensor_copy(brows[:, :], A[1][0:HEADS1, 0:BIASC]), [bt])
        afree[1] = [bt]
        ro = pool.do(lambda e: e.dma_start(scratch[:, 0:BIASC], brows[:, :]), [bt], (rows_out, 16))
        hankel = bass.AP(scratch.tensor, 0, [[1, P], [512, HEADS1], [1, SEQ]])
        bias_ok = pool.do(lambda e: e.dma_start(bias[:, :, :], hankel), [ro], (bias_in, 16))

        def mod_gain(dst, gname, k, after):
            a = dve.do(lambda e: e.tensor_scalar(dst, mod[:, k:k + KT], 1.0, None, ALU.add), after)
            return dve.do(lambda e: e.tensor_tensor(dst, dst, V(gname, 0, KT), ALU.mult), [a, vec_ok])

        def modulated(goff, shift, ready_t, rs):
            ready = {}
            for kt in range(KT):
                b = kt % 2
                t = dve.do(lambda e: e.scalar_tensor_tensor(tmp[:, b, 0:SEQ], X[:, kt, COLS1], g1m[:, goff + kt:goff + kt + 1],
                                                                            rstd[:, COLS1], ALU.mult, ALU.mult),
                           ready_t + [rs] + (ready[kt - 2] if kt >= 2 else []))
                ready[kt] = split_out(xh[:, kt, COLS1], xl[:, kt, COLS1], tmp[:, b, 0:SEQ], [t], bias_=mod[:, shift + kt:shift + kt + 1])
            return ready

        gm = mod_gain(g1m[:, 0:KT], "norm1_g", KT, [m])
        ready = modulated(0, 0, [gm], r1)
        src1 = lambda kt: (xh[:, kt, COLS1], xl[:, kt, COLS1])

        qk_ok = {}
        REV = lambda ap: ap[:, :, ::-1]
        for i in range(7):
            nt = 2 if i < 6 else 1
            g, tok = gemm(f"qk{i}", nt, KT, src1, SEQ, lambda kt: ready[kt])
            fr = []
            for t in range(nt):
                ti = 2 * i + t
                isq = 1 <= ti <= 4 or ti >= 9
                dst = qk[:, ti, :].rearrange("p (b q) -> p b q", b=2)
                ps = G[g][:, t, 0:SEQ].rearrange("p (b q) -> p b q", b=2)
                ps = REV(ps) if isq else ps
                if t == 0:
                    qk_ok[ti] = act.do(lambda e: e.activation(dst, ps, ACT.Copy), [tok])
                else:
                    qk_ok[ti] = dve.do(lambda e: e.tensor_copy(dst, ps), [tok])
                fr.append(qk_ok[ti])
            gfree[g] = fr
        vsrc = lambda kt, a, m: (xh[:, kt, META + a:META + a + m], xl[:, kt, META + a:META + a + m])
        v_ok = []
        for name, w, c0 in (("va", P, 0), ("vb", 4 * P, P)):
            g, tok = token_major(name, w, KT, vsrc, [(0, P), (P, P)], True)
            a_ = act.do(lambda e: e.activation(vtok[:, 0, c0:c0 + w], G[g][:, 0, 0:w], ACT.Copy), [tok])
            b_ = dve.do(lambda e: e.tensor_copy(vtok[:, 1, c0:c0 + w], G[g][:, 1, 0:w]), [tok])
            gfree[g] = [a_, b_]
            v_ok += [a_, b_]

        heads = [dict(q=1 + h % 4, k=0, row=(h // 4) * HD, v=(h // 4) * HD, bias=h, out=h % 4, sink=h) for h in (0, 4, 1, 5, 2, 6, 3, 7)]
        heads += [dict(q=9 + h // 2, k=5 + h // 2, row=(h % 2) * HD, v=P + h * HD, bias=8 + h, out=4 + h // 2, sink=None) for h in range(8)]
        s_tok, e_tok, pt_tok, pv_tok, o_ok, pT_free = {}, {}, {}, {}, {}, {}

        def scores1(i):
            h = heads[i]
            r, bank, b = h["row"], A[i % 2], i % 2
            q = lambda n: qk[r:r + HD, h["q"], n * P:(n + 1) * P]
            k = lambda w: qk[r:r + HD, h["k"], 0:w]
            pe.do(lambda e: e.matmul(bank[:, 0:SEQ], q(1), k(SEQ), start=True, stop=True), [qk_ok[h["q"]], qk_ok[h["k"]]] + afree[i % 2], False)
            t = pe.do(lambda e: e.matmul(bank[:, SEQ:SEQ + P], q(0), k(P), start=True, stop=True))
            w = [t, bias_ok] + ([e_tok[i - 2]] if i >= 2 else [])
            dve.do(lambda e: e.scalar_tensor_tensor(sc1[:, b, 0:SEQ], bank[:, 0:SEQ], HD ** -0.5, bias[:, h["bias"], :], ALU.mult, ALU.add), w, False)
            t = dve.do(lambda e: e.scalar_tensor_tensor(sc1[:, b, SEQ:SEQ + P], bank[:, SEQ:SEQ + P], HD ** -0.5, bias[:, h["bias"], P:SEQ],
                                                        ALU.mult, ALU.add))
            afree[i % 2] = [t]
            st = stat[:, i % 4, :]
            mx = st[:, 6:8]
            neg = h["sink"] is None
            md = st[:, 0:2] if neg else mx
            dve.do(lambda e: e.tensor_reduce(md[:, 0:1], sc1[:, b, 0:SEQ], AX_X, ALU.max, negate=neg), [t], False)
            t = dve.do(lambda e: e.tensor_reduce(md[:, 1:2], sc1[:, b, SEQ:SEQ + P], AX_X, ALU.max, negate=neg))
            if not neg:
                sink = V("sinks", h["sink"])
                t = dve.do(lambda e: e.tensor_scalar(st[:, 0:2], mx, sink, -1.0, ALU.max, ALU.mult), [t])
            act.do(lambda e: e.activation(p1[:, b, 0:SEQ], sc1[:, b, 0:SEQ], ACT.Exp, bias=st[:, 0:1], accum_out=st[:, 2:3]),
                   [t] + ([pt_tok[i - 2]] if i >= 2 else []))
            u = act.do(lambda e: e.activation(p1[:, b, SEQ:384], sc1[:, b, SEQ:384], ACT.Exp, bias=st[:, 1:2], accum_out=st[:, 3:4]))
            e_tok[i] = u
            if not neg:
                sk = act.do(lambda e: e.activation(st[:, 4:6], st[:, 0:2], ACT.Exp, bias=sink))
                u2 = dve.do(lambda e: e.tensor_tensor(st[:, 4:6], st[:, 4:6], st[:, 2:4], ALU.add), [sk, u])
                u2 = dve.do(lambda e: e.reciprocal(st[:, 4:6], st[:, 4:6]), [u2])
            else:
                u2 = dve.do(lambda e: e.reciprocal(st[:, 4:6], st[:, 2:4]), [u])
            dve.do(lambda e: e.tensor_scalar(p1[:, b, 0:SEQ], p1[:, b, 0:SEQ], st[:, 4:5], None, ALU.mult), [u2], False)
            s_tok[i] = dve.do(lambda e: e.tensor_scalar(p1[:, b, SEQ:384], p1[:, b, SEQ:384], st[:, 5:6], None, ALU.mult))

        def transposes1(i):
            b = i % 2
            for j in range(3):
                t = pe.do(lambda e: e.transpose(A[2][:, j * P:(j + 1) * P], p1[:, b, j * P:(j + 1) * P], ident),
                          [s_tok[i], con_ok] + afree[2], None if j == 2 else False)
            pt_tok[i] = t
            c = act.do(lambda e: e.activation(pT1[:, b, :], A[2][:, 0:384], ACT.Copy), [t] + ([pv_tok[i - 2]] if i >= 2 else []))
            afree[2] = [c]
            pT_free[i] = c

        def values1(i):
            h, b, half = heads[i], i % 2, i % 2
            vv = lambda kt: vtok[:, kt, h["v"]:h["v"] + HD]
            o = A[3][half * HD:(half + 1) * HD, :]
            pe.do(lambda e: e.matmul(o[:, P:SEQ], vv(0), pT1[:, b, 0:P], start=True, stop=False), [pT_free[i]] + v_ok + afree[3], False)
            pe.do(lambda e: e.matmul(o[:, P:SEQ], vv(1), pT1[:, b, P:SEQ], start=False, stop=True), signal=False)
            t = pe.do(lambda e: e.matmul(o[:, 0:P], vv(0), pT1[:, b, SEQ:384], start=True, stop=True))
            pv_tok[i] = t
            if half:
                tile = h["out"]
                ps = REV(A[3][:, 0:SEQ].rearrange("p (b q) -> p b q", b=2))
                d = lambda x: x[:, tile, :].rearrange("p (b q) -> p b q", b=2)
                o_ok[tile] = split_out(d(oh), d(ol), ps, [t])
                afree[3] = o_ok[tile]

        sig_ok = {}

        def gates(i):
            g, tok = gemm(f"gate{i}", 2, KT, src1, SEQ, lambda kt: ready[kt])
            d = sig[:, 2 * i:2 * i + 2, :]
            a_ = act.do(lambda e: e.activation(d, G[g][:, :, 0:SEQ], ACT.Tanh, scale=0.5), [tok])
            gfree[g] = [a_]
            sig_ok[i] = dve.do(lambda e: e.tensor_scalar(d, d, 0.5, 0.5, ALU.mult, ALU.add), [a_])

        for i in range(HEADS1 + 2):
            if i < HEADS1:
                scores1(i)
                if i % 2 == 0:
                    gates(i // 2)
                m = ada_tiles(8 + i)
            if 1 <= i <= HEADS1:
                transposes1(i - 1)
            if i >= 2:
                values1(i - 2)
        afree[1] = afree[1] + [s_tok[15]]
        afree[0] = afree[0] + [s_tok[15]]

        merged_ok = {}
        for i in range(4):
            ga_, ta = gemm(f"bra{i}", 2, 4, lambda kt: (oh[:, kt, :], ol[:, kt, :]), SEQ, lambda kt: o_ok[kt])
            gb_, tb = gemm(f"brb{i}", 2, 4, lambda kt: (oh[:, 4 + kt, :], ol[:, 4 + kt, :]), SEQ, lambda kt: o_ok[4 + kt])
            hb = hidf[:, i % 2, :].rearrange("p (t q) -> p t q", t=2)
            sa, sb2 = sig[:, 2 * i:2 * i + 2, :], sig[:, 8 + 2 * i:10 + 2 * i, :]
            a_ = dve.do(lambda e: e.tensor_tensor(sa, sa, G[ga_][:, :, 0:SEQ], ALU.mult), [ta, sig_ok[i], sig_ok[4 + i]])
            b_ = dve.do(lambda e: e.tensor_tensor(sb2, sb2, G[gb_][:, :, 0:SEQ], ALU.mult), [tb])
            gfree[ga_], gfree[gb_] = [a_], [b_]
            c_ = dve.do(lambda e: e.tensor_tensor(hb, sa, sb2, ALU.add), [a_, b_] + (merged_ok[2 * i - 4] if i >= 2 else []))
            sl = (slice(None), slice(2 * i, 2 * i + 2), COLS1)
            merged_ok[2 * i] = merged_ok[2 * i + 1] = split_out(xh[sl], xl[sl], hb, [c_])

        def add_residual(g, tok, i, cols, scalar, hooks, after=()):
            n = cols.stop - cols.start
            fr = []
            for t in range(2):
                kt = 2 * i + t
                s_ = scalar(kt) if callable(scalar) else scalar
                fr.append(dve.do(lambda e: e.scalar_tensor_tensor(X[:, kt, cols], G[g][:, t, 0:n], s_, X[:, kt, cols],
                                                                                      ALU.mult, ALU.add), [tok] + list(after)))
                square_in(X[:, kt, cols], kt == 0, cols, [fr[-1]])
                for hook in hooks:
                    hook(kt, fr[-1])
            gfree[g] = fr
            return fr[-1]

        gm2 = mod_gain(g1m[:, KT:2 * KT], "norm2_g", 4 * KT, [m])
        for i in range(4):
            g, tok = gemm(f"wout{i}", 2, KT, src1, SEQ, lambda kt: merged_ok[kt])
            add_residual(g, tok, i, COLS1, lambda kt: mod[:, 2 * KT + kt:2 * KT + kt + 1], [])
        r = rstd_of(0, rstd, COLS1)
        ready2 = modulated(KT, 3 * KT, [gm2], r)

        hid_ok, hf_free = {}, [[], []]
        meta_ok = pool.do(lambda e: e.dma_start(X[:, :, 0:META], metaT), signal=(meta_in, 16))
        for i in range(FF1 // 2):
            g, tok = gemm(f"mlp_in{i}", 2, KT, src1, SEQ, lambda kt: ready2[kt])
            b = i % 2
            hb = hidf[:, b, :].rearrange("p (t q) -> p t q", t=2)
            a_ = act.do(lambda e: e.activation(hb, G[g][:, :, 0:SEQ], ACT.Relu), [tok] + hf_free[b])
            gfree[g] = [a_]
            c_ = dve.do(lambda e: e.tensor_tensor(hb, hb, hb, ALU.mult), [a_])
            sl = slice(2 * i * SEQ, (2 * i + 2) * SEQ)
            hid_ok[2 * i] = hid_ok[2 * i + 1] = split_out(hh[:, sl], hl[:, sl], hidf[:, b, :], [c_])
            hf_free[b] = hid_ok[2 * i]
        hid1 = lambda kt: (hh[:, kt * SEQ:(kt + 1) * SEQ], hl[:, kt * SEQ:(kt + 1) * SEQ])
        for i in range(4):
            g, tok = gemm(f"mlp_out{i}", 2, FF1, hid1, SEQ, lambda kt: hid_ok[kt])
            add_residual(g, tok, i, COLS1, lambda kt: mod[:, 5 * KT + kt:5 * KT + kt + 1], [])

        ALL = slice(0, T)
        r = rstd_of(0, rstd, COLS1)
        full = lambda t: (lambda kt: t[:, kt, :])
        ready3, prep = norm_input(full(xh), full(xl), "ffn1_norm0", ALL)
        for kt in range(KT):
            t = dve.do(lambda e: e.scalar_tensor_tensor(X[:, kt, COLS1], X[:, kt, COLS1], V("final_g", kt), rstd[:, COLS1],
                                                                     ALU.mult, ALU.mult), [r, meta_ok, sq_state["tok"]])
            square_in(X[:, kt, ALL], kt == 0, ALL, [t])
            prep(kt, t)

        def swiglu(f_, layer, ready, cols, hooks, between=None, rs=None, gu_after=()):
            n = cols.stop - cols.start
            hid_ok, h_free, gu_free = {}, [[], []], [list(gu_after), list(gu_after)]
            src = lambda kt: (xh[:, kt, cols], xl[:, kt, cols])
            for j in range(FF2):
                g, tok = gemm(f"{f_}_{layer}_gu{j}", 2, KT, src, n, lambda kt: ready[kt])
                if j == 0 and rs is None:
                    rs = rstd_of(0, rstd, cols)
                b = j % 2
                rb = rstd[:, cols].unsqueeze(1).broadcast_to([P, 2, n])
                a_ = dve.do(lambda e: e.tensor_tensor(gu[:, b, :, 0:n], G[g][:, :, 0:n], rb, ALU.mult),
                            [tok, rs] + gu_free[b])
                gfree[g] = [a_]
                s_ = act.do(lambda e: e.activation(gu[:, b, 0, 0:n], gu[:, b, 0, 0:n], ACT.Silu), [a_])
                c_ = dve.do(lambda e: e.tensor_tensor(hidf[:, b, 0:n], gu[:, b, 0, 0:n], gu[:, b, 1, 0:n], ALU.mult),
                            [s_] + h_free[b])
                gu_free[b] = [c_]
                sl = slice(j * n, (j + 1) * n)
                hid_ok[j] = split_out(hh[:, sl], hl[:, sl], hidf[:, b, 0:n], [c_])
                h_free[b] = hid_ok[j]
                if between and j == 3:
                    between()
            hid = lambda kt: (hh[:, kt * n:(kt + 1) * n], hl[:, kt * n:(kt + 1) * n])
            for i in range(4):
                g, tok = gemm(f"{f_}_{layer}_down{i}", 2, FF2, hid, n, lambda kt: hid_ok[kt])
                last = add_residual(g, tok, i, cols, 0.5, hooks)
            return last

        swiglu("ffn1", 0, ready3, ALL, [])

        r = rstd_of(0, rstd, ALL)
        pad_t = pool.do(lambda e: e.memset(U[:, :, 0:PADC], 0.0), [r])
        u_ok = {}
        pool_ready = {}
        body = slice(PADC, PADC + T)
        for kt in range(KT):
            u_ok[kt] = dve.do(lambda e: e.scalar_tensor_tensor(U[:, kt, body], X[:, kt, :], V("mix_norm0", kt), rstd[:, :],
                                                                            ALU.mult, ALU.mult), [r])
        for gi in (3, 2, 1, 0):
            ks = slice(2 * gi, 2 * gi + 2)
            eng = pool if gi in (2, 0) else dve
            cur, t, lo_, nxt = U, u_ok[2 * gi + 1], 1, (SA, SB_)
            deps = [u_ok[2 * gi], u_ok[2 * gi + 1], pad_t]
            for st in range(gi + 1):
                sh = 1 << st
                dst = nxt[st % 2]
                t = eng.do(lambda e: e.tensor_tensor(dst[:, ks, lo_:PADC + T], cur[:, ks, lo_:PADC + T],
                                                                                     cur[:, ks, lo_ - sh:PADC + T - sh], ALU.add), deps)
                deps, cur, lo_ = [t], dst, lo_ + 2 * sh
            w = POOL_W[gi]
            fix = con[:, cat["count_fix"] + gi * PADC:cat["count_fix"] + gi * PADC + w].unsqueeze(1).broadcast_to([P, 2, w])
            t = eng.do(lambda e: e.tensor_tensor(cur[:, ks, PADC:PADC + w], cur[:, ks, PADC:PADC + w], fix, ALU.mult),
                       [t, con_ok])
            for kt in (2 * gi, 2 * gi + 1):
                t2 = dve.do(lambda e: e.scalar_tensor_tensor(cur[:, kt, body], cur[:, kt, body], 1.0 / w, U[:, kt, body],
                                                                                  ALU.mult, ALU.subtract), [t])
                pool_ready[kt] = split_out(xh[:, kt, :], xl[:, kt, :], cur[:, kt, body], [t2])
        ready4, prep = norm_input(full(xh), full(xl), "ffn2_norm0", ALL)
        for gi in range(4):
            g, tok = gemm(f"pool{gi}", 2, 2, (lambda gi: (lambda kt: (xh[:, 2 * gi + kt, :], xl[:, 2 * gi + kt, :])))(gi), T,
                          (lambda gi: (lambda kt: pool_ready[2 * gi + kt]))(gi))
            add_residual(g, tok, gi, ALL, lambda kt: V("pool_scale", kt), [prep])
        kv_ready, prep_kv = norm_input(lambda kt: hh[:, kvx + kt * T:kvx + (kt + 1) * T], lambda kt: hl[:, kvx + kt * T:kvx + (kt + 1) * T],
                                       "kv_in_norm", ALL)
        ready5, prep5 = norm_input(full(xh), full(xl), "ffn1_norm1", ALL)
        swiglu("ffn2", 0, ready4, ALL, [prep_kv, prep5])

        kvsrc = lambda kt: (hh[:, kvx + kt * T:kvx + (kt + 1) * T], hl[:, kvx + kt * T:kvx + (kt + 1) * T])
        g, tok = gemm("ckv", 2, KT, kvsrc, T, lambda kt: kv_ready[kt])
        rs1 = rstd_of(0, rstd, ALL)
        rb = rstd[:, :].unsqueeze(1).broadcast_to([P, 2, T])
        ck = dve.do(lambda e: e.tensor_tensor(gu[:, 0, :, :], G[g][:, :, 0:T], rb, ALU.mult), [tok, rs1])
        gfree[g] = [ck]
        g, tok = gemm("krope", 1, KT, kvsrc, T, lambda kt: kv_ready[kt])
        for kt in range(KVR):
            square_in(gu[:, 0, kt, :], kt == 0, ALL, [ck])
        ka_ = dve.do(lambda e: e.tensor_tensor(tmp[0:64, 0, :], G[g][0:64, 0, 0:T], rstd[0:64, :], ALU.mult), [tok, rs1])
        gfree[g] = [ka_]
        cosT, sinT = (lambda r0, r1, c: con[r0:r1, cat["cos"] + c.start:cat["cos"] + c.stop]), (lambda r0, r1, c: con[r0:r1, cat["sin"] + c.start:cat["sin"] + c.stop])
        kb_ = dve.do(lambda e: e.tensor_tensor(krot[:, :], tmp[0:32, 0, :], cosT(0, 32, ALL), ALU.mult), [ka_])
        kc_ = dve.do(lambda e: e.tensor_tensor(tmp[0:32, 1, :], tmp[32:64, 0, :], sinT(32, 64, ALL), ALU.mult), [kb_])
        kd_ = dve.do(lambda e: e.tensor_tensor(krot[:, :], krot[:, :], tmp[0:32, 1, :], ALU.add), [kc_])
        kr_ok = dve.do(lambda e: e.tensor_copy(khead[HD:QK, :, :], krot[:, :].unsqueeze(1).broadcast_to([ROPE, MH, T])), [kd_])
        kv_done = {}

        def kv_up():
            rk = rstd_of(1, rstd2, ALL)
            for kt in range(KVR):
                t = dve.do(lambda e: e.scalar_tensor_tensor(tmp[:, kt, :], ckvf[:, kt, :], V("kv_latent_norm", kt), rstd2[:, :],
                                                                         ALU.mult, ALU.mult), [rk, cc, kd_])
                c0 = kvx + kt * T
                kv_done[kt] = split_out(hh[:, c0:c0 + T], hl[:, c0:c0 + T], tmp[:, kt, :], [t, tok])
            lat = lambda kt: (hh[:, kvx + kt * T:kvx + (kt + 1) * T], hl[:, kvx + kt * T:kvx + (kt + 1) * T])
            ks = []
            for i in range(2):
                g_, tk = gemm(f"uk{i}", 2, KVR, lat, T, lambda kt: kv_done[kt])
                a_ = act.do(lambda e: e.activation(khead[0:HD, 4 * i:4 * i + 4:2, :], G[g_][0:HD, :, 0:T], ACT.Copy), [tk])
                b_ = dve.do(lambda e: e.tensor_copy(khead[0:HD, 4 * i + 1:4 * i + 4:2, :], G[g_][HD:P, :, 0:T]), [tk, a_])
                gfree[g_] = [a_, b_]
                ks += [a_, b_]
            lat_t = lambda kt, a, m_: (hh[:, kvx + kt * T + a:kvx + kt * T + a + m_], hl[:, kvx + kt * T + a:kvx + kt * T + a + m_])
            g_, tk = token_major("uv", 4 * P, KVR, lat_t, [(0, P), (P, P)], False)
            a_ = act.do(lambda e: e.activation(v2[:, 0, :], G[g_][:, 0, :], ACT.Copy), [tk])
            b_ = dve.do(lambda e: e.tensor_copy(v2[:, 1, :], G[g_][:, 1, :]), [tk])
            gfree[g_] = [a_, b_]
            g2, tk = token_major("uv", 4 * P, KVR, lat_t, [(2 * P, META)], True)
            c_ = act.do(lambda e: e.activation(v2[0:META, 2, :], G[g2][0:META, 0, :], ACT.Copy), [tk])
            gfree[g2] = [c_]
            kv_done["k"], kv_done["v"] = ks + [kr_ok], [a_, b_, c_]

        cc = pool.do(lambda e: e.tensor_copy(ckvf[:, :, :], gu[:, 0, :, :]), [ck])
        mix_ready, prep_mix = norm_input(lambda kt: xh[:, kt, COLS1], lambda kt: xl[:, kt, COLS1], "mix_norm1", COLS1)


        swiglu("ffn1", 1, ready5, COLS1, [prep_mix], kv_up, rs1, [cc])

        g, tok = gemm("dq0", 2, KT, src1, SEQ, lambda kt: mix_ready[kt])
        r = rstd_of(0, rstd, COLS1)
        rb2 = rstd[:, COLS1].unsqueeze(1).broadcast_to([P, 2, SEQ])
        cq = [dve.do(lambda e: e.tensor_tensor(cqf[:, 0:2, :], G[g][:, :, 0:SEQ], rb2, ALU.mult), [tok, r])] * 2
        gfree[g] = [cq[0]]
        g, tok = gemm("dq1", 1, KT, src1, SEQ, lambda kt: mix_ready[kt])
        cq.append(dve.do(lambda e: e.tensor_tensor(cqf[:, 2, :], G[g][:, 0, 0:SEQ], rstd[:, COLS1], ALU.mult), [tok, r]))
        gfree[g] = [cq[2]]
        cq_ok = {}
        for kt in range(QR):
            square_in(cqf[:, kt, :], kt == 0, COLS1, [cq[kt]])
            cq_ok[kt] = split_out(cqh[:, kt, :], cql[:, kt, :], cqf[:, kt, :], [cq[kt]], scale=V("q_latent_norm", kt))
        cqs = lambda kt: (cqh[:, kt, :], cql[:, kt, :])
        q_ok = []
        for i in range(2):
            g, tok = gemm(f"uqn{i}", 2, QR, cqs, SEQ, lambda kt: cq_ok[kt])
            if i == 0:
                rq = rstd_of(2, rstd2, COLS1)
            r64 = lambda lo_: rstd2[lo_:lo_ + HD, COLS1].unsqueeze(1).broadcast_to([HD, 2, SEQ])
            a_ = dve.do(lambda e: e.tensor_tensor(qhead[0:HD, 4 * i:4 * i + 4:2, :], G[g][0:HD, :, 0:SEQ], r64(0), ALU.mult), [tok, rq])
            b_ = dve.do(lambda e: e.tensor_tensor(qhead[0:HD, 4 * i + 1:4 * i + 4:2, :], G[g][HD:P, :, 0:SEQ], r64(HD), ALU.mult), [tok, rq])
            gfree[g] = [a_, b_]
            q_ok += [a_, b_]
        ra = dve.do(lambda e: e.tensor_tensor(gu[:, 0, 0, 0:SEQ], rstd2[:, COLS1], cosT(0, P, COLS1), ALU.mult), [rq])
        rb_ = dve.do(lambda e: e.tensor_tensor(gu[:, 0, 1, 0:SEQ], rstd2[:, COLS1], sinT(0, P, COLS1), ALU.mult), [rq])
        for i in range(2):
            g, tok = gemm(f"uqr{i}", 2, QR, cqs, SEQ, lambda kt: cq_ok[kt])
            a_ = dve.do(lambda e: e.tensor_tensor(gu[:, 1, :, 0:SEQ], G[g][:, :, 0:SEQ], gu[:, 0, :, 0:SEQ], ALU.mult), [tok, ra, rb_] + q_ok[-1:])
            gfree[g] = [a_]
            for n in range(4):
                q_ok.append(dve.do(lambda e: e.tensor_tensor(qhead[HD:QK, 4 * i + n, :], gu[n * ROPE:(n + 1) * ROPE, 1, 0, 0:SEQ],
                                                                            gu[n * ROPE:(n + 1) * ROPE, 1, 1, 0:SEQ], ALU.add), [a_]))

        KW = (META + P, T)
        OFF = (T, 0)
        mask = lambda w: con[:, cat["mla_mask"] + T - w:cat["mla_mask"] + T]
        s2, e2, pt2, pv2, o2_ok, ptc = {}, {}, {}, {}, {}, {}

        def scores2(i):
            bank, b = A[i % 2], i % 2
            for n in (1, 0):
                t = pe.do(lambda e: e.matmul(bank[:, OFF[n]:OFF[n] + KW[n]], qhead[:, i, n * P:(n + 1) * P], khead[:, i, 0:KW[n]],
                                                         start=True, stop=True), q_ok + kv_done["k"] + afree[i % 2], None if n == 0 else False)
            w = [t] + ([e2[i - 2]] if i >= 2 else [])
            for n in (1, 0):
                t = dve.do(lambda e: e.scalar_tensor_tensor(sc2[:, b, OFF[n]:OFF[n] + KW[n]], bank[:, OFF[n]:OFF[n] + KW[n]],
                                                                        1.0 / math.sqrt(QK), mask(KW[n]), ALU.mult, ALU.add), w)
            afree[i % 2] = [t]
            st = stat[:, i % 4, :]
            for n in (1, 0):
                t = dve.do(lambda e: e.tensor_reduce(st[:, n:n + 1], sc2[:, b, OFF[n]:OFF[n] + KW[n]], AX_X, ALU.max, negate=True), [t])
            for n in (1, 0):
                u = act.do(lambda e: e.activation(p2[:, b, OFF[n]:OFF[n] + KW[n]], sc2[:, b, OFF[n]:OFF[n] + KW[n]], ACT.Exp,
                                                              bias=st[:, n:n + 1], accum_out=st[:, 2 + n:3 + n]), [t] + ([pt2[i - 2]] if i >= 2 else []))
            e2[i] = u
            u = dve.do(lambda e: e.reciprocal(st[:, 4:6], st[:, 2:4]), [u])
            for n in (1, 0):
                s2[i] = dve.do(lambda e: e.tensor_scalar(p2[:, b, OFF[n]:OFF[n] + KW[n]], p2[:, b, OFF[n]:OFF[n] + KW[n]],
                                                                     st[:, 4 + n:5 + n], None, ALU.mult), [u])

        def transposes2(i):
            b = i % 2
            waits = [s2[i]] + afree[2] + gfree[1] + gfree[0]
            for j, c0 in enumerate((0, P, T)):
                pe.do(lambda e: e.transpose(A[2][:, j * P:(j + 1) * P], p2[:, b, c0:c0 + P], ident), waits, False)
            for j, c0 in enumerate((2 * P, T + P)):
                t = pe.do(lambda e: e.transpose(G[1][0:META, 0, j * P:(j + 1) * P], p2[:, b, c0:c0 + META], ident),
                          signal=None if j else False)
            pt2[i] = t
            a_ = act.do(lambda e: e.activation(pT2[:, b, :], A[2][:, 0:384], ACT.Copy), [t] + ([pv2[i - 2]] if i >= 2 else []))
            b_ = dve.do(lambda e: e.tensor_copy(pT2m[:, b, :], G[1][0:META, 0, 0:SEQ]), [t] + ([pv2[i - 2]] if i >= 2 else []))
            afree[2], gfree[1] = [a_], [b_]
            ptc[i] = [a_, b_]

        def values2(i):
            b, half = i % 2, i % 2
            vv = lambda kt, m_: v2[0:m_, kt, i * HD:(i + 1) * HD]
            o = A[3][half * HD:(half + 1) * HD, :]
            mm = lambda out, a, c, s0, s1: (lambda e: e.matmul(out, a, c, start=s0, stop=s1))
            pe.do(mm(o[:, P:SEQ], vv(0, P), pT2[:, b, 0:P], True, False), ptc[i] + kv_done["v"] + afree[3], False)
            pe.do(mm(o[:, P:SEQ], vv(1, P), pT2[:, b, P:SEQ], False, False), signal=False)
            pe.do(mm(o[:, P:SEQ], vv(2, META), pT2m[:, b, 0:P], False, True), signal=False)
            pe.do(mm(o[:, 0:P], vv(0, P), pT2[:, b, SEQ:384], True, False), signal=False)
            pv2[i] = pe.do(mm(o[:, 0:P], v2[0:META, 1, i * HD:(i + 1) * HD], pT2m[:, b, P:SEQ], False, True))
            if half:
                o2_ok[i // 2] = split_out(o2h[:, i // 2, :], o2l[:, i // 2, :], A[3][:, 0:SEQ], [pv2[i]])
                afree[3] = o2_ok[i // 2]

        for i in range(MH + 2):
            if i < MH:
                scores2(i)
            if 1 <= i <= MH:
                transposes2(i - 1)
            if i >= 2:
                values2(i - 2)
        afree[0] = afree[0] + afree[1]

        ready6, prep = norm_input(lambda kt: xh[:, kt, COLS1], lambda kt: xl[:, kt, COLS1], "ffn2_norm1", COLS1)
        for i in range(4):
            g, tok = gemm(f"wo{i}", 2, 4, lambda kt: (o2h[:, kt, :], o2l[:, kt, :]), SEQ, lambda kt: o2_ok[kt])
            add_residual(g, tok, i, COLS1, 1.0, [prep])
        swiglu("ffn2", 1, ready6, COLS1, [])

        r = rstd_of(0, rstd, COLS1)
        for kt in range(KT):
            t = dve.do(lambda e: e.scalar_tensor_tensor(X[:, kt, COLS1], X[:, kt, COLS1], V("final_norm", kt), rstd[:, COLS1],
                                                                     ALU.mult, ALU.mult), [r, sq_state["tok"]])
            if kt % 2:
                st_ = sp.do(lambda e: e.dma_start(outT[:, kt - 1:kt + 1, :], X[:, kt - 1:kt + 1, COLS1]), [t], (stored, 16))

        nc.sync.wait_ge(stored.sem, stored.value)


def _features(v):
    return np.ascontiguousarray(np.asarray(v).reshape(-1, P).T)


def kernel(**inputs):
    import concourse.bacc as _bacc
    from concourse.bass_utils import run_bass_kernel_spmd as _run

    a = {k: np.asarray(v) for k, v in inputs.items()}
    chunks, _ = weight_plan()
    wstream = np.zeros((len(chunks), P, CH * P), np.float32)
    for c, blocks in enumerate(chunks):
        for off, (name, layer, rows, cols) in enumerate(blocks):
            w = a[name]
            if name == "pool_w_2":
                w = w[0, layer]
            elif layer is not None:
                w = w[layer]
            wstream[c, :, off * P:(off + 1) * P] = w[np.ix_(rows, cols)]
    vat, vn = vector_plan()
    parts = {
        "c": a["c"], "ada_b": a["ada_b"], "norm1_g": a["norm1_g"], "norm2_g": a["norm2_g"], "final_g": a["final_g"],
        "pool_scale": a["pool_scale_2"], "kv_in_norm": a["kv_in_norm_2"], "final_norm": a["final_norm_2"],
        "kv_latent_norm": a["kv_latent_norm_2"], "q_latent_norm": a["q_latent_norm_2"],
    }
    for n in ("ffn1_norm", "mix_norm", "ffn2_norm"):
        for l in range(2):
            parts[f"{n}{l}"] = a[n + "_2"][l]
    vecs = np.zeros((P, vn), np.float32)
    for n, v in parts.items():
        w = _features(v)
        vecs[:, vat[n]:vat[n] + w.shape[1]] = w
    vecs[:, vat["sinks"]:vat["sinks"] + SWA_HEADS] = np.broadcast_to(a["attn_sinks"].reshape(1, -1), (P, SWA_HEADS))
    bias_oh, sel = bias_constants()
    feature_major = lambda v: np.ascontiguousarray(v.T.reshape(KT, P, -1).transpose(1, 0, 2))
    arrays = {
        "in_xT": feature_major(a["x"][0]), "in_metaT": feature_major(a["meta_tokens_2"]), "in_vecs": vecs,
        "in_consts": constants(), "in_bias_oh": bias_oh,
        "in_bias_rows": np.concatenate([a["rel_bias"], sel]), "in_wstream": wstream,
    }
    nc = _bacc.Bacc("TRN2", target_bir_lowering=False, num_devices=1)
    aps = [nc.dram_tensor(n, v.shape, F32, kind="ExternalInput").ap() for n, v in arrays.items()]
    scratch = nc.dram_tensor("bias_scratch", (HEADS1, 512), F32).ap()
    out = nc.dram_tensor("out_T", (P, KT, SEQ), F32, kind="ExternalOutput").ap()
    build_program(nc, *aps, scratch, out)
    r = _run(nc, [arrays], core_ids=[0])
    got = r.results[0]["out_T"]
    return np.ascontiguousarray(got.transpose(1, 0, 2).reshape(D, SEQ).T.reshape(1, SEQ, D))
```

```python
from contextlib import ExitStack
import math

import numpy as np

import concourse.bass as bass
from concourse import mybir

F32 = mybir.dt.float32
F32R = mybir.dt.float32r
ALU = mybir.AluOpType
ACT = mybir.ActivationFunctionType
AX_X = mybir.AxisListType.X

P = 128
D = 1024
KT = D // P
META = 16
SEQ = 256
T = META + SEQ
HD = 64
SWA_HEADS, SWA_KV, MOBA_HEADS = 8, 2, 8
HEADS1 = SWA_HEADS + MOBA_HEADS
WINDOW = 128
NB = 32
MAX_DISTANCE = 2048
FF1 = 4 * D // P
FF2 = 2816 // P
KVR = 256 // P
QR = 384 // P
MH, ROPE = 8, 32
QK = HD + ROPE
POOL_W = (2, 4, 8, 16)
PADC = 16
EPS = 1e-6
MASKED = -3.0e38
BIASC = 384

CH = 8
NRAW, NSPLIT = 8, 5
AHEAD = 3
LOADING = 3

W_IN_OFF = dict(qa=0, ka=512, va=640, qb=768, kb=1280, vb=1792, ga=2304, gb=3328)


_PIECES = [(i, part) for i in range(4, 12) for part in range(4)]
ADA_QK, ADA_HEADS, ADA_MLP = _PIECES[:8], _PIECES[8:24], _PIECES[24:]


def _r(a, n=P):
    return np.arange(a, a + n)


def weight_plan():
    groups = []

    def group(name, blocks, flush=False):
        groups.append((name, blocks, flush))

    def dense(name, arr, layer, tiles, nk, rows=None):
        rows = rows or (lambda kt: _r(kt * P))
        group(name, [(arr, layer, rows(kt), c) for kt in range(nk) for c in tiles])

    def ada(i, part):
        group(f"ada{i}_{part}", [("ada_w", 0, _r(kt * P), _r((4 * i + t) * P)) for kt in (2 * part, 2 * part + 1) for t in range(4)], True)

    for i in range(4):
        for part in range(4):
            ada(i, part)
    o = W_IN_OFF
    tiles = [_r(o["ka"])]
    tiles += [np.concatenate([_r(o["qa"] + j * HD, HD), _r(o["qa"] + (j + 4) * HD, HD)]) for j in range(4)]
    tiles += [_r(o["kb"] + j * P) for j in range(4)] + [_r(o["qb"] + j * P) for j in range(4)]
    for i in range(0, 13, 2):
        ada(*ADA_QK[i // 2])
        dense(f"qk{i // 2}", "w_in", 0, tiles[i:i + 2], KT)
    ada(*ADA_QK[7])
    group("va", [("w_in", 0, _r(kt * P), _r(o["va"])) for kt in range(KT)], True)
    group("vb", [("w_in", 0, _r(kt * P), _r(o["vb"] + j * P)) for kt in range(KT) for j in range(4)], True)
    for i in range(HEADS1):
        ada(*ADA_HEADS[i])
        t = i - i % 2
        group(f"gate{i}", [("w_in", 0, _r(kt * P), _r(o["ga"] + (t + n) * P)) for kt in _r(i % 2 * 4, 4) for n in range(2)])
    rows_a = lambda kt: np.concatenate([_r(kt * HD, HD), _r((kt + 4) * HD, HD)])
    for i in range(4):
        t2 = [_r((2 * i + n) * P) for n in range(2)]
        dense(f"bra{i}", "w_branch_a", 0, t2, 4, rows_a)
        dense(f"brb{i}", "w_branch_b", 0, t2, 4)
    for i in range(4):
        dense(f"wout{i}", "w_out", 0, [_r((2 * i + n) * P) for n in range(2)], KT)
    for i in range(FF1 // 2):
        if i % 2 == 0:
            ada(*ADA_MLP[i // 2])
        dense(f"mlp_in{i}", "w_mlp_in", 0, [_r((2 * i + n) * P) for n in range(2)], KT)
    for i in range(4):
        dense(f"mlp_out{i}", "w_mlp_out", 0, [_r((2 * i + n) * P) for n in range(2)], FF1)

    def gate_up(f, layer, j):
        blocks = []
        for kt in range(KT):
            blocks += [(f"{f}_w_gate_2", layer, _r(kt * P), _r(j * P)), (f"{f}_w_up_2", layer, _r(kt * P), _r(j * P))]
        group(f"{f}_{layer}_gu{j}", blocks)

    def down(f, layer):
        for i in range(4):
            dense(f"{f}_{layer}_down{i}", f"{f}_w_down_2", layer, [_r((2 * i + n) * P) for n in range(2)], FF2)

    for j in range(FF2):
        gate_up("ffn1", 0, j)
    down("ffn1", 0)
    for g in range(4):
        group(f"pool{g}", [("pool_w_2", g, _r(kt * P), _r(n * P)) for kt in range(2) for n in range(2)])
    for j in range(FF2):
        gate_up("ffn2", 0, j)
    down("ffn2", 0)
    dense("ckv", "w_dkv_2", None, [_r(0), _r(P)], KT)
    rope = _r(KVR * P, ROPE)
    swap = np.concatenate([rope[ROPE // 2:], rope[:ROPE // 2]])
    dense("krope", "w_dkv_2", None, [np.concatenate([rope, swap, rope, swap])], KT)
    for j in range(FF2):
        gate_up("ffn1", 1, j)
        if j == 3:
            for i in range(2):
                dense(f"uk{i}", "w_uk_2", None, [_r((2 * i + n) * P) for n in range(2)], KVR)
            group("uv", [("w_uv_2", None, _r(kt * P), _r(j4 * P)) for kt in range(KVR) for j4 in range(4)], True)
    down("ffn1", 1)
    dense("dq0", "w_dq_2", 0, [_r(0), _r(P)], KT)
    dense("dq1", "w_dq_2", 0, [_r(2 * P)], KT)
    head = lambda h: h * QK
    nope = [np.concatenate([_r(head(2 * j + n), HD) for n in range(2)]) for j in range(4)]
    for i in range(2):
        dense(f"uqn{i}", "w_uq_2", 0, nope[2 * i:2 * i + 2], QR)
    for i in range(2):
        rp = [_r(head(4 * i + n) + HD, ROPE) for n in range(4)]
        sw = [np.concatenate([r[ROPE // 2:], r[:ROPE // 2]]) for r in rp]
        dense(f"uqr{i}", "w_uq_2", 0, [np.concatenate(rp), np.concatenate(sw)], QR)
    for i in range(4):
        dense(f"wo{i}", "w_o_2", 0, [_r((2 * i + n) * P) for n in range(2)], 4)
    for j in range(FF2):
        gate_up("ffn2", 1, j)
    down("ffn2", 1)

    chunks, where, was_ada = [[]], {}, False
    for name, blocks, flush in groups:
        if (flush or was_ada) and chunks[-1]:
            chunks.append([])
        where[name], was_ada = [], name.startswith("ada")
        for b in blocks:
            if len(chunks[-1]) == CH:
                chunks.append([])
            where[name].append((len(chunks) - 1, len(chunks[-1])))
            chunks[-1].append(b)
    return chunks, where


def vector_plan():
    at, n = {}, 0
    for name, w in (("c", KT), ("ada_b", 6 * KT), ("norm1_g", KT), ("norm2_g", KT), ("final_g", KT),
                    ("ffn1_norm0", KT), ("ffn1_norm1", KT), ("mix_norm0", KT), ("mix_norm1", KT),
                    ("ffn2_norm0", KT), ("ffn2_norm1", KT), ("pool_scale", KT), ("kv_in_norm", KT),
                    ("final_norm", KT), ("kv_latent_norm", KVR), ("q_latent_norm", QR), ("sinks", SWA_HEADS)):
        at[name] = n
        n += w
    return at, n


def constant_plan():
    at, n = {}, 0
    for name, w in (("ident", P), ("cos", T), ("sin", T), ("mla_mask", T), ("count_fix", 4 * PADC)):
        at[name] = n
        n += w
    return at, n


def constants():
    at, n = constant_plan()
    out = np.zeros((P, n), np.float32)
    out[:, at["ident"]:at["ident"] + P] = np.eye(P, dtype=np.float32)
    inv = (1.0 / (np.float32(10000.0) ** (np.arange(0, ROPE, 2, dtype=np.float32) / ROPE))).astype(np.float32)
    ang = np.arange(T, dtype=np.float32)[None, :] * inv[:, None]
    cos, sin = np.cos(ang).astype(np.float32), np.sin(ang).astype(np.float32)
    for g in range(P // ROPE):
        r = g * ROPE
        out[r:r + ROPE, at["cos"]:at["cos"] + T] = np.concatenate([cos, cos])
        out[r:r + ROPE, at["sin"]:at["sin"] + T] = np.concatenate([-sin, sin])
    out[0:64, at["mla_mask"] + T - 64:at["mla_mask"] + T] = MASKED
    for g, w in enumerate(POOL_W):
        t = np.arange(PADC)
        out[:, at["count_fix"] + g * PADC:at["count_fix"] + (g + 1) * PADC] = w / np.minimum(t + 1, w)
    return out


def bias_constants():
    dist = 255 - np.arange(BIASC)
    n = np.maximum(dist, 0)
    half = NB // 2
    large = half + (np.log(np.maximum(n, 1).astype(np.float32) / half) / math.log(MAX_DISTANCE / half)
                    * (NB - half)).astype(np.int32)
    bucket = np.where(n < half, n, np.minimum(large, NB - 1))
    out = np.zeros((NB + 2, BIASC), np.float32)
    out[bucket, np.arange(BIASC)] = 1.0
    out[NB, (dist < 0) | (dist >= WINDOW)] = MASKED
    out[NB + 1, dist < 0] = MASKED
    sel = np.zeros((2, HEADS1), np.float32)
    sel[0, :SWA_HEADS] = 1.0
    sel[1, SWA_HEADS:] = 1.0
    return out, sel


class Counter:

    def __init__(self, sem):
        self.sem, self.value = sem, 0

    def add(self, n=1):
        self.value += n
        return (self, self.value)


class Queue:

    def __init__(self, engine, counter=None):
        self.engine, self.counter, self.passed = engine, counter, {}

    def do(self, make, after=(), signal=None):
        for token in after:
            if token is None:
                continue
            counter, value = token
            if self.passed.get(counter, 0) < value:
                self.passed[counter] = value
                self.engine.wait_ge(counter.sem, value)
        made = make(self.engine)
        if signal is False:
            return None
        counter, n = (self.counter, 1) if signal is None else signal
        made.then_inc(counter.sem, n)
        return counter.add(n)


def build_program(nc, xT, metaT, vecs, consts, bias_oh, bias_rows, wstream, scratch, outT):
    chunks, where = weight_plan()
    last_use = {}
    for name, places in where.items():
        for c, off in places:
            last_use[c] = max(last_use.get(c, 0), off)
    vat, vn = vector_plan()
    cat, cn = constant_plan()

    ctx = ExitStack()
    with ctx:
        def sb(name, shape, dt=F32, to=ctx):
            return to.enter_context(nc.sbuf_tensor("sb_" + name, shape, dt))

        def counter(name):
            return Counter(ctx.enter_context(nc.semaphore(name)))

        X = sb("X", [P, KT, T])
        xh, xl = sb("xh", [P, KT, T], F32R), sb("xl", [P, KT, T], F32R)
        raw = sb("raw", [P, NRAW, CH * P])
        whi, wlo = sb("whi", [P, NSPLIT, CH * P], F32R), sb("wlo", [P, NSPLIT, CH * P], F32R)
        vec = sb("vec", [P, vn])
        con = sb("con", [P, cn])
        mean_ones = sb("mean_ones", [P, 3, P])
        sumsq, sq = sb("sumsq", [P, T]), sb("sq", [P, 2, T])
        root, rstd, rstd2 = sb("root", [P, T]), sb("rstd", [P, T]), sb("rstd2", [P, T])
        mod, csil, g1m = sb("mod", [P, 6 * KT]), sb("csil", [P, KT]), sb("g1m", [P, 2 * KT])
        gu, hidf, tmp = sb("gu", [P, 2, 2, T]), sb("hidf", [P, 2, 2 * SEQ]), sb("tmp", [P, 2, T])
        shift_out = sb("shift_out", [P, 2, 2])
        eps_c, one_col = sb("eps_c", [P, 2]), sb("one_col", [P, 2])
        stat = sb("stat", [P, 4, 8])
        with ExitStack() as s:
            qk = sb("qk", [P, 13, SEQ], to=s)
            vtok = sb("vtok", [P, 2, 640], to=s)
            sig = sb("sig", [P, 16, SEQ], to=s)
            bias = sb("bias", [P, HEADS1, SEQ], to=s)
            sc1, p1, pT1 = (sb(n, [P, 2, 384], to=s) for n in ("sc1", "p1", "pT1"))
        with ExitStack() as s:
            U, SA, SB_ = (sb(n, [P, KT, PADC + T], to=s) for n in ("U", "SA", "SB"))
        with ExitStack() as s:
            qhead = sb("qhead", [QK, MH, SEQ], to=s)
            sc2, p2 = (sb(n, [P, 2, 416], to=s) for n in ("sc2", "p2"))
            pT2, pT2m = sb("pT2", [P, 2, 384], to=s), sb("pT2m", [META, 2, 256], to=s)
            cqf = sb("cqf", [P, QR, SEQ], to=s)
            cqh, cql = sb("cqh", [P, QR, SEQ], F32R, to=s), sb("cql", [P, QR, SEQ], F32R, to=s)
            o2h, o2l = sb("o2h", [P, 4, SEQ], F32R, to=s), sb("o2l", [P, 4, SEQ], F32R, to=s)
        hh, hl = sb("hh", [P, FF1 * SEQ], F32R), sb("hl", [P, FF1 * SEQ], F32R)
        with ExitStack() as s:
            boh, brow, brows = sb("boh", [NB + 2, BIASC], to=s), sb("brow", [NB + 2, HEADS1], to=s), sb("brows", [HEADS1, BIASC], to=s)
        with ExitStack() as s:
            khead = sb("khead", [QK, MH, T], to=s)
            v2 = sb("v2", [P, 3, MH * HD], to=s)
            krot = sb("krot", [ROPE, T], to=s)
        oh, ol = sb("oh", [P, 8, SEQ], F32R), sb("ol", [P, 8, SEQ], F32R)
        ckvf = sb("ckvf", [P, KVR, T])
        kvx = FF2 * T
        G = [ctx.enter_context(nc.psum_tensor(f"G{i}", [P, 2, 512], F32)) for i in range(2)]
        A = [ctx.enter_context(nc.psum_tensor(f"A{i}", [P, 512], F32)) for i in range(4)]

        pe_done, act_done, dve_done = counter("pe_done"), counter("act_done"), counter("dve_done")
        pool_done, hi_done, lo_done = counter("pool_done"), counter("hi_done"), counter("lo_done")
        loaded = [counter(f"loaded{i}") for i in range(NRAW)]
        small_in, x_in, con_in, meta_in = counter("small_in"), counter("x_in"), counter("con_in"), counter("meta_in")
        rows_in, rows_out, bias_in, stored = counter("rows_in"), counter("rows_out"), counter("bias_in"), counter("stored")
        pe, act, dve = Queue(nc.tensor, pe_done), Queue(nc.scalar, act_done), Queue(nc.vector, dve_done)
        pool, sp = Queue(nc.gpsimd, pool_done), Queue(nc.sync)

        def V(name, k=0, n=1):
            return vec[:, vat[name] + k:vat[name] + k + n]

        ident = con[:, cat["ident"]:cat["ident"] + P]
        f = lambda ap: ap.bitcast(F32)
        COLS1 = slice(META, T)

        vec_ok = sp.do(lambda e: e.dma_start(vec[:, :], vecs), signal=(small_in, 16))
        x_ok = sp.do(lambda e: e.dma_start(X[:, :, META:T], xT), signal=(x_in, 16))

        load_of, hi_of, lo_of, free_of = {}, {}, {}, {}
        plain = {c for n in where if n.startswith("ada") for c, _ in where[n]}

        def load_chunk(c):
            if c >= len(chunks) or c in load_of:
                return
            slot, w = c % NRAW, len(chunks[c]) * P
            before = [] if c < NRAW else [free_of[c - NRAW] if c - NRAW in plain else lo_of[c - NRAW]]
            load_of[c] = sp.do(lambda e: e.dma_start(raw[:, slot, 0:w], wstream[c, :, 0:w]), before, (loaded[slot], 16))

        split_at, split_order = {}, [c for c in range(len(chunks)) if c not in plain]
        for i, c in enumerate(split_order):
            split_at[c] = i

        def load_upto(c):
            for k in range(c + 1):
                if k not in load_of:
                    ok = k < NRAW or ((free_of if k - NRAW in plain else lo_of).get(k - NRAW) is not None)
                    if not ok:
                        return
                    load_chunk(k)

        def split_chunk(c):
            if c in lo_of:
                return
            load_upto(c)
            i, w, slot = split_at[c], len(chunks[c]) * P, c % NRAW
            s = i % NSPLIT
            before = free_of[split_order[i - NSPLIT]] if i >= NSPLIT else None
            hi_of[c] = act.do(lambda e: e.activation(whi[:, s, 0:w], raw[:, slot, 0:w], ACT.Copy), [load_of[c], before], (hi_done, 1))
            lo_of[c] = dve.do(lambda e: e.tensor_tensor(wlo[:, s, 0:w], raw[:, slot, 0:w], f(whi[:, s, 0:w]), ALU.subtract),
                              [hi_of[c], before], (lo_done, 1))
            load_upto(c + NRAW)

        def need(c):
            ahead = -1
            for k in range(c, min(c + NRAW - LOADING, len(chunks))):
                if k in plain:
                    load_upto(k)
                    continue
                ahead += 1
                if ahead > AHEAD:
                    break
                i = split_at[k]
                if i >= NSPLIT and split_order[i - NSPLIT] not in free_of:
                    break
                load_upto(k)
                if k not in load_of:
                    break
                split_chunk(k)

        def used(c, off, token_wanted):
            return token_wanted or off == last_use[c]

        def mark(c, off, token):
            if off == last_use[c]:
                free_of[c] = token
                load_upto(c + NRAW)

        def weights(c, off, n=1):
            s = split_at[c] % NSPLIT
            return whi[:, s, off * P:(off + n) * P], wlo[:, s, off * P:(off + n) * P]

        gnext, gfree = [0], [[], []]

        def next_pair():
            g = gnext[0] % 2
            gnext[0] += 1
            before, gfree[g] = list(gfree[g]), []
            return g, before

        def gemm(name, ntiles, nk, src, n, ready=None, pair=None, k0=0, ktotal=None):
            g, before = next_pair() if pair is None else (pair, [])
            ktotal = ktotal or nk
            places, i, token = where[name], 0, None
            for kt in range(k0, k0 + nk):
                for t in range(ntiles):
                    c, off = places[i]
                    i += 1
                    need(c)
                    xs, xr = src(kt)
                    w_h, w_l = weights(c, off)
                    waits = before + [hi_of[c], lo_of[c]] + (ready(kt) if ready else [])
                    out = G[g][:, t, 0:n]
                    first = lambda e: e.matmul(out, w_h, xs, start=kt == 0, stop=False)
                    pe.do(first, waits, signal=False)
                    pe.do(lambda e: e.matmul(out, w_h, xr, start=False, stop=False), signal=False)
                    end = i == nk * ntiles
                    last = lambda e: e.matmul(out, w_l, xs, start=False, stop=kt == ktotal - 1)
                    tok = pe.do(last, signal=None if used(c, off, end) else False)
                    mark(c, off, tok)
                    if end:
                        token = tok
            return g, token

        def token_major(name, width, nk, src, rows, tile0, ready=None):
            g, before = next_pair()
            places, nb, token = where[name], width // P, None
            for kt in range(nk):
                c, off = places[kt * nb]
                need(c)
                w_h, w_l = weights(c, off, nb)
                for i, (a, m) in enumerate(rows):
                    xs, xr = src(kt, a, m)
                    out = G[g][0:m, i, 0:width]
                    waits = before + [hi_of[c], lo_of[c]] + (ready(kt) if ready else [])
                    for j, (s_, m_) in enumerate(((xs, w_h), (xr, w_h), (xs, w_l))):
                        end = i == len(rows) - 1 and j == 2
                        fn = lambda e: e.matmul(out, s_, m_, start=kt == 0 and j == 0, stop=kt == nk - 1 and j == 2)
                        tok = pe.do(fn, waits, None if end else False)
                    if i == len(rows) - 1:
                        if tile0:
                            mark(c, off + nb - 1, tok)
                        token = tok
            return g, token

        def split_out(hi, lo, src, after, scale=None, bias_=None, in1=None):
            kw = {}
            if scale is not None:
                kw["scale"] = scale
            if bias_ is not None:
                kw["bias"] = bias_
            fn = ACT.Copy if bias_ is None and scale is None else ACT.Identity
            th = act.do(lambda e: e.activation(hi, src, fn, **kw), after)
            if scale is not None:
                tl = dve.do(lambda e: e.scalar_tensor_tensor(lo, src, scale, f(hi), ALU.mult, ALU.subtract), [th] + after)
            elif bias_ is not None:
                tl = dve.do(lambda e: e.scalar_tensor_tensor(lo, src, bias_, f(hi), ALU.add, ALU.subtract), [th] + after)
            else:
                tl = dve.do(lambda e: e.tensor_tensor(lo, src, f(hi), ALU.subtract), [th] + after)
            return [th, tl]

        sq_state = dict(n=0, tok=None, used=None)

        def square_in(src, first, cols, after):
            dst = sumsq[:, cols]
            if first:
                sq_state["tok"] = pool.do(lambda e: e.tensor_tensor(dst, src, src, ALU.mult), after + [sq_state["used"]])
            else:
                s = sq[:, sq_state["n"] % 2, cols]
                sq_state["n"] += 1
                a = pool.do(lambda e: e.tensor_tensor(s, src, src, ALU.mult), after)
                sq_state["tok"] = pool.do(lambda e: e.tensor_tensor(dst, dst, s, ALU.add), [a, sq_state["tok"]])

        afree = [[], [], [], []]

        def rstd_of(which, dst, cols):
            n = cols.stop - cols.start
            t = pe.do(lambda e: e.matmul(A[0][:, 0:n], mean_ones[:, which, :], sumsq[:, cols], start=True, stop=True),
                      [sq_state["tok"]] + afree[0])
            sq_state["used"] = t
            r = act.do(lambda e: e.activation(root[:, cols], A[0][:, 0:n], ACT.Sqrt, bias=eps_c[:, 0:1]), [t])
            afree[0] = [r]
            return dve.do(lambda e: e.reciprocal(dst[:, cols], root[:, cols]), [r])

        def norm_input(hi, lo, gain, cols):
            ready = {}

            def tile(kt, tok):
                ready[kt] = split_out(hi(kt), lo(kt), X[:, kt, cols], [tok], scale=V(gain, kt))
            return ready, tile

        dve.do(lambda e: e.memset(eps_c[:, :], EPS))
        dve.do(lambda e: e.memset(one_col[:, :], 1.0))
        for i, n in enumerate((D, KVR * P, QR * P)):
            ones_t = dve.do(lambda e: e.memset(mean_ones[:, i, :], 1.0 / n))
        load_upto(NRAW - 1)
        for kt in range(KT):
            square_in(X[:, kt, COLS1], kt == 0, COLS1, [x_ok])
        cs = act.do(lambda e: e.activation(csil[:, :], V("c", 0, KT), ACT.Silu), [vec_ok])
        afree[0] = [ones_t]
        ada_free, ada_sum, ada_total = [None, None], [None, None], [None, None]

        ada_sets = [(gu[:, 0, :, :].rearrange("p a b -> p (a b)")[:, 0:4 * P], gu[:, 1, :, :].rearrange("p a b -> p (a b)")[:, 0:4 * P]),
                    (hidf[:, 0, :], hidf[:, 1, :])]

        def ada_set(i):
            return 0 if i >= 10 else i % 2

        def ada_piece(i, part):
            c, off = where[f"ada{i}_{part}"][0]
            need(c)
            for odd in range(2):
                kt = 2 * part + odd
                acc, w = ada_sets[ada_set(i)][odd], raw[:, c % NRAW, odd * 4 * P:(odd + 1) * 4 * P]
                if part == 0:
                    t = dve.do(lambda e: e.tensor_scalar(acc, w, csil[:, kt:kt + 1], None, ALU.mult), [load_of[c], cs, ada_free[ada_set(i)]])
                else:
                    t = dve.do(lambda e: e.scalar_tensor_tensor(acc, w, csil[:, kt:kt + 1], acc, ALU.mult, ALU.add),
                               [load_of[c], ada_sum[odd]])
                ada_sum[odd] = t
            mark(c, CH - 1, t)
            if part == 3:
                even, odd = ada_sets[ada_set(i)]
                ada_total[ada_set(i)] = dve.do(lambda e: e.tensor_tensor(even, even, odd, ALU.add), ada_sum)

        def ada_finish(i):
            g, before = next_pair()
            acc = ada_sets[ada_set(i)][0]
            for t in range(4):
                tok = pe.do(lambda e: e.matmul(G[g][:, 0, t:t + 1], acc[:, t * P:(t + 1) * P], one_col[:, 0:1], start=True, stop=True),
                            before + [ada_total[ada_set(i)], ones_t], None if t == 3 else False)
            ada_free[ada_set(i)] = tok
            m = dve.do(lambda e: e.tensor_tensor(mod[:, 4 * i:4 * i + 4], G[g][:, 0, 0:4], V("ada_b", 4 * i, 4), ALU.add), [tok, vec_ok])
            gfree[g] = [m]
            return m

        for i in range(4):
            for part in range(4):
                ada_piece(i, part)
            m = ada_finish(i)
            if i == 0:
                con_ok = sp.do(lambda e: e.dma_start(con[:, :], consts), signal=(con_in, 16))
                sp.do(lambda e: e.dma_start(boh[:, :], bias_oh), signal=(rows_in, 16))
                rin = sp.do(lambda e: e.dma_start(brow[:, :], bias_rows), signal=(rows_in, 16))
        bt = pe.do(lambda e: e.matmul(A[1][0:HEADS1, 0:BIASC], brow[:, :], boh[:, :], start=True, stop=True), [rin])
        bt = dve.do(lambda e: e.tensor_copy(brows[:, :], A[1][0:HEADS1, 0:BIASC]), [bt])
        afree[1] = [bt]
        ro = pool.do(lambda e: e.dma_start(scratch[:, 0:BIASC], brows[:, :]), [bt], (rows_out, 16))
        hankel = bass.AP(scratch.tensor, 0, [[1, P], [512, HEADS1], [1, SEQ]])
        bias_ok = pool.do(lambda e: e.dma_start(bias[:, :, :], hankel), [ro], (bias_in, 16))

        r1 = rstd_of(0, rstd, COLS1)
        def mod_gain(dst, gname, k, after):
            a = dve.do(lambda e: e.tensor_scalar(dst, mod[:, k:k + KT], 1.0, None, ALU.add), after)
            return dve.do(lambda e: e.tensor_tensor(dst, dst, V(gname, 0, KT), ALU.mult), [a, vec_ok])

        def modulated(goff, shift, ready_t, rs):
            ready = {}
            for kt in range(KT):
                b = kt % 2
                t = dve.do(lambda e: e.scalar_tensor_tensor(tmp[:, b, 0:SEQ], X[:, kt, COLS1], g1m[:, goff + kt:goff + kt + 1],
                                                                            rstd[:, COLS1], ALU.mult, ALU.mult),
                           ready_t + [rs] + (ready[kt - 2] if kt >= 2 else []))
                ready[kt] = split_out(xh[:, kt, COLS1], xl[:, kt, COLS1], tmp[:, b, 0:SEQ], [t], bias_=mod[:, shift + kt:shift + kt + 1])
            return ready

        gm = mod_gain(g1m[:, 0:KT], "norm1_g", KT, [m])
        ready = modulated(0, 0, [gm], r1)
        src1 = lambda kt: (xh[:, kt, COLS1], xl[:, kt, COLS1])

        qk_ok = {}
        REV = lambda ap: ap[:, :, ::-1]
        for i in range(7):
            nt = 2 if i < 6 else 1
            ada_piece(*ADA_QK[i])
            g, tok = gemm(f"qk{i}", nt, KT, src1, SEQ, lambda kt: ready[kt])
            fr = []
            for t in range(nt):
                ti = 2 * i + t
                isq = 1 <= ti <= 4 or ti >= 9
                dst = qk[:, ti, :].rearrange("p (b q) -> p b q", b=2)
                ps = G[g][:, t, 0:SEQ].rearrange("p (b q) -> p b q", b=2)
                ps = REV(ps) if isq else ps
                if t == 0:
                    qk_ok[ti] = act.do(lambda e: e.activation(dst, ps, ACT.Copy), [tok])
                else:
                    qk_ok[ti] = dve.do(lambda e: e.tensor_copy(dst, ps), [tok])
                fr.append(qk_ok[ti])
            gfree[g] = fr
            if i == 4:
                ada_finish(4)
        vsrc = lambda kt, a, m: (xh[:, kt, META + a:META + a + m], xl[:, kt, META + a:META + a + m])
        v_ok = []
        ada_piece(*ADA_QK[7])
        for name, w, c0 in (("va", P, 0), ("vb", 4 * P, P)):
            g, tok = token_major(name, w, KT, vsrc, [(0, P), (P, P)], True)
            a_ = act.do(lambda e: e.activation(vtok[:, 0, c0:c0 + w], G[g][:, 0, 0:w], ACT.Copy), [tok])
            b_ = dve.do(lambda e: e.tensor_copy(vtok[:, 1, c0:c0 + w], G[g][:, 1, 0:w]), [tok])
            gfree[g] = [a_, b_]
            v_ok += [a_, b_]
        ada_finish(5)

        heads = [dict(q=1 + h % 4, k=0, row=(h // 4) * HD, v=(h // 4) * HD, bias=h, out=h % 4, sink=h) for h in (0, 4, 1, 5, 2, 6, 3, 7)]
        heads += [dict(q=9 + h // 2, k=5 + h // 2, row=(h % 2) * HD, v=P + h * HD, bias=8 + h, out=4 + h // 2, sink=None) for h in range(8)]
        s_tok, e_tok, pt_tok, pv_tok, o_ok, pT_free = {}, {}, {}, {}, {}, {}

        def scores1(i):
            h = heads[i]
            r, bank, b = h["row"], A[i % 2], i % 2
            q = lambda n: qk[r:r + HD, h["q"], n * P:(n + 1) * P]
            k = lambda w: qk[r:r + HD, h["k"], 0:w]
            pe.do(lambda e: e.matmul(bank[:, 0:SEQ], q(1), k(SEQ), start=True, stop=True), [qk_ok[h["q"]], qk_ok[h["k"]]] + afree[i % 2], False)
            t = pe.do(lambda e: e.matmul(bank[:, SEQ:SEQ + P], q(0), k(P), start=True, stop=True))
            w = [t, bias_ok] + ([e_tok[i - 2]] if i >= 2 else [])
            dve.do(lambda e: e.scalar_tensor_tensor(sc1[:, b, 0:SEQ], bank[:, 0:SEQ], HD ** -0.5, bias[:, h["bias"], :], ALU.mult, ALU.add), w, False)
            t = dve.do(lambda e: e.scalar_tensor_tensor(sc1[:, b, SEQ:SEQ + P], bank[:, SEQ:SEQ + P], HD ** -0.5, bias[:, h["bias"], P:SEQ],
                                                        ALU.mult, ALU.add))
            afree[i % 2] = [t]
            st = stat[:, i % 4, :]
            mx = st[:, 6:8]
            neg = h["sink"] is None
            md = st[:, 0:2] if neg else mx
            dve.do(lambda e: e.tensor_reduce(md[:, 0:1], sc1[:, b, 0:SEQ], AX_X, ALU.max, negate=neg), [t], False)
            t = dve.do(lambda e: e.tensor_reduce(md[:, 1:2], sc1[:, b, SEQ:SEQ + P], AX_X, ALU.max, negate=neg))
            if not neg:
                sink = V("sinks", h["sink"])
                t = dve.do(lambda e: e.tensor_scalar(st[:, 0:2], mx, sink, -1.0, ALU.max, ALU.mult), [t])
            act.do(lambda e: e.activation(p1[:, b, 0:SEQ], sc1[:, b, 0:SEQ], ACT.Exp, bias=st[:, 0:1], accum_out=st[:, 2:3]),
                   [t] + ([pt_tok[i - 2]] if i >= 2 else []))
            u = act.do(lambda e: e.activation(p1[:, b, SEQ:384], sc1[:, b, SEQ:384], ACT.Exp, bias=st[:, 1:2], accum_out=st[:, 3:4]))
            e_tok[i] = u

        def weights1(i):
            h, b, st, u = heads[i], i % 2, stat[:, i % 4, :], e_tok[i]
            if h["sink"] is not None:
                sink = V("sinks", h["sink"])
                sk = act.do(lambda e: e.activation(st[:, 4:6], st[:, 0:2], ACT.Exp, bias=sink))
                u2 = dve.do(lambda e: e.tensor_tensor(st[:, 4:6], st[:, 4:6], st[:, 2:4], ALU.add), [sk, u])
                u2 = dve.do(lambda e: e.reciprocal(st[:, 4:6], st[:, 4:6]), [u2])
            else:
                u2 = dve.do(lambda e: e.reciprocal(st[:, 4:6], st[:, 2:4]), [u])
            pool.do(lambda e: e.tensor_scalar(p1[:, b, 0:SEQ], p1[:, b, 0:SEQ], st[:, 4:5], None, ALU.mult), [u2], False)
            s_tok[i] = pool.do(lambda e: e.tensor_scalar(p1[:, b, SEQ:384], p1[:, b, SEQ:384], st[:, 5:6], None, ALU.mult))

        def transposes1(i):
            b = i % 2
            for j in range(3):
                t = pe.do(lambda e: e.transpose(A[2][:, j * P:(j + 1) * P], p1[:, b, j * P:(j + 1) * P], ident),
                          [s_tok[i], con_ok] + afree[2], None if j == 2 else False)
            pt_tok[i] = t
            c = act.do(lambda e: e.activation(pT1[:, b, :], A[2][:, 0:384], ACT.Copy), [t] + ([pv_tok[i - 2]] if i >= 2 else []))
            afree[2] = [c]
            pT_free[i] = c

        def values1(i):
            h, b, half = heads[i], i % 2, i % 2
            vv = lambda kt: vtok[:, kt, h["v"]:h["v"] + HD]
            o = A[3][half * HD:(half + 1) * HD, :]
            pe.do(lambda e: e.matmul(o[:, P:SEQ], vv(0), pT1[:, b, 0:P], start=True, stop=False), [pT_free[i]] + v_ok + afree[3], False)
            pe.do(lambda e: e.matmul(o[:, P:SEQ], vv(1), pT1[:, b, P:SEQ], start=False, stop=True), signal=False)
            t = pe.do(lambda e: e.matmul(o[:, 0:P], vv(0), pT1[:, b, SEQ:384], start=True, stop=True))
            pv_tok[i] = t
            if half:
                tile = h["out"]
                ps = REV(A[3][:, 0:SEQ].rearrange("p (b q) -> p b q", b=2))
                d = lambda x: x[:, tile, :].rearrange("p (b q) -> p b q", b=2)
                o_ok[tile] = split_out(d(oh), d(ol), ps, [t])
                afree[3] = o_ok[tile]

        sig_ok = {}

        gate_pair = [None]

        def gates(i):
            half = i % 2
            g, tok = gemm(f"gate{i}", 2, 4, src1, SEQ, lambda kt: ready[kt], gate_pair[0] if half else None, 4 * half, KT)
            gate_pair[0] = g
            if half:
                d = sig[:, i - 1:i + 1, :]
                a_ = act.do(lambda e: e.activation(d, G[g][:, :, 0:SEQ], ACT.Tanh, scale=0.5), [tok])
                gfree[g] = [a_]
                sig_ok[i // 2] = dve.do(lambda e: e.tensor_scalar(d, d, 0.5, 0.5, ALU.mult, ALU.add), [a_])

        for i in range(HEADS1 + 2):
            if i < HEADS1:
                scores1(i)
                ada_piece(*ADA_HEADS[i])
                gates(i)
            if 1 <= i <= HEADS1:
                transposes1(i - 1)
            if i < HEADS1:
                weights1(i)
            if i >= 2:
                values1(i - 2)
            if i % 4 == 1 and 5 <= i < 17:
                ada_finish(6 + i // 4 - 1)
        m = ada_finish(9)
        afree[1] = afree[1] + [s_tok[15]]
        afree[0] = afree[0] + [s_tok[15]]

        merged_ok = {}
        merged = lambda kt, nt=1: (hh[:, kt * SEQ:(kt + nt) * SEQ], hh[:, (KT + kt) * SEQ:(KT + kt + nt) * SEQ])
        for i in range(4):
            ga_, ta = gemm(f"bra{i}", 2, 4, lambda kt: (oh[:, kt, :], ol[:, kt, :]), SEQ, lambda kt: o_ok[kt])
            gb_, tb = gemm(f"brb{i}", 2, 4, lambda kt: (oh[:, 4 + kt, :], ol[:, 4 + kt, :]), SEQ, lambda kt: o_ok[4 + kt])
            hb = hidf[:, i % 2, :].rearrange("p (t q) -> p t q", t=2)
            sa, sb2 = sig[:, 2 * i:2 * i + 2, :], sig[:, 8 + 2 * i:10 + 2 * i, :]
            a_ = dve.do(lambda e: e.tensor_tensor(sa, sa, G[ga_][:, :, 0:SEQ], ALU.mult), [ta, sig_ok[i], sig_ok[4 + i]])
            b_ = dve.do(lambda e: e.tensor_tensor(sb2, sb2, G[gb_][:, :, 0:SEQ], ALU.mult), [tb])
            gfree[ga_], gfree[gb_] = [a_], [b_]
            c_ = dve.do(lambda e: e.tensor_tensor(hb, sa, sb2, ALU.add), [a_, b_] + (merged_ok[2 * i - 4] if i >= 2 else []))
            merged_ok[2 * i] = merged_ok[2 * i + 1] = split_out(merged(2 * i, 2)[0].rearrange("p (t q) -> p t q", t=2),
                                                                merged(2 * i, 2)[1].rearrange("p (t q) -> p t q", t=2), hb, [c_])

        def add_residual(g, tok, i, cols, scalar, hooks, after=()):
            n = cols.stop - cols.start
            fr = []
            for t in range(2):
                kt = 2 * i + t
                s_ = scalar(kt) if callable(scalar) else scalar
                fr.append(dve.do(lambda e: e.scalar_tensor_tensor(X[:, kt, cols], G[g][:, t, 0:n], s_, X[:, kt, cols],
                                                                                      ALU.mult, ALU.add), [tok] + list(after)))
                square_in(X[:, kt, cols], kt == 0, cols, [fr[-1]])
                for hook in hooks:
                    hook(kt, fr[-1])
            gfree[g] = fr
            return fr[-1]

        gm2 = mod_gain(g1m[:, KT:2 * KT], "norm2_g", 4 * KT, [m])
        SHIFT = slice(META - 2, T)
        sh_cols = lambda t: t[:, :, META - 2:META]
        shift2 = mod[:, 3 * KT:4 * KT].unsqueeze(2).broadcast_to([P, KT, 2])
        shift_ok = split_out(sh_cols(xh), sh_cols(xl), shift2, [m] + merged_ok[0])
        ready2 = {}

        def prep2(kt, tok):
            ready2[kt] = split_out(xh[:, kt, COLS1], xl[:, kt, COLS1], X[:, kt, COLS1], [tok, gm2], scale=g1m[:, KT + kt:KT + kt + 1]) + shift_ok
        for i in range(4):
            g, tok = gemm(f"wout{i}", 2, KT, merged, SEQ, lambda kt: merged_ok[kt])
            add_residual(g, tok, i, COLS1, lambda kt: mod[:, 2 * KT + kt:2 * KT + kt + 1], [prep2])

        hid_ok, hf_free, squared = {}, [[], []], {}

        def split_hidden(i):
            sl = slice(2 * i * SEQ, (2 * i + 2) * SEQ)
            hid_ok[2 * i] = hid_ok[2 * i + 1] = hf_free[i % 2] = split_out(hh[:, sl], hl[:, sl], hidf[:, i % 2, :], [squared[i]])

        meta_ok = pool.do(lambda e: e.dma_start(X[:, :, 0:META], metaT), signal=(meta_in, 16))
        for i in range(FF1 // 2):
            if i % 2 == 0:
                ada_piece(*ADA_MLP[i // 2])
            g, tok = gemm(f"mlp_in{i}", 2, KT, lambda kt: (xh[:, kt, SHIFT], xl[:, kt, SHIFT]), SEQ + 2, lambda kt: ready2[kt])
            if i == 0:
                r = rstd_of(0, rstd, COLS1)
            if i == 7:
                m = ada_finish(10)
            if i:
                split_hidden(i - 1)
            b = i % 2
            hb = hidf[:, b, :].rearrange("p (t q) -> p t q", t=2)
            rb = rstd[:, COLS1].unsqueeze(1).broadcast_to([P, 2, SEQ])
            w = dve.do(lambda e: e.tensor_copy(shift_out[:, b, :], G[g][:, :, 0]), [tok] + hf_free[b])
            c_ = dve.do(lambda e: e.tensor_tensor(hb, G[g][:, :, 2:2 + SEQ], rb, ALU.mult), [r])
            gfree[g] = [c_]
            for t in range(2):
                a_ = act.do(lambda e: e.activation(hb[:, t, :], hb[:, t, :], ACT.Relu, bias=shift_out[:, b, t:t + 1]), [c_])
            squared[i] = act.do(lambda e: e.activation(hb, hb, ACT.Square), [a_])
        split_hidden(FF1 // 2 - 1)
        hid1 = lambda kt: (hh[:, kt * SEQ:(kt + 1) * SEQ], hl[:, kt * SEQ:(kt + 1) * SEQ])
        for i in range(4):
            g, tok = gemm(f"mlp_out{i}", 2, FF1, hid1, SEQ, lambda kt: hid_ok[kt])
            if i == 0:
                m = ada_finish(11)
            add_residual(g, tok, i, COLS1, lambda kt: mod[:, 5 * KT + kt:5 * KT + kt + 1], [], [m])

        ALL = slice(0, T)
        r = rstd_of(0, rstd, COLS1)
        full = lambda t: (lambda kt: t[:, kt, :])
        ready3, prep = norm_input(full(xh), full(xl), "ffn1_norm0", ALL)
        for kt in range(KT):
            t = dve.do(lambda e: e.scalar_tensor_tensor(X[:, kt, COLS1], X[:, kt, COLS1], V("final_g", kt), rstd[:, COLS1],
                                                                     ALU.mult, ALU.mult), [r, meta_ok, sq_state["tok"]])
            square_in(X[:, kt, ALL], kt == 0, ALL, [t])
            prep(kt, t)

        def swiglu(f_, layer, ready, cols, hooks, between=None, rs=None, gu_after=()):
            n = cols.stop - cols.start
            hid_ok, h_free, gu_free = {}, [[], []], [list(gu_after), list(gu_after)]
            src = lambda kt: (xh[:, kt, cols], xl[:, kt, cols])
            for j in range(FF2):
                g, tok = gemm(f"{f_}_{layer}_gu{j}", 2, KT, src, n, lambda kt: ready[kt])
                if j == 0 and rs is None:
                    rs = rstd_of(0, rstd, cols)
                b = j % 2
                rb = rstd[:, cols].unsqueeze(1).broadcast_to([P, 2, n])
                a_ = dve.do(lambda e: e.tensor_tensor(gu[:, b, :, 0:n], G[g][:, :, 0:n], rb, ALU.mult),
                            [tok, rs] + gu_free[b])
                gfree[g] = [a_]
                s_ = act.do(lambda e: e.activation(gu[:, b, 0, 0:n], gu[:, b, 0, 0:n], ACT.Silu), [a_])
                c_ = dve.do(lambda e: e.tensor_tensor(hidf[:, b, 0:n], gu[:, b, 0, 0:n], gu[:, b, 1, 0:n], ALU.mult),
                            [s_] + h_free[b])
                gu_free[b] = [c_]
                sl = slice(j * n, (j + 1) * n)
                hid_ok[j] = split_out(hh[:, sl], hl[:, sl], hidf[:, b, 0:n], [c_])
                h_free[b] = hid_ok[j]
                if between and j == 3:
                    between()
            hid = lambda kt: (hh[:, kt * n:(kt + 1) * n], hl[:, kt * n:(kt + 1) * n])
            for i in range(4):
                g, tok = gemm(f"{f_}_{layer}_down{i}", 2, FF2, hid, n, lambda kt: hid_ok[kt])
                last = add_residual(g, tok, i, cols, 0.5, hooks)
            return last

        mix0_ready, prep_mix0 = norm_input(full(xh), full(xl), "mix_norm0", ALL)
        swiglu("ffn1", 0, ready3, ALL, [prep_mix0])

        r = None
        body = slice(PADC, PADC + T)
        ready4, prep = norm_input(full(xh), full(xl), "ffn2_norm0", ALL)
        zs = []
        for gi in range(4):
            g, tok = gemm(f"pool{gi}", 2, 2, lambda kt: (xh[:, 2 * gi + kt, :], xl[:, 2 * gi + kt, :]), T, lambda kt: mix0_ready[2 * gi + kt])
            if gi == 0:
                r = rstd_of(0, rstd, ALL)
                pad_t = pool.do(lambda e: e.memset(U[:, :, 0:PADC], 0.0), [r])
            zs.append(dve.do(lambda e: e.tensor_tensor(U[:, 2 * gi:2 * gi + 2, body], G[g][:, :, 0:T],
                                                       rstd[:, :].unsqueeze(1).broadcast_to([P, 2, T]), ALU.mult), [tok, r]))
            gfree[g] = [zs[-1]]
        for gi in range(4):
            ks = slice(2 * gi, 2 * gi + 2)
            eng = dve if gi != 2 else pool
            cur, lo_, nxt, deps = U, 1, (SA, SB_), [zs[gi], pad_t]
            for st in range(gi + 1):
                sh = 1 << st
                dst = nxt[st % 2]
                t = eng.do(lambda e: e.tensor_tensor(dst[:, ks, lo_:PADC + T], cur[:, ks, lo_:PADC + T], cur[:, ks, lo_ - sh:PADC + T - sh], ALU.add), deps)
                deps, cur, lo_ = [t], dst, lo_ + 2 * sh
            w = POOL_W[gi]
            fix = con[:, cat["count_fix"] + gi * PADC:cat["count_fix"] + gi * PADC + w].unsqueeze(1).broadcast_to([P, 2, w])
            t = eng.do(lambda e: e.tensor_tensor(cur[:, ks, PADC:PADC + w], cur[:, ks, PADC:PADC + w], fix, ALU.mult), [t, con_ok])
            t = dve.do(lambda e: e.scalar_tensor_tensor(cur[:, ks, body], cur[:, ks, body], 1.0 / w, U[:, ks, body], ALU.mult, ALU.subtract), [t])
            for kt in (2 * gi, 2 * gi + 1):
                a_ = dve.do(lambda e: e.scalar_tensor_tensor(X[:, kt, :], cur[:, kt, body], V("pool_scale", kt), X[:, kt, :], ALU.mult, ALU.add),
                            [t, sq_state["used"]])
                square_in(X[:, kt, :], kt == 0, ALL, [a_])
                prep(kt, a_)
        kv_ready, prep_kv = norm_input(lambda kt: hh[:, kvx + kt * T:kvx + (kt + 1) * T], lambda kt: hl[:, kvx + kt * T:kvx + (kt + 1) * T],
                                       "kv_in_norm", ALL)
        ready5, prep5 = norm_input(full(xh), full(xl), "ffn1_norm1", ALL)
        swiglu("ffn2", 0, ready4, ALL, [prep_kv, prep5])

        kvsrc = lambda kt: (hh[:, kvx + kt * T:kvx + (kt + 1) * T], hl[:, kvx + kt * T:kvx + (kt + 1) * T])
        g, tok = gemm("ckv", 2, KT, kvsrc, T, lambda kt: kv_ready[kt])
        rs1 = rstd_of(0, rstd, ALL)
        rb = rstd[:, :].unsqueeze(1).broadcast_to([P, 2, T])
        ck = dve.do(lambda e: e.tensor_tensor(gu[:, 0, :, :], G[g][:, :, 0:T], rb, ALU.mult), [tok, rs1])
        gfree[g] = [ck]
        g, tok = gemm("krope", 1, KT, kvsrc, T, lambda kt: kv_ready[kt])
        for kt in range(KVR):
            square_in(gu[:, 0, kt, :], kt == 0, ALL, [ck])
        ka_ = dve.do(lambda e: e.tensor_tensor(tmp[0:64, 0, :], G[g][0:64, 0, 0:T], rstd[0:64, :], ALU.mult), [tok, rs1])
        gfree[g] = [ka_]
        cosT, sinT = (lambda r0, r1, c: con[r0:r1, cat["cos"] + c.start:cat["cos"] + c.stop]), (lambda r0, r1, c: con[r0:r1, cat["sin"] + c.start:cat["sin"] + c.stop])
        kb_ = dve.do(lambda e: e.tensor_tensor(krot[:, :], tmp[0:32, 0, :], cosT(0, 32, ALL), ALU.mult), [ka_])
        kc_ = dve.do(lambda e: e.tensor_tensor(tmp[0:32, 1, :], tmp[32:64, 0, :], sinT(32, 64, ALL), ALU.mult), [kb_])
        kd_ = dve.do(lambda e: e.tensor_tensor(krot[:, :], krot[:, :], tmp[0:32, 1, :], ALU.add), [kc_])
        kr_ok = dve.do(lambda e: e.tensor_copy(khead[HD:QK, :, :], krot[:, :].unsqueeze(1).broadcast_to([ROPE, MH, T])), [kd_])
        kv_done = {}

        def kv_up():
            rk = rstd_of(1, rstd2, ALL)
            for kt in range(KVR):
                t = dve.do(lambda e: e.scalar_tensor_tensor(tmp[:, kt, :], ckvf[:, kt, :], V("kv_latent_norm", kt), rstd2[:, :],
                                                                         ALU.mult, ALU.mult), [rk, cc, kd_])
                c0 = kvx + kt * T
                kv_done[kt] = split_out(hh[:, c0:c0 + T], hl[:, c0:c0 + T], tmp[:, kt, :], [t, tok])
            lat = lambda kt: (hh[:, kvx + kt * T:kvx + (kt + 1) * T], hl[:, kvx + kt * T:kvx + (kt + 1) * T])
            ks = []
            for i in range(2):
                g_, tk = gemm(f"uk{i}", 2, KVR, lat, T, lambda kt: kv_done[kt])
                a_ = act.do(lambda e: e.activation(khead[0:HD, 4 * i:4 * i + 4:2, :], G[g_][0:HD, :, 0:T], ACT.Copy), [tk])
                b_ = dve.do(lambda e: e.tensor_copy(khead[0:HD, 4 * i + 1:4 * i + 4:2, :], G[g_][HD:P, :, 0:T]), [tk, a_])
                gfree[g_] = [a_, b_]
                ks += [a_, b_]
            lat_t = lambda kt, a, m_: (hh[:, kvx + kt * T + a:kvx + kt * T + a + m_], hl[:, kvx + kt * T + a:kvx + kt * T + a + m_])
            g_, tk = token_major("uv", 4 * P, KVR, lat_t, [(0, P), (P, P)], False)
            a_ = act.do(lambda e: e.activation(v2[:, 0, :], G[g_][:, 0, :], ACT.Copy), [tk])
            b_ = dve.do(lambda e: e.tensor_copy(v2[:, 1, :], G[g_][:, 1, :]), [tk])
            gfree[g_] = [a_, b_]
            g2, tk = token_major("uv", 4 * P, KVR, lat_t, [(2 * P, META)], True)
            c_ = act.do(lambda e: e.activation(v2[0:META, 2, :], G[g2][0:META, 0, :], ACT.Copy), [tk])
            gfree[g2] = [c_]
            kv_done["k"], kv_done["v"] = ks + [kr_ok], [a_, b_, c_]

        cc = pool.do(lambda e: e.tensor_copy(ckvf[:, :, :], gu[:, 0, :, :]), [ck])
        mix_ready, prep_mix = norm_input(lambda kt: xh[:, kt, COLS1], lambda kt: xl[:, kt, COLS1], "mix_norm1", COLS1)


        swiglu("ffn1", 1, ready5, COLS1, [prep_mix], kv_up, rs1, [cc])

        g, tok = gemm("dq0", 2, KT, src1, SEQ, lambda kt: mix_ready[kt])
        r = rstd_of(0, rstd, COLS1)
        rb2 = rstd[:, COLS1].unsqueeze(1).broadcast_to([P, 2, SEQ])
        cq = [dve.do(lambda e: e.tensor_tensor(cqf[:, 0:2, :], G[g][:, :, 0:SEQ], rb2, ALU.mult), [tok, r])] * 2
        gfree[g] = [cq[0]]
        g, tok = gemm("dq1", 1, KT, src1, SEQ, lambda kt: mix_ready[kt])
        cq.append(dve.do(lambda e: e.tensor_tensor(cqf[:, 2, :], G[g][:, 0, 0:SEQ], rstd[:, COLS1], ALU.mult), [tok, r]))
        gfree[g] = [cq[2]]
        cq_ok = {}
        for kt in range(QR):
            square_in(cqf[:, kt, :], kt == 0, COLS1, [cq[kt]])
            cq_ok[kt] = split_out(cqh[:, kt, :], cql[:, kt, :], cqf[:, kt, :], [cq[kt]], scale=V("q_latent_norm", kt))
        cqs = lambda kt: (cqh[:, kt, :], cql[:, kt, :])
        q_ok = []
        for i in range(2):
            g, tok = gemm(f"uqn{i}", 2, QR, cqs, SEQ, lambda kt: cq_ok[kt])
            if i == 0:
                rq = rstd_of(2, rstd2, COLS1)
            r64 = lambda lo_: rstd2[lo_:lo_ + HD, COLS1].unsqueeze(1).broadcast_to([HD, 2, SEQ])
            a_ = dve.do(lambda e: e.tensor_tensor(qhead[0:HD, 4 * i:4 * i + 4:2, :], G[g][0:HD, :, 0:SEQ], r64(0), ALU.mult), [tok, rq])
            b_ = dve.do(lambda e: e.tensor_tensor(qhead[0:HD, 4 * i + 1:4 * i + 4:2, :], G[g][HD:P, :, 0:SEQ], r64(HD), ALU.mult), [tok, rq])
            gfree[g] = [a_, b_]
            q_ok += [a_, b_]
        ra = dve.do(lambda e: e.tensor_tensor(gu[:, 0, 0, 0:SEQ], rstd2[:, COLS1], cosT(0, P, COLS1), ALU.mult), [rq])
        rb_ = dve.do(lambda e: e.tensor_tensor(gu[:, 0, 1, 0:SEQ], rstd2[:, COLS1], sinT(0, P, COLS1), ALU.mult), [rq])
        for i in range(2):
            g, tok = gemm(f"uqr{i}", 2, QR, cqs, SEQ, lambda kt: cq_ok[kt])
            a_ = dve.do(lambda e: e.tensor_tensor(gu[:, 1, :, 0:SEQ], G[g][:, :, 0:SEQ], gu[:, 0, :, 0:SEQ], ALU.mult), [tok, ra, rb_] + q_ok[-1:])
            gfree[g] = [a_]
            for n in range(4):
                q_ok.append(dve.do(lambda e: e.tensor_tensor(qhead[HD:QK, 4 * i + n, :], gu[n * ROPE:(n + 1) * ROPE, 1, 0, 0:SEQ],
                                                                            gu[n * ROPE:(n + 1) * ROPE, 1, 1, 0:SEQ], ALU.add), [a_]))

        KW = (META + P, T)
        OFF = (T, 0)
        mask = lambda w: con[:, cat["mla_mask"] + T - w:cat["mla_mask"] + T]
        s2, e2, pt2, pv2, o2_ok, ptc = {}, {}, {}, {}, {}, {}

        def scores2(i):
            bank, b = A[i % 2], i % 2
            for n in (1, 0):
                t = pe.do(lambda e: e.matmul(bank[:, OFF[n]:OFF[n] + KW[n]], qhead[:, i, n * P:(n + 1) * P], khead[:, i, 0:KW[n]],
                                                         start=True, stop=True), q_ok + kv_done["k"] + afree[i % 2], None if n == 0 else False)
            w = [t] + ([e2[i - 2]] if i >= 2 else [])
            for n in (1, 0):
                t = dve.do(lambda e: e.scalar_tensor_tensor(sc2[:, b, OFF[n]:OFF[n] + KW[n]], bank[:, OFF[n]:OFF[n] + KW[n]],
                                                                        1.0 / math.sqrt(QK), mask(KW[n]), ALU.mult, ALU.add), w)
            afree[i % 2] = [t]
            st = stat[:, i % 4, :]
            for n in (1, 0):
                t = dve.do(lambda e: e.tensor_reduce(st[:, n:n + 1], sc2[:, b, OFF[n]:OFF[n] + KW[n]], AX_X, ALU.max, negate=True), [t])
            for n in (1, 0):
                u = act.do(lambda e: e.activation(p2[:, b, OFF[n]:OFF[n] + KW[n]], sc2[:, b, OFF[n]:OFF[n] + KW[n]], ACT.Exp,
                                                              bias=st[:, n:n + 1], accum_out=st[:, 2 + n:3 + n]), [t] + ([pt2[i - 2]] if i >= 2 else []))
            e2[i] = u
            u = dve.do(lambda e: e.reciprocal(st[:, 4:6], st[:, 2:4]), [u])
            for n in (1, 0):
                s2[i] = pool.do(lambda e: e.tensor_scalar(p2[:, b, OFF[n]:OFF[n] + KW[n]], p2[:, b, OFF[n]:OFF[n] + KW[n]],
                                                                     st[:, 4 + n:5 + n], None, ALU.mult), [u])

        def transposes2(i):
            b = i % 2
            waits = [s2[i]] + afree[2] + gfree[1] + gfree[0]
            for j, c0 in enumerate((0, P, T)):
                pe.do(lambda e: e.transpose(A[2][:, j * P:(j + 1) * P], p2[:, b, c0:c0 + P], ident), waits, False)
            for j, c0 in enumerate((2 * P, T + P)):
                t = pe.do(lambda e: e.transpose(G[1][0:META, 0, j * P:(j + 1) * P], p2[:, b, c0:c0 + META], ident),
                          signal=None if j else False)
            pt2[i] = t
            a_ = act.do(lambda e: e.activation(pT2[:, b, :], A[2][:, 0:384], ACT.Copy), [t] + ([pv2[i - 2]] if i >= 2 else []))
            b_ = dve.do(lambda e: e.tensor_copy(pT2m[:, b, :], G[1][0:META, 0, 0:SEQ]), [t] + ([pv2[i - 2]] if i >= 2 else []))
            afree[2], gfree[1] = [a_], [b_]
            ptc[i] = [a_, b_]

        def values2(i):
            b, half = i % 2, i % 2
            vv = lambda kt, m_: v2[0:m_, kt, i * HD:(i + 1) * HD]
            o = A[3][half * HD:(half + 1) * HD, :]
            mm = lambda out, a, c, s0, s1: (lambda e: e.matmul(out, a, c, start=s0, stop=s1))
            pe.do(mm(o[:, P:SEQ], vv(0, P), pT2[:, b, 0:P], True, False), ptc[i] + kv_done["v"] + afree[3], False)
            pe.do(mm(o[:, P:SEQ], vv(1, P), pT2[:, b, P:SEQ], False, False), signal=False)
            pe.do(mm(o[:, P:SEQ], vv(2, META), pT2m[:, b, 0:P], False, True), signal=False)
            pe.do(mm(o[:, 0:P], vv(0, P), pT2[:, b, SEQ:384], True, False), signal=False)
            pv2[i] = pe.do(mm(o[:, 0:P], v2[0:META, 1, i * HD:(i + 1) * HD], pT2m[:, b, P:SEQ], False, True))
            if half:
                o2_ok[i // 2] = split_out(o2h[:, i // 2, :], o2l[:, i // 2, :], A[3][:, 0:SEQ], [pv2[i]])
                afree[3] = o2_ok[i // 2]

        for i in range(MH + 2):
            if i < MH:
                scores2(i)
            if 1 <= i <= MH:
                transposes2(i - 1)
            if i >= 2:
                values2(i - 2)
        afree[0] = afree[0] + afree[1]

        ready6, prep = norm_input(lambda kt: xh[:, kt, COLS1], lambda kt: xl[:, kt, COLS1], "ffn2_norm1", COLS1)
        for i in range(4):
            g, tok = gemm(f"wo{i}", 2, 4, lambda kt: (o2h[:, kt, :], o2l[:, kt, :]), SEQ, lambda kt: o2_ok[kt])
            add_residual(g, tok, i, COLS1, 1.0, [prep])
        swiglu("ffn2", 1, ready6, COLS1, [])

        r = rstd_of(0, rstd, COLS1)
        for kt in range(KT):
            t = dve.do(lambda e: e.scalar_tensor_tensor(X[:, kt, COLS1], X[:, kt, COLS1], V("final_norm", kt), rstd[:, COLS1],
                                                                     ALU.mult, ALU.mult), [r, sq_state["tok"]])
            if kt % 2:
                st_ = sp.do(lambda e: e.dma_start(outT[:, kt - 1:kt + 1, :], X[:, kt - 1:kt + 1, COLS1]), [t], (stored, 16))

        nc.sync.wait_ge(stored.sem, stored.value)


def _features(v):
    return np.ascontiguousarray(np.asarray(v).reshape(-1, P).T)


def kernel(**inputs):
    import concourse.bacc as _bacc
    from concourse.bass_utils import run_bass_kernel_spmd as _run

    a = {k: np.asarray(v) for k, v in inputs.items()}
    chunks, _ = weight_plan()
    wstream = np.zeros((len(chunks), P, CH * P), np.float32)
    for c, blocks in enumerate(chunks):
        for off, (name, layer, rows, cols) in enumerate(blocks):
            w = a[name]
            if name == "pool_w_2":
                w = w[0, layer]
            elif layer is not None:
                w = w[layer]
            wstream[c, :, off * P:(off + 1) * P] = w[np.ix_(rows, cols)]
    vat, vn = vector_plan()
    parts = {
        "c": a["c"], "ada_b": a["ada_b"], "norm1_g": a["norm1_g"], "norm2_g": a["norm2_g"], "final_g": a["final_g"],
        "pool_scale": a["pool_scale_2"], "kv_in_norm": a["kv_in_norm_2"], "final_norm": a["final_norm_2"],
        "kv_latent_norm": a["kv_latent_norm_2"], "q_latent_norm": a["q_latent_norm_2"],
    }
    for n in ("ffn1_norm", "mix_norm", "ffn2_norm"):
        for l in range(2):
            parts[f"{n}{l}"] = a[n + "_2"][l]
    vecs = np.zeros((P, vn), np.float32)
    for n, v in parts.items():
        w = _features(v)
        vecs[:, vat[n]:vat[n] + w.shape[1]] = w
    vecs[:, vat["sinks"]:vat["sinks"] + SWA_HEADS] = np.broadcast_to(a["attn_sinks"].reshape(1, -1), (P, SWA_HEADS))
    bias_oh, sel = bias_constants()
    feature_major = lambda v: np.ascontiguousarray(v.T.reshape(KT, P, -1).transpose(1, 0, 2))
    arrays = {
        "in_xT": feature_major(a["x"][0]), "in_metaT": feature_major(a["meta_tokens_2"]), "in_vecs": vecs,
        "in_consts": constants(), "in_bias_oh": bias_oh,
        "in_bias_rows": np.concatenate([a["rel_bias"], sel]), "in_wstream": wstream,
    }
    nc = _bacc.Bacc("TRN2", target_bir_lowering=False, num_devices=1)
    aps = [nc.dram_tensor(n, v.shape, F32, kind="ExternalInput").ap() for n, v in arrays.items()]
    scratch = nc.dram_tensor("bias_scratch", (HEADS1, 512), F32).ap()
    out = nc.dram_tensor("out_T", (P, KT, SEQ), F32, kind="ExternalOutput").ap()
    build_program(nc, *aps, scratch, out)
    r = _run(nc, [arrays], core_ids=[0])
    got = r.results[0]["out_T"]
    return np.ascontiguousarray(got.transpose(1, 0, 2).reshape(D, SEQ).T.reshape(1, SEQ, D))
```

```python
from contextlib import ExitStack
import math

import numpy as np

import concourse.bass as bass
from concourse import mybir

F32 = mybir.dt.float32
F32R = mybir.dt.float32r
ALU = mybir.AluOpType
ACT = mybir.ActivationFunctionType
AX_X = mybir.AxisListType.X

P = 128
D = 1024
KT = D // P
META = 16
SEQ = 256
T = META + SEQ
HD = 64
SWA_HEADS, SWA_KV, MOBA_HEADS = 8, 2, 8
HEADS1 = SWA_HEADS + MOBA_HEADS
WINDOW = 128
NB = 32
MAX_DISTANCE = 2048
FF1 = 4 * D // P
FF2 = 2816 // P
KVR = 256 // P
QR = 384 // P
MH, ROPE = 8, 32
QK = HD + ROPE
POOL_W = (2, 4, 8, 16)
POOL_ORDER = (0, 1, 3, 2)
POOL_KT = [2 * g + n for g in POOL_ORDER for n in range(2)]
PADC = 16
EPS = 1e-6
MASKED = -3.0e38
BIASC = 384

CH = 8
NRAW, NSPLIT = 8, 5
AHEAD = 3
LOADING = 3

W_IN_OFF = dict(qa=0, ka=512, va=640, qb=768, kb=1280, vb=1792, ga=2304, gb=3328)


_PIECES = [(i, part) for i in (4, 5, 8, 9, 6, 7, 10, 11) for part in range(4)]
ADA_QK, ADA_HEADS, ADA_BRANCH, ADA_MLP = _PIECES[:4], _PIECES[4:20], _PIECES[20:24], _PIECES[24:]


def _r(a, n=P):
    return np.arange(a, a + n)


def weight_plan():
    groups = []

    def group(name, blocks, flush=False):
        groups.append((name, blocks, flush))

    def dense(name, arr, layer, tiles, nk, rows=None):
        rows = rows or (lambda kt: _r(kt * P))
        group(name, [(arr, layer, rows(kt), c) for kt in range(nk) for c in tiles])

    def ada(i, part):
        group(f"ada{i}_{part}", [("ada_w", 0, _r(kt * P), _r((4 * i + t) * P)) for kt in (2 * part, 2 * part + 1) for t in range(4)], True)

    for i in range(4):
        for part in range(4):
            ada(i, part)
    o = W_IN_OFF
    tiles = [_r(o["ka"])]
    tiles += [np.concatenate([_r(o["qa"] + j * HD, HD), _r(o["qa"] + (j + 4) * HD, HD)]) for j in range(4)]
    tiles += [_r(o["kb"] + j * P) for j in range(4)] + [_r(o["qb"] + j * P) for j in range(4)]
    for i in range(0, 13, 2):
        if i % 4 == 0:
            ada(*ADA_QK[i // 4])
        dense(f"qk{i // 2}", "w_in", 0, tiles[i:i + 2], KT)
    group("va", [("w_in", 0, _r(kt * P), _r(o["va"])) for kt in range(KT)], True)
    group("vb", [("w_in", 0, _r(kt * P), _r(o["vb"] + j * P)) for kt in range(KT) for j in range(4)], True)
    for i in range(HEADS1):
        ada(*ADA_HEADS[i])
        t = i - i % 2
        group(f"gate{i}", [("w_in", 0, _r(kt * P), _r(o["ga"] + (t + n) * P)) for kt in _r(i % 2 * 4, 4) for n in range(2)])
    rows_a = lambda kt: np.concatenate([_r(kt * HD, HD), _r((kt + 4) * HD, HD)])
    for i in range(4):
        if i >= 2:
            ada(*ADA_BRANCH[i - 2])
        dense(f"bra{i}", "w_branch_a", 0, [_r((2 * i + n) * P) for n in range(2)], 4, rows_a)
    for i in range(4):
        if i == 0:
            ada(*ADA_BRANCH[2])
        dense(f"brb{i}", "w_branch_b", 0, [_r((2 * i + n) * P) for n in range(2)], 4)
    for i in range(4):
        if i == 0:
            ada(*ADA_BRANCH[3])
        dense(f"wout{i}", "w_out", 0, [_r((2 * i + n) * P) for n in range(2)], KT)
    for i in range(FF1 // 2):
        if i % 2 == 0:
            ada(*ADA_MLP[i // 2])
        dense(f"mlp_in{i}", "w_mlp_in", 0, [_r((2 * i + n) * P) for n in range(2)], KT)
    for i in range(4):
        dense(f"mlp_out{i}", "w_mlp_out", 0, [_r((2 * i + n) * P) for n in range(2)], FF1)

    def gate_up(f, layer, j):
        blocks = []
        for kt in range(KT):
            blocks += [(f"{f}_w_gate_2", layer, _r(kt * P), _r(j * P)), (f"{f}_w_up_2", layer, _r(kt * P), _r(j * P))]
        group(f"{f}_{layer}_gu{j}", blocks)

    def gate_up_01(f, layer, order=range(KT)):
        group(f"{f}_{layer}_gu01", [(f"{f}_w_{m}_2", layer, _r(kt * P), _r(j * P)) for kt in order for j in (0, 1) for m in ("gate", "up")])

    def down(f, layer):
        for i in range(4):
            dense(f"{f}_{layer}_down{i}", f"{f}_w_down_2", layer, [_r((2 * i + n) * P) for n in range(2)], FF2)

    gate_up_01("ffn1", 0)
    for j in range(2, FF2):
        gate_up("ffn1", 0, j)
    down("ffn1", 0)
    for g in range(4):
        group(f"pool{g}", [("pool_w_2", g, _r(kt * P), _r(n * P)) for kt in range(2) for n in range(2)])
    gate_up_01("ffn2", 0, POOL_KT)
    for j in range(2, FF2):
        gate_up("ffn2", 0, j)
    down("ffn2", 0)
    dense("ckv", "w_dkv_2", None, [_r(0), _r(P)], KT)
    rope = _r(KVR * P, ROPE)
    swap = np.concatenate([rope[ROPE // 2:], rope[:ROPE // 2]])
    dense("krope", "w_dkv_2", None, [np.concatenate([rope, swap, rope, swap])], KT)
    gate_up_01("ffn1", 1)
    for j in range(2, FF2):
        gate_up("ffn1", 1, j)
        if j == 3:
            for i in range(2):
                dense(f"uk{i}", "w_uk_2", None, [_r((2 * i + n) * P) for n in range(2)], KVR)
            group("uv", [("w_uv_2", None, _r(kt * P), _r(j4 * P)) for kt in range(KVR) for j4 in range(4)], True)
    down("ffn1", 1)
    dense("dq0", "w_dq_2", 0, [_r(0), _r(P)], KT)
    dense("dq1", "w_dq_2", 0, [_r(2 * P)], KT)
    head = lambda h: h * QK
    nope = [np.concatenate([_r(head(2 * j + n), HD) for n in range(2)]) for j in range(4)]
    for i in range(2):
        dense(f"uqn{i}", "w_uq_2", 0, nope[2 * i:2 * i + 2], QR)
        rp = [_r(head(4 * i + n) + HD, ROPE) for n in range(4)]
        sw = [np.concatenate([r[ROPE // 2:], r[:ROPE // 2]]) for r in rp]
        dense(f"uqr{i}", "w_uq_2", 0, [np.concatenate(rp), np.concatenate(sw)], QR)
    for i in range(4):
        dense(f"wo{i}", "w_o_2", 0, [_r((2 * i + n) * P) for n in range(2)], 4)
    gate_up_01("ffn2", 1)
    for j in range(2, FF2):
        gate_up("ffn2", 1, j)
    down("ffn2", 1)

    chunks, where, was_ada = [[]], {}, False
    for name, blocks, flush in groups:
        if (flush or was_ada) and chunks[-1]:
            chunks.append([])
        where[name], was_ada = [], name.startswith("ada")
        for b in blocks:
            if len(chunks[-1]) == CH:
                chunks.append([])
            where[name].append((len(chunks) - 1, len(chunks[-1])))
            chunks[-1].append(b)
    return chunks, where


def vector_plan():
    at, n = {}, 0
    for name, w in (("c", KT), ("ada_b", 6 * KT), ("norm1_g", KT), ("norm2_g", KT), ("final_g", KT),
                    ("ffn1_norm0", KT), ("ffn1_norm1", KT), ("mix_norm0", KT), ("mix_norm1", KT),
                    ("ffn2_norm0", KT), ("ffn2_norm1", KT), ("pool_scale", KT), ("kv_in_norm", KT),
                    ("final_norm", KT), ("kv_latent_norm", KVR), ("q_latent_norm", QR), ("sinks", SWA_HEADS)):
        at[name] = n
        n += w
    return at, n


def constant_plan():
    at, n = {}, 0
    for name, w in (("ident", P), ("cos", T), ("sin", T), ("mla_mask", T), ("count_fix", 4 * PADC)):
        at[name] = n
        n += w
    return at, n


def constants():
    at, n = constant_plan()
    out = np.zeros((P, n), np.float32)
    out[:, at["ident"]:at["ident"] + P] = np.eye(P, dtype=np.float32)
    inv = (1.0 / (np.float32(10000.0) ** (np.arange(0, ROPE, 2, dtype=np.float32) / ROPE))).astype(np.float32)
    ang = np.arange(T, dtype=np.float32)[None, :] * inv[:, None]
    cos, sin = np.cos(ang).astype(np.float32), np.sin(ang).astype(np.float32)
    for g in range(P // ROPE):
        r = g * ROPE
        out[r:r + ROPE, at["cos"]:at["cos"] + T] = np.concatenate([cos, cos])
        out[r:r + ROPE, at["sin"]:at["sin"] + T] = np.concatenate([-sin, sin])
    out[0:64, at["mla_mask"] + T - 64:at["mla_mask"] + T] = MASKED
    for g, w in enumerate(POOL_W):
        t = np.arange(PADC)
        out[:, at["count_fix"] + g * PADC:at["count_fix"] + (g + 1) * PADC] = w / np.minimum(t + 1, w)
    return out


def bias_constants():
    dist = 255 - np.arange(BIASC)
    n = np.maximum(dist, 0)
    half = NB // 2
    large = half + (np.log(np.maximum(n, 1).astype(np.float32) / half) / math.log(MAX_DISTANCE / half)
                    * (NB - half)).astype(np.int32)
    bucket = np.where(n < half, n, np.minimum(large, NB - 1))
    out = np.zeros((NB + 2, BIASC), np.float32)
    out[bucket, np.arange(BIASC)] = 1.0
    out[NB, (dist < 0) | (dist >= WINDOW)] = MASKED
    out[NB + 1, dist < 0] = MASKED
    sel = np.zeros((2, HEADS1), np.float32)
    sel[0, :SWA_HEADS] = 1.0
    sel[1, SWA_HEADS:] = 1.0
    return out, sel


class Counter:

    def __init__(self, sem):
        self.sem, self.value = sem, 0

    def add(self, n=1):
        self.value += n
        return (self, self.value)


class Queue:

    def __init__(self, engine, counter=None):
        self.engine, self.counter, self.passed = engine, counter, {}

    def do(self, make, after=(), signal=None):
        for token in after:
            if token is None:
                continue
            counter, value = token
            if self.passed.get(counter, 0) < value:
                self.passed[counter] = value
                self.engine.wait_ge(counter.sem, value)
        made = make(self.engine)
        if signal is False:
            return None
        counter, n = (self.counter, 1) if signal is None else signal
        made.then_inc(counter.sem, n)
        return counter.add(n)


def build_program(nc, xT, metaT, vecs, consts, bias_oh, bias_rows, wstream, scratch, outT):
    chunks, where = weight_plan()
    last_use = {}
    for name, places in where.items():
        for c, off in places:
            last_use[c] = max(last_use.get(c, 0), off)
    vat, vn = vector_plan()
    cat, cn = constant_plan()

    ctx = ExitStack()
    with ctx:
        def sb(name, shape, dt=F32, to=ctx):
            return to.enter_context(nc.sbuf_tensor("sb_" + name, shape, dt))

        def counter(name):
            return Counter(ctx.enter_context(nc.semaphore(name)))

        X = sb("X", [P, KT, T])
        xh, xl = sb("xh", [P, KT, T], F32R), sb("xl", [P, KT, T], F32R)
        raw = sb("raw", [P, NRAW, CH * P])
        whi, wlo = sb("whi", [P, NSPLIT, CH * P], F32R), sb("wlo", [P, NSPLIT, CH * P], F32R)
        vec = sb("vec", [P, vn])
        con = sb("con", [P, cn])
        mean_ones = sb("mean_ones", [P, 3, P])
        sumsq, sumsq2, sq = sb("sumsq", [P, T]), sb("sumsq2", [P, T]), sb("sq", [P, 2, T])
        root, rstd, rstd2 = sb("root", [P, T]), sb("rstd", [P, T]), sb("rstd2", [P, T])
        mod, csil, g1m = sb("mod", [P, 6 * KT]), sb("csil", [P, KT]), sb("g1m", [P, 2 * KT])
        gu, hidf, tmp = sb("gu", [P, 2, 2, T]), sb("hidf", [P, 2, 2 * SEQ]), sb("tmp", [P, 2, T])
        shift_out = sb("shift_out", [P, 2, 2])
        warm = sb("warm", [P, 2])
        scale_w = sb("scale_w", [P, KT])
        eps_c, one_col = sb("eps_c", [P, 2]), sb("one_col", [P, 2])
        stat = sb("stat", [P, 4, 8])
        with ExitStack() as s:
            qk = sb("qk", [P, 13, SEQ], to=s)
            vtok = sb("vtok", [P, 2, 640], to=s)
            sig = sb("sig", [P, 16, SEQ], to=s)
            bias = sb("bias", [P, HEADS1, SEQ], to=s)
            sc1, p1, pT1 = (sb(n, [P, 2, 384], to=s) for n in ("sc1", "p1", "pT1"))
        with ExitStack() as s:
            U, SA, SB_ = (sb(n, [P, KT, PADC + T], to=s) for n in ("U", "SA", "SB"))
        with ExitStack() as s:
            qhead = sb("qhead", [QK, MH, SEQ], to=s)
            sc2, p2 = (sb(n, [P, 3, 416], to=s) for n in ("sc2", "p2"))
            pT2, pT2m = sb("pT2", [P, 2, 384], to=s), sb("pT2m", [META, 2, 256], to=s)
            cqf = sb("cqf", [P, QR, SEQ], to=s)
            cqh, cql = sb("cqh", [P, QR, SEQ], F32R, to=s), sb("cql", [P, QR, SEQ], F32R, to=s)
            o2h, o2l = sb("o2h", [P, 4, SEQ], F32R, to=s), sb("o2l", [P, 4, SEQ], F32R, to=s)
        hh, hl = sb("hh", [P, FF1 * SEQ], F32R), sb("hl", [P, FF1 * SEQ], F32R)
        with ExitStack() as s:
            boh, brow, brows = sb("boh", [NB + 2, BIASC], to=s), sb("brow", [NB + 2, HEADS1], to=s), sb("brows", [HEADS1, BIASC], to=s)
        with ExitStack() as s:
            khead = sb("khead", [QK, MH, T], to=s)
            v2 = sb("v2", [P, 3, MH * HD], to=s)
            krot = sb("krot", [ROPE, T], to=s)
        oh, ol = sb("oh", [P, 8, SEQ], F32R), sb("ol", [P, 8, SEQ], F32R)
        ckvf = sb("ckvf", [P, KVR, T])
        kvx = FF2 * T
        G = [ctx.enter_context(nc.psum_tensor(f"G{i}", [P, 2, 512], F32)) for i in range(2)]
        A = [ctx.enter_context(nc.psum_tensor(f"A{i}", [P, 512], F32)) for i in range(4)]

        pe_done, act_done, dve_done = counter("pe_done"), counter("act_done"), counter("dve_done")
        pool_done, hi_done, lo_done = counter("pool_done"), counter("hi_done"), counter("lo_done")
        loaded = [counter(f"loaded{i}") for i in range(NRAW)]
        small_in, x_in, con_in, meta_in = counter("small_in"), counter("x_in"), counter("con_in"), counter("meta_in")
        rows_in, rows_out, bias_in, stored = counter("rows_in"), counter("rows_out"), counter("bias_in"), counter("stored")
        pe, act, dve = Queue(nc.tensor, pe_done), Queue(nc.scalar, act_done), Queue(nc.vector, dve_done)
        pool, sp = Queue(nc.gpsimd, pool_done), Queue(nc.sync)

        def V(name, k=0, n=1):
            return vec[:, vat[name] + k:vat[name] + k + n]

        ident = con[:, cat["ident"]:cat["ident"] + P]
        f = lambda ap: ap.bitcast(F32)
        COLS1 = slice(META, T)

        vec_ok = sp.do(lambda e: e.dma_start(vec[:, :], vecs), signal=(small_in, 16))
        x_ok = sp.do(lambda e: e.dma_start(X[:, :, META:T], xT), signal=(x_in, 16))

        load_of, hi_of, lo_of, free_of = {}, {}, {}, {}
        plain = {c for n in where if n.startswith("ada") for c, _ in where[n]}

        def load_chunk(c):
            if c >= len(chunks) or c in load_of:
                return
            slot, w = c % NRAW, len(chunks[c]) * P
            before = [] if c < NRAW else [free_of[c - NRAW] if c - NRAW in plain else lo_of[c - NRAW]]
            load_of[c] = sp.do(lambda e: e.dma_start(raw[:, slot, 0:w], wstream[c, :, 0:w]), before, (loaded[slot], 16))

        split_at, split_order = {}, [c for c in range(len(chunks)) if c not in plain]
        for i, c in enumerate(split_order):
            split_at[c] = i

        def load_upto(c):
            for k in range(c + 1):
                if k not in load_of:
                    ok = k < NRAW or ((free_of if k - NRAW in plain else lo_of).get(k - NRAW) is not None)
                    if not ok:
                        return
                    load_chunk(k)

        def split_hi(c):
            if c in hi_of:
                return
            i, w, slot = split_at[c], len(chunks[c]) * P, c % NRAW
            before = free_of[split_order[i - NSPLIT]] if i >= NSPLIT else None
            hi_of[c] = act.do(lambda e: e.activation(whi[:, i % NSPLIT, 0:w], raw[:, slot, 0:w], ACT.Copy), [load_of[c], before], (hi_done, 1))

        def split_lo(c):
            if c in lo_of:
                return
            split_hi(c)
            s, w, slot = split_at[c] % NSPLIT, len(chunks[c]) * P, c % NRAW
            lo_of[c] = dve.do(lambda e: e.tensor_tensor(wlo[:, s, 0:w], raw[:, slot, 0:w], f(whi[:, s, 0:w]), ALU.subtract),
                              [hi_of[c]], (lo_done, 1))
            load_upto(c + NRAW)

        def need(c):
            ahead = []
            for k in range(c, min(c + NRAW - LOADING, len(chunks))):
                load_upto(k)
                if k in plain:
                    continue
                i = split_at[k]
                if len(ahead) > AHEAD + 1 or k not in load_of or (i >= NSPLIT and split_order[i - NSPLIT] not in free_of):
                    break
                ahead.append(k)
            if c not in plain:
                split_lo(c)
            for k in ahead:
                split_hi(k)
            for k in ahead[:-1]:
                split_lo(k)

        def used(c, off, token_wanted):
            return token_wanted or off == last_use[c]

        def mark(c, off, token):
            if off == last_use[c]:
                free_of[c] = token
                load_upto(c + NRAW)

        def weights(c, off, n=1):
            s = split_at[c] % NSPLIT
            return whi[:, s, off * P:(off + n) * P], wlo[:, s, off * P:(off + n) * P]

        gnext, gfree, afree = [0], [[], []], [[], [], [], []]

        def next_pair():
            g = gnext[0] % 2
            gnext[0] += 1
            before, gfree[g] = list(gfree[g]), []
            return g, before

        def gemm(name, ntiles, nk, src, n, ready=None, pair=None, k0=0, ktotal=None, mid=None, order=None, each=None, banks=None):
            if banks:
                g, before = None, afree[banks[0]] + afree[banks[1]]
                outs = [A[b][:, 0:n] for b in banks]
            elif ntiles > 2:
                g, before = next_pair()
                before = before + afree[1] + afree[2]
                outs = [A[1][:, 0:n], A[2][:, 0:n], G[g][:, 0, 0:n], G[g][:, 1, 0:n]]
            else:
                g, before = next_pair() if pair is None else (pair, [])
                outs = [G[g][:, t, 0:n] for t in range(ntiles)]
            ktotal = ktotal or nk
            places, i, token = where[name], 0, None
            for step, kt in enumerate(order or range(k0, k0 + nk), k0):
                for t in range(ntiles):
                    c, off = places[i]
                    if mid and i == (nk * ntiles) // 2:
                        mid()
                    i += 1
                    need(c)
                    xs, xr = src(kt)
                    w_h, w_l = weights(c, off)
                    waits = before + [hi_of[c], lo_of[c]] + (ready(kt) if ready else [])
                    out = outs[t]
                    first = lambda e: e.matmul(out, w_h, xs, start=step == 0, stop=False)
                    pe.do(first, waits, signal=False)
                    pe.do(lambda e: e.matmul(out, w_h, xr, start=False, stop=False), signal=False)
                    end = i == nk * ntiles
                    last = lambda e: e.matmul(out, w_l, xs, start=False, stop=step == ktotal - 1)
                    tok = pe.do(last, signal=None if used(c, off, end) else False)
                    mark(c, off, tok)
                    if end:
                        token = tok
                if each:
                    each(step)
            return g, token

        def token_major(name, width, nk, src, rows, tile0, ready=None):
            g, before = next_pair()
            places, nb, token = where[name], width // P, None
            for kt in range(nk):
                c, off = places[kt * nb]
                need(c)
                w_h, w_l = weights(c, off, nb)
                for i, (a, m) in enumerate(rows):
                    xs, xr = src(kt, a, m)
                    out = G[g][0:m, i, 0:width]
                    waits = before + [hi_of[c], lo_of[c]] + (ready(kt) if ready else [])
                    for j, (s_, m_) in enumerate(((xs, w_h), (xr, w_h), (xs, w_l))):
                        end = i == len(rows) - 1 and j == 2
                        fn = lambda e: e.matmul(out, s_, m_, start=kt == 0 and j == 0, stop=kt == nk - 1 and j == 2)
                        tok = pe.do(fn, waits, None if end else False)
                    if i == len(rows) - 1:
                        if tile0:
                            mark(c, off + nb - 1, tok)
                        token = tok
            return g, token

        def split_out(hi, lo, src, after, scale=None, bias_=None):
            kw = {}
            if scale is not None:
                kw["scale"] = scale
            if bias_ is not None:
                kw["bias"] = bias_
            fn = ACT.Copy if bias_ is None and scale is None else ACT.Identity
            th = act.do(lambda e: e.activation(hi, src, fn, **kw), after)
            if scale is not None:
                tl = dve.do(lambda e: e.scalar_tensor_tensor(lo, src, scale, f(hi), ALU.mult, ALU.subtract), [th] + after)
            elif bias_ is not None:
                tl = dve.do(lambda e: e.scalar_tensor_tensor(lo, src, bias_, f(hi), ALU.add, ALU.subtract), [th] + after)
            else:
                tl = dve.do(lambda e: e.tensor_tensor(lo, src, f(hi), ALU.subtract), [th] + after)
            return [th, tl]

        sq_state = dict(n=0, tok=None, used=None)

        def square_in(src, first, cols, after):
            dst = sumsq[:, cols]
            if first:
                sq_state["tok"] = pool.do(lambda e: e.tensor_tensor(dst, src, src, ALU.mult), after + [sq_state["used"]])
            else:
                s = sq[:, sq_state["n"] % 2, cols]
                sq_state["n"] += 1
                a = pool.do(lambda e: e.tensor_tensor(s, src, src, ALU.mult), after)
                sq_state["tok"] = pool.do(lambda e: e.tensor_tensor(dst, dst, s, ALU.add), [a, sq_state["tok"]])

        def rstd_of(which, dst, cols):
            n = cols.stop - cols.start
            t = pe.do(lambda e: e.matmul(A[0][:, 0:n], mean_ones[:, which, :], sumsq[:, cols], start=True, stop=True),
                      [sq_state["tok"]] + afree[0])
            sq_state["used"] = t
            r = act.do(lambda e: e.activation(root[:, cols], A[0][:, 0:n], ACT.Sqrt, bias=eps_c[:, 0:1]), [t])
            afree[0] = [r]
            return dve.do(lambda e: e.reciprocal(dst[:, cols], root[:, cols]), [r])

        def preload(function):
            act.do(lambda e: e.activation(warm[:, 0:1], eps_c[:, 0:1], function), [ones_t])

        def norm_input(hi, lo, gain, cols):
            ready = {}

            def tile(kt, tok):
                ready[kt] = split_out(hi(kt), lo(kt), X[:, kt, cols], [tok], scale=V(gain, kt))
            return ready, tile

        dve.do(lambda e: e.memset(eps_c[:, :], EPS))
        dve.do(lambda e: e.memset(one_col[:, :], 1.0))
        for i, n in enumerate((D, KVR * P, QR * P)):
            ones_t = dve.do(lambda e: e.memset(mean_ones[:, i, :], 1.0 / n))
        load_upto(NRAW - 1)
        for kt in range(KT):
            square_in(X[:, kt, COLS1], kt == 0, COLS1, [x_ok])
        cs = act.do(lambda e: e.activation(csil[:, :], V("c", 0, KT), ACT.Silu), [vec_ok])
        afree[0] = [ones_t]
        ada_free, ada_sum, ada_total = {}, [None, None], {}

        ada_sets = [(gu[:, 0, :, :].rearrange("p a b -> p (a b)")[:, 0:4 * P], gu[:, 1, :, :].rearrange("p a b -> p (a b)")[:, 0:4 * P]),
                    (hidf[:, 0, :], hidf[:, 1, :])]

        ada_sets += [(sig[:, 4 * n:4 * n + 2, :].rearrange("p a b -> p (a b)"), sig[:, 4 * n + 2:4 * n + 4, :].rearrange("p a b -> p (a b)"))
                     for n in range(4)] + [(sc1[:, :, :].rearrange("p a b -> p (a b)")[:, 0:4 * P], p1[:, :, :].rearrange("p a b -> p (a b)")[:, 0:4 * P])]

        def ada_set(i):
            if i < 4:
                return 2 + i
            if i == 7:
                return 6
            return 0 if i >= 10 else i % 2

        def ada_piece(i, part):
            c, off = where[f"ada{i}_{part}"][0]
            load_upto(c)
            for odd in range(2):
                kt = 2 * part + odd
                acc, w = ada_sets[ada_set(i)][odd], raw[:, c % NRAW, odd * 4 * P:(odd + 1) * 4 * P]
                if part == 0:
                    t = dve.do(lambda e: e.tensor_scalar(acc, w, csil[:, kt:kt + 1], None, ALU.mult), [load_of[c], cs, ada_free.get(ada_set(i))])
                else:
                    t = dve.do(lambda e: e.scalar_tensor_tensor(acc, w, csil[:, kt:kt + 1], acc, ALU.mult, ALU.add),
                               [load_of[c], ada_sum[odd]])
                ada_sum[odd] = t
            mark(c, CH - 1, t)
            if part == 3:
                even, odd = ada_sets[ada_set(i)]
                ada_total[ada_set(i)] = dve.do(lambda e: e.tensor_tensor(even, even, odd, ALU.add), ada_sum)

        def ada_finish(i, n=1):
            g, before = next_pair()
            for t in range(4 * n):
                s_ = ada_set(i + t // 4)
                acc = ada_sets[s_][0][:, t % 4 * P:(t % 4 + 1) * P]
                tok = pe.do(lambda e: e.matmul(G[g][:, 0, t:t + 1], acc, one_col[:, 0:1], start=True, stop=True),
                            before + [ada_total[s_], ones_t], None if t % 4 == 3 else False)
                ada_free[s_] = tok
            m = dve.do(lambda e: e.tensor_tensor(mod[:, 4 * i:4 * (i + n)], G[g][:, 0, 0:4 * n], V("ada_b", 4 * i, 4 * n), ALU.add), [tok, vec_ok])
            gfree[g] = [m]
            return m

        for i in range(4):
            for part in range(4):
                ada_piece(i, part)
            if i == 1:
                r1 = rstd_of(0, rstd, COLS1)
        sp.do(lambda e: e.dma_start(boh[:, :], bias_oh), signal=(rows_in, 16))
        rin = sp.do(lambda e: e.dma_start(brow[:, :], bias_rows), signal=(rows_in, 16))
        con_ok = sp.do(lambda e: e.dma_start(con[:, :], consts), signal=(con_in, 16))
        m = ada_finish(0, 4)

        def mod_gain(dst, gname, k, after):
            a = dve.do(lambda e: e.tensor_scalar(dst, mod[:, k:k + KT], 1.0, None, ALU.add), after)
            return dve.do(lambda e: e.tensor_tensor(dst, dst, V(gname, 0, KT), ALU.mult), [a, vec_ok])

        def modulated(goff, shift, ready_t, rs):
            ready, scaled = {}, {}
            for kt in range(KT + 1):
                if kt in (2, 5):
                    split_lo(where["qk0"][0][0] + kt // 5)
                if kt < KT:
                    b = kt % 2
                    scaled[kt] = dve.do(lambda e: e.scalar_tensor_tensor(tmp[:, b, 0:SEQ], X[:, kt, COLS1], g1m[:, goff + kt:goff + kt + 1],
                                                                         rstd[:, COLS1], ALU.mult, ALU.mult),
                                        ready_t + [rs] + (ready[kt - 2] if kt >= 2 else []))
                if kt:
                    ready[kt - 1] = split_out(xh[:, kt - 1, COLS1], xl[:, kt - 1, COLS1], tmp[:, (kt - 1) % 2, 0:SEQ], [scaled[kt - 1]],
                                              bias_=mod[:, shift + kt - 1:shift + kt])
            return ready

        preload(ACT.Exp)
        gm = mod_gain(g1m[:, 0:KT], "norm1_g", KT, [m])
        ready = modulated(0, 0, [gm], r1)
        src1 = lambda kt: (xh[:, kt, COLS1], xl[:, kt, COLS1])

        qk_ok = {}
        REV = lambda ap: ap[:, :, ::-1]
        for i in range(7):
            nt = 2 if i < 6 else 1
            if i % 2 == 0:
                ada_piece(*ADA_QK[i // 2])
            g, tok = gemm(f"qk{i}", nt, KT, src1, SEQ, lambda kt: ready[kt])
            fr = []
            for t in range(nt):
                ti = 2 * i + t
                isq = 1 <= ti <= 4 or ti >= 9
                dst = qk[:, ti, :].rearrange("p (b q) -> p b q", b=2)
                ps = G[g][:, t, 0:SEQ].rearrange("p (b q) -> p b q", b=2)
                ps = REV(ps) if isq else ps
                if t == 0:
                    qk_ok[ti] = act.do(lambda e: e.activation(dst, ps, ACT.Copy), [tok])
                else:
                    qk_ok[ti] = dve.do(lambda e: e.tensor_copy(dst, ps), [tok])
                fr.append(qk_ok[ti])
            gfree[g] = fr
            if i == 0:
                bt = pe.do(lambda e: e.matmul(A[1][0:HEADS1, 0:BIASC], brow[:, :], boh[:, :], start=True, stop=True), [rin])
                bt = act.do(lambda e: e.activation(brows[:, :], A[1][0:HEADS1, 0:BIASC], ACT.Copy), [bt])
                afree[1] = [bt]
                ro = pool.do(lambda e: e.dma_start(scratch[:, 0:BIASC], brows[:, :]), [bt], (rows_out, 16))
            if i == 2:
                hankel = bass.AP(scratch.tensor, 0, [[1, P], [512, HEADS1], [1, SEQ]])
                bias_ok = pool.do(lambda e: e.dma_start(bias[:, :, :], hankel), [ro, qk_ok[2]], (bias_in, 16))
        vsrc = lambda kt, a, m: (xh[:, kt, META + a:META + a + m], xl[:, kt, META + a:META + a + m])
        v_ok = []
        for name, w, c0 in (("va", P, 0), ("vb", 4 * P, P)):
            g, tok = token_major(name, w, KT, vsrc, [(0, P), (P, P)], True)
            a_ = act.do(lambda e: e.activation(vtok[:, 0, c0:c0 + w], G[g][:, 0, 0:w], ACT.Copy), [tok])
            b_ = dve.do(lambda e: e.tensor_copy(vtok[:, 1, c0:c0 + w], G[g][:, 1, 0:w]), [tok])
            gfree[g] = [a_, b_]
            v_ok += [a_, b_]
        ada_finish(4)

        heads = [dict(q=1 + h % 4, k=0, row=(h // 4) * HD, v=(h // 4) * HD, bias=h, out=h % 4, sink=h) for h in (0, 4, 1, 5, 2, 6, 3, 7)]
        heads += [dict(q=9 + h // 2, k=5 + h // 2, row=(h % 2) * HD, v=P + h * HD, bias=8 + h, out=4 + h // 2, sink=None) for h in range(8)]
        s_tok, e_tok, pt_tok, pv_tok, o_ok, pT_free = {}, {}, {}, {}, {}, {}

        def scores1(i):
            h = heads[i]
            r, bank, b = h["row"], A[i % 2], i % 2
            q = lambda n: qk[r:r + HD, h["q"], n * P:(n + 1) * P]
            k = lambda w: qk[r:r + HD, h["k"], 0:w]
            pe.do(lambda e: e.matmul(bank[:, 0:SEQ], q(1), k(SEQ), start=True, stop=True), [qk_ok[h["q"]], qk_ok[h["k"]]] + afree[i % 2], False)
            t = pe.do(lambda e: e.matmul(bank[:, SEQ:SEQ + P], q(0), k(P), start=True, stop=True))
            w = [t, bias_ok] + ([e_tok[i - 2]] if i >= 2 else [])
            dve.do(lambda e: e.scalar_tensor_tensor(sc1[:, b, 0:SEQ], bank[:, 0:SEQ], HD ** -0.5, bias[:, h["bias"], :], ALU.mult, ALU.add), w, False)
            t = dve.do(lambda e: e.scalar_tensor_tensor(sc1[:, b, SEQ:SEQ + P], bank[:, SEQ:SEQ + P], HD ** -0.5, bias[:, h["bias"], P:SEQ],
                                                        ALU.mult, ALU.add))
            afree[i % 2] = [t]
            st = stat[:, i % 4, :]
            mx = st[:, 6:8]
            neg = h["sink"] is None
            md = st[:, 0:2] if neg else mx
            dve.do(lambda e: e.tensor_reduce(md[:, 0:1], sc1[:, b, 0:SEQ], AX_X, ALU.max, negate=neg), [t], False)
            t = dve.do(lambda e: e.tensor_reduce(md[:, 1:2], sc1[:, b, SEQ:SEQ + P], AX_X, ALU.max, negate=neg))
            if not neg:
                sink = V("sinks", h["sink"])
                t = dve.do(lambda e: e.tensor_scalar(st[:, 0:2], mx, sink, -1.0, ALU.max, ALU.mult), [t])
            act.do(lambda e: e.activation(p1[:, b, 0:SEQ], sc1[:, b, 0:SEQ], ACT.Exp, bias=st[:, 0:1], accum_out=st[:, 2:3]),
                   [t] + ([pt_tok[i - 2]] if i >= 2 else []))
            u = act.do(lambda e: e.activation(p1[:, b, SEQ:384], sc1[:, b, SEQ:384], ACT.Exp, bias=st[:, 1:2], accum_out=st[:, 3:4]))
            e_tok[i] = u

        def weights1(i):
            h, b, st, u = heads[i], i % 2, stat[:, i % 4, :], e_tok[i]
            if h["sink"] is not None:
                sink = V("sinks", h["sink"])
                sk = act.do(lambda e: e.activation(st[:, 4:6], st[:, 0:2], ACT.Exp, bias=sink))
                u2 = dve.do(lambda e: e.tensor_tensor(st[:, 4:6], st[:, 4:6], st[:, 2:4], ALU.add), [sk, u])
                u2 = dve.do(lambda e: e.reciprocal(st[:, 4:6], st[:, 4:6]), [u2])
            else:
                u2 = dve.do(lambda e: e.reciprocal(st[:, 4:6], st[:, 2:4]), [u])
            pool.do(lambda e: e.tensor_scalar(p1[:, b, 0:SEQ], p1[:, b, 0:SEQ], st[:, 4:5], None, ALU.mult), [u2], False)
            s_tok[i] = pool.do(lambda e: e.tensor_scalar(p1[:, b, SEQ:384], p1[:, b, SEQ:384], st[:, 5:6], None, ALU.mult))

        def transposes1(i):
            b = i % 2
            for j in range(3):
                t = pe.do(lambda e: e.transpose(A[2][:, j * P:(j + 1) * P], p1[:, b, j * P:(j + 1) * P], ident),
                          [s_tok[i], con_ok] + afree[2], None if j == 2 else False)
            pt_tok[i] = t
            c = act.do(lambda e: e.activation(pT1[:, b, :], A[2][:, 0:384], ACT.Copy), [t] + ([pv_tok[i - 2]] if i >= 2 else []))
            afree[2] = [c]
            pT_free[i] = c

        def values1(i):
            h, b, half = heads[i], i % 2, i % 2
            vv = lambda kt: vtok[:, kt, h["v"]:h["v"] + HD]
            o = A[3][half * HD:(half + 1) * HD, :]
            pe.do(lambda e: e.matmul(o[:, P:SEQ], vv(0), pT1[:, b, 0:P], start=True, stop=False), [pT_free[i]] + v_ok + afree[3], False)
            pe.do(lambda e: e.matmul(o[:, P:SEQ], vv(1), pT1[:, b, P:SEQ], start=False, stop=True), signal=False)
            t = pe.do(lambda e: e.matmul(o[:, 0:P], vv(0), pT1[:, b, SEQ:384], start=True, stop=True))
            pv_tok[i] = t
            if half:
                tile = h["out"]
                ps = REV(A[3][:, 0:SEQ].rearrange("p (b q) -> p b q", b=2))
                d = lambda x: x[:, tile, :].rearrange("p (b q) -> p b q", b=2)
                o_ok[tile] = split_out(d(oh), d(ol), ps, [t])
                afree[3] = o_ok[tile]

        sig_ok = {}

        gate_pair = [None]

        def gates(i):
            half = i % 2
            g, tok = gemm(f"gate{i}", 2, 4, src1, SEQ, lambda kt: ready[kt], gate_pair[0] if half else None, 4 * half, KT)
            gate_pair[0] = g
            if half:
                d = sig[:, i - 1:i + 1, :]
                a_ = act.do(lambda e: e.activation(d, G[g][:, :, 0:SEQ], ACT.Tanh, scale=0.5), [tok])
                gfree[g] = [a_]
                sig_ok[i // 2] = dve.do(lambda e: e.tensor_scalar(d, d, 0.5, 0.5, ALU.mult, ALU.add), [a_])

        branch_a = {}

        def branch_a_gemm(i):
            g, tok = gemm(f"bra{i}", 2, 4, lambda kt: (oh[:, kt, :], ol[:, kt, :]), SEQ, lambda kt: o_ok[kt])
            sa = sig[:, 2 * i:2 * i + 2, :]
            branch_a[i] = dve.do(lambda e: e.tensor_tensor(sa, sa, G[g][:, :, 0:SEQ], ALU.mult), [tok, sig_ok[i]])
            gfree[g] = [branch_a[i]]

        for i in range(HEADS1 + 2):
            if i < HEADS1:
                scores1(i)
                ada_piece(*ADA_HEADS[i])
                weights1(i)
                gates(i)
            else:
                branch_a_gemm(i - HEADS1)
            if 1 <= i <= HEADS1:
                transposes1(i - 1)
            if i >= 2:
                values1(i - 2)
            if i % 4 == 0 and 0 < i <= HEADS1:
                m = ada_finish(ADA_HEADS[i - 4][0])
        ada_free[ada_set(7)] = pt_tok[HEADS1 - 1]
        for i in (2, 3):
            ada_piece(*ADA_BRANCH[i - 2])
            branch_a_gemm(i)

        merged_ok, both = {}, {}
        merged = lambda kt, nt=1: (hh[:, kt * SEQ:(kt + nt) * SEQ], hh[:, (KT + kt) * SEQ:(KT + kt + nt) * SEQ])
        pair_of = lambda t: t.rearrange("p (t q) -> p t q", t=2)

        def split_merged(i):
            mh, ml = merged(2 * i, 2)
            merged_ok[2 * i] = merged_ok[2 * i + 1] = split_out(mh, ml, hidf[:, i % 2, :], [both[i]])

        for i in range(4):
            if i == 0:
                ada_piece(*ADA_BRANCH[2])
            g, tok = gemm(f"brb{i}", 2, 4, lambda kt: (oh[:, 4 + kt, :], ol[:, 4 + kt, :]), SEQ, lambda kt: o_ok[4 + kt])
            hb = pair_of(hidf[:, i % 2, :])
            b_ = dve.do(lambda e: e.tensor_tensor(hb, sig[:, 8 + 2 * i:10 + 2 * i, :], G[g][:, :, 0:SEQ], ALU.mult),
                        [tok, sig_ok[4 + i]] + (merged_ok[2 * i - 4] if i >= 2 else []))
            gfree[g] = [b_]
            if i:
                split_merged(i - 1)
            both[i] = (dve if i == 3 else pool).do(lambda e: e.tensor_tensor(hb, hb, sig[:, 2 * i:2 * i + 2, :], ALU.add), [b_, branch_a[i]])
        split_merged(3)

        def add_residual(g, tok, i, cols, scalar, hooks, after=()):
            n = cols.stop - cols.start
            fr = []
            for t in range(2):
                kt = 2 * i + t
                s_ = scalar(kt) if callable(scalar) else scalar
                fr.append(dve.do(lambda e: e.scalar_tensor_tensor(X[:, kt, cols], G[g][:, t, 0:n], s_, X[:, kt, cols],
                                                                                      ALU.mult, ALU.add), [tok] + list(after)))
                square_in(X[:, kt, cols], kt == 0, cols, [fr[-1]])
            for hook in hooks:
                for t in range(2):
                    hook(2 * i + t, fr[t])
            gfree[g] = fr
            return fr[-1]

        preload(ACT.Sqrt)
        gm2 = mod_gain(g1m[:, KT:2 * KT], "norm2_g", 4 * KT, [m])
        SHIFT = slice(META - 2, T)
        sh_cols = lambda t: t[:, :, META - 2:META]
        shift2 = mod[:, 3 * KT:4 * KT].unsqueeze(2).broadcast_to([P, KT, 2])
        ready2 = {}

        def prep2(kt, tok):
            ready2[kt] = split_out(xh[:, kt, COLS1], xl[:, kt, COLS1], X[:, kt, COLS1], [tok, gm2], scale=g1m[:, KT + kt:KT + kt + 1])
        for i in range(4):
            if i == 0:
                ada_piece(*ADA_BRANCH[3])
            g, tok = gemm(f"wout{i}", 2, KT, merged, SEQ, lambda kt: merged_ok[kt])
            if i == 1:
                m = ada_finish(7)
                shift_ok = split_out(sh_cols(xh), sh_cols(xl), shift2, [m])
            add_residual(g, tok, i, COLS1, lambda kt: mod[:, 2 * KT + kt:2 * KT + kt + 1], [prep2])

        hid_ok, hf_free, scaled, squared = {}, [[], []], {}, {}
        hf = lambda i: hidf[:, i % 2, :].rearrange("p (t q) -> p t q", t=2)

        def relu_square(i):
            for t in range(2):
                a_ = act.do(lambda e: e.activation(hf(i)[:, t, :], hf(i)[:, t, :], ACT.Relu, bias=shift_out[:, i % 2, t:t + 1]), [scaled[i]])
            squared[i] = act.do(lambda e: e.activation(hf(i), hf(i), ACT.Square), [a_])

        def split_hidden(i):
            sl = slice(2 * i * SEQ, (2 * i + 2) * SEQ)
            hid_ok[2 * i] = hid_ok[2 * i + 1] = hf_free[i % 2] = split_out(hh[:, sl], hl[:, sl], hidf[:, i % 2, :], [squared[i]])

        meta_ok = pool.do(lambda e: e.dma_start(X[:, :, 0:META], metaT), signal=(meta_in, 16))
        for i in range(FF1 // 2):
            if i % 2 == 0:
                ada_piece(*ADA_MLP[i // 2])
            g, tok = gemm(f"mlp_in{i}", 2, KT, lambda kt: (xh[:, kt, SHIFT], xl[:, kt, SHIFT]), SEQ + 2, lambda kt: ready2[kt] + shift_ok,
                          mid=(lambda: relu_square(i - 1)) if i else None)
            if i == 0:
                r = rstd_of(0, rstd, COLS1)
            if i == 7:
                m = ada_finish(10)
            b = i % 2
            rb = rstd[:, COLS1].unsqueeze(1).broadcast_to([P, 2, SEQ])
            dve.do(lambda e: e.tensor_copy(shift_out[:, b, :], G[g][:, :, 0]), [tok] + hf_free[b], False)
            scaled[i] = dve.do(lambda e: e.tensor_tensor(hf(i), G[g][:, :, 2:2 + SEQ], rb, ALU.mult), [r])
            gfree[g] = [scaled[i]]
            if i:
                split_hidden(i - 1)
        relu_square(FF1 // 2 - 1)
        split_hidden(FF1 // 2 - 1)
        hid1 = lambda kt: (hh[:, kt * SEQ:(kt + 1) * SEQ], hl[:, kt * SEQ:(kt + 1) * SEQ])
        ALL = slice(0, T)
        fgg = dve.do(lambda e: e.tensor_tensor(g1m[:, 0:KT], V("final_g", 0, KT), V("ffn1_norm0", 0, KT), ALU.mult), [ready[KT - 1][1]])
        ready3, second = {}, {}

        def prep_final(kt, tok):
            ready3[kt] = split_out(xh[:, kt, COLS1], xl[:, kt, COLS1], X[:, kt, COLS1], [tok, fgg], scale=g1m[:, kt:kt + 1]) + meta_split
            s, dst = tmp[:, kt % 2, 0:SEQ], sumsq2[:, COLS1]
            a = act.do(lambda e: e.activation(s, X[:, kt, COLS1], ACT.Square, scale=V("final_g", kt)), [tok, second.get(kt - 2)])
            if kt == 0:
                second[kt] = pool.do(lambda e: e.tensor_copy(dst, s), [a])
            else:
                second[kt] = pool.do(lambda e: e.tensor_tensor(dst, dst, s, ALU.add), [a, second[kt - 1]])

        for i in range(4):
            g, tok = gemm(f"mlp_out{i}", 2, FF1, hid1, SEQ, lambda kt: hid_ok[kt])
            if i == 0:
                m = ada_finish(11)
                mx, mg = X[:, :, 0:META], V("ffn1_norm0", 0, KT).unsqueeze(2).broadcast_to([P, KT, META])
                scaled_m, squares_m = (hidf[:, 0, n * P:(n + 1) * P].rearrange("p (k t) -> p k t", k=KT) for n in range(2))
                a_ = dve.do(lambda e: e.tensor_tensor(scaled_m, mx, mg, ALU.mult), [meta_ok] + hf_free[0])
                meta_split = split_out(xh[:, :, 0:META], xl[:, :, 0:META], scaled_m, [a_])
                a_ = dve.do(lambda e: e.tensor_tensor(squares_m, mx, mx, ALU.mult))
                meta_sq = dve.do(lambda e: e.tensor_reduce(sumsq2[:, 0:META], squares_m.rearrange("p k t -> p t k"), AX_X, ALU.add), [a_])
            add_residual(g, tok, i, COLS1, lambda kt: mod[:, 5 * KT + kt:5 * KT + kt + 1], [prep_final], [m])

        final_r = {}

        def final_factor():
            t1 = pe.do(lambda e: e.matmul(A[0][:, 0:SEQ], mean_ones[:, 0, :], sumsq[:, COLS1], start=True, stop=True), [sq_state["tok"]] + afree[0])
            t2 = pe.do(lambda e: e.matmul(A[3][:, 0:T], mean_ones[:, 0, :], sumsq2[:, :], start=True, stop=True), [second[KT - 1], meta_sq] + afree[3])
            sq_state["used"] = t1
            v = dve.do(lambda e: e.tensor_scalar(rstd2[:, COLS1], A[0][:, 0:SEQ], EPS, None, ALU.add), [t1])
            m2 = dve.do(lambda e: e.tensor_scalar(rstd[:, 0:META], A[3][:, 0:META], EPS, None, ALU.add), [t2])
            m1 = dve.do(lambda e: e.scalar_tensor_tensor(rstd[:, COLS1], rstd2[:, COLS1], EPS, A[3][:, COLS1], ALU.mult, ALU.add), [v])
            afree[0], afree[3] = [v], [m1]
            q = act.do(lambda e: e.activation(root[:, :], rstd[:, :], ACT.Sqrt), [m1])
            q2 = act.do(lambda e: e.activation(sumsq[:, COLS1], rstd2[:, COLS1], ACT.Sqrt), [v])
            both_ok = dve.do(lambda e: e.reciprocal(rstd[:, :], root[:, :]), [q])
            final_r["own"] = dve.do(lambda e: e.reciprocal(rstd2[:, COLS1], sumsq[:, COLS1]), [q2])
            return both_ok

        def final_x():
            for kt in range(KT):
                dve.do(lambda e: e.scalar_tensor_tensor(X[:, kt, COLS1], X[:, kt, COLS1], V("final_g", kt), rstd2[:, COLS1], ALU.mult, ALU.mult),
                       [final_r["own"]])

        full = lambda t: (lambda kt: t[:, kt, :])

        def swiglu(f_, layer, ready, cols, hooks, between=None, factor=None, gu_after=(), order=None, each=None):
            n = cols.stop - cols.start
            rs = {}
            hid_ok, h_free, gu_free = {}, [[], []], [list(gu_after), list(gu_after)]
            src = lambda kt: (xh[:, kt, cols], xl[:, kt, cols])
            rb = rstd[:, cols].unsqueeze(1).broadcast_to([P, 2, n])

            def factor_now():
                rs["ok"] = factor() if factor else rstd_of(0, rstd, cols)
                preload(ACT.Silu)

            def leave(j, g, tok):
                b = j % 2
                if g is None:
                    for t in range(2):
                        a_ = dve.do(lambda e: e.tensor_tensor(gu[:, b, t, 0:n], A[1 + t][:, 0:n], rstd[:, cols], ALU.mult),
                                    [tok, rs["ok"]] + gu_free[b])
                        afree[1 + t] = [a_]
                else:
                    a_ = dve.do(lambda e: e.tensor_tensor(gu[:, b, :, 0:n], G[g][:, :, 0:n], rb, ALU.mult),
                                [tok, rs["ok"]] + gu_free[b])
                    gfree[g] = [a_]
                s_ = act.do(lambda e: e.activation(gu[:, b, 0, 0:n], gu[:, b, 0, 0:n], ACT.Silu), [a_])
                c_ = dve.do(lambda e: e.tensor_tensor(hidf[:, b, 0:n], gu[:, b, 0, 0:n], gu[:, b, 1, 0:n], ALU.mult),
                            [s_] + h_free[b])
                gu_free[b] = [c_]
                sl = slice(j * n, (j + 1) * n)
                hid_ok[j] = split_out(hh[:, sl], hl[:, sl], hidf[:, b, 0:n], [c_])
                h_free[b] = hid_ok[j]

            second, tok = gemm(f"{f_}_{layer}_gu01", 4, KT, src, n, lambda kt: ready[kt], mid=None if each else factor_now, order=order, each=each)
            if each:
                factor_now()
            g2, tok2 = gemm(f"{f_}_{layer}_gu2", 2, KT, src, n, lambda kt: ready[kt])
            for j in range(FF2):
                if j < 3:
                    leave(j, (None, second, g2)[j], (tok, tok, tok2)[j])
                else:
                    g, tok = gemm(f"{f_}_{layer}_gu{j}", 2, KT, src, n, lambda kt: ready[kt])
                    leave(j, g, tok)
                if between and j == 3:
                    between()
            preload(ACT.Sqrt)
            hid = lambda kt: (hh[:, kt * n:(kt + 1) * n], hl[:, kt * n:(kt + 1) * n])
            for i in range(4):
                g, tok = gemm(f"{f_}_{layer}_down{i}", 2, FF2, hid, n, lambda kt: hid_ok[kt])
                last = add_residual(g, tok, i, cols, 0.5, hooks)
            return last

        for gi, w in enumerate(POOL_W):
            scale_w_ok = dve.do(lambda e: e.tensor_scalar(scale_w[:, 2 * gi:2 * gi + 2], V("pool_scale", 2 * gi, 2), 1.0 / w, None, ALU.mult))
        mix0_ready, prep_mix0 = norm_input(full(xh), full(xl), "mix_norm0", ALL)
        swiglu("ffn1", 0, ready3, ALL, [prep_mix0], final_x, final_factor)

        body = slice(PADC, PADC + T)
        mix_gemm = lambda gi, **kw: gemm(f"pool{gi}", 2, 2, lambda kt: (xh[:, 2 * gi + kt, :], xl[:, 2 * gi + kt, :]), T,
                                         lambda kt: mix0_ready[2 * gi + kt], **kw)
        rb = rstd[:, :].unsqueeze(1).broadcast_to([P, 2, T])
        z_ok, x_less = {}, {}
        g0, t0 = mix_gemm(0)
        pad_t = pool.do(lambda e: e.memset(U[:, :, 0:PADC], 0.0), [t0])
        g1, t1 = mix_gemm(1)
        _, t2 = mix_gemm(2, banks=(1, 2))
        r = rstd_of(0, rstd, ALL)
        z_ok[0] = dve.do(lambda e: e.tensor_tensor(U[:, 0:2, body], G[g0][:, :, 0:T], rb, ALU.mult), [t0, r])
        gfree[g0] = [z_ok[0]]
        g3, t3 = mix_gemm(3)
        z_ok[1] = dve.do(lambda e: e.tensor_tensor(U[:, 2:4, body], G[g1][:, :, 0:T], rb, ALU.mult), [t1])
        gfree[g1] = [z_ok[1]]
        for n in range(2):
            z_ok[2] = dve.do(lambda e: e.tensor_tensor(U[:, 4 + n, body], A[1 + n][:, 0:T], rstd[:, :], ALU.mult), [t2])
            afree[1 + n] = [z_ok[2]]
        ready4, prep = norm_input(full(xh), full(xl), "ffn2_norm0", ALL)

        scaled_z = [gu[:, n // 2, n % 2, :] for n in range(4)] + [tmp[:, n, :] for n in range(2)] + [sq[:, n, :] for n in range(2)]

        def minus_z(kts):
            for kt in kts:
                a_ = act.do(lambda e: e.activation(scaled_z[kt], U[:, kt, body], ACT.Copy, scale=V("pool_scale", kt)), [z_ok[kt // 2], sq_state["tok"]])
                x_less[kt] = pool.do(lambda e: e.tensor_tensor(X[:, kt, :], X[:, kt, :], scaled_z[kt], ALU.subtract), [a_])

        def windows(gi, eng):
            ks = slice(2 * gi, 2 * gi + 2)
            cur, lo_, deps = U, 1, [z_ok[gi], pad_t]
            for st in range(gi + 1):
                sh, dst = 1 << st, (SA, SB_)[st % 2]
                t = eng.do(lambda e: e.tensor_tensor(dst[:, ks, lo_:PADC + T], cur[:, ks, lo_:PADC + T], cur[:, ks, lo_ - sh:PADC + T - sh], ALU.add), deps)
                deps, cur, lo_ = [t], dst, lo_ + 2 * sh
            w = POOL_W[gi]
            fix = con[:, cat["count_fix"] + gi * PADC:cat["count_fix"] + gi * PADC + w].unsqueeze(1).broadcast_to([P, 2, w])
            return cur, eng.do(lambda e: e.tensor_tensor(cur[:, ks, PADC:PADC + w], cur[:, ks, PADC:PADC + w], fix, ALU.mult), [t, con_ok])

        squared_ok = {}

        def finish(gi, cur, t):
            a_ = [dve.do(lambda e: e.scalar_tensor_tensor(X[:, kt, :], cur[:, kt, body], scale_w[:, kt:kt + 1], X[:, kt, :], ALU.mult, ALU.add),
                         [t, x_less[kt], scale_w_ok]) for kt in (2 * gi, 2 * gi + 1)]
            for n in range(2):
                prep(2 * gi + n, a_[n])
            for n in range(2):
                kt = 2 * gi + n
                squared_ok[kt] = act.do(lambda e: e.activation(U[:, kt, body], X[:, kt, :], ACT.Square), [a_[n]])

        minus_z((0, 1, 2, 3))
        finish(0, *windows(0, dve))
        z_ok[3] = dve.do(lambda e: e.tensor_tensor(U[:, 6:8, body], G[g3][:, :, 0:T], rb, ALU.mult), [t3])
        gfree[g3] = [z_ok[3]]
        minus_z((6, 7))
        w2 = windows(2, pool)
        minus_z((4, 5))
        finish(1, *windows(1, dve))
        finish(3, *windows(3, dve))
        finish(2, *w2)

        def mean_square(step):
            kt = POOL_KT[step]
            squared_ok["sum"] = pe.do(lambda e: e.matmul(A[0][:, 0:T], mean_ones[:, 0, :], U[:, kt, body], start=step == 0, stop=step == KT - 1),
                                      [squared_ok[kt]] + afree[0])

        def pool_factor():
            mean_square(KT - 1)
            q = act.do(lambda e: e.activation(root[:, :], A[0][:, 0:T], ACT.Sqrt, bias=eps_c[:, 0:1]), [squared_ok["sum"]])
            afree[0] = [q]
            return dve.do(lambda e: e.reciprocal(rstd[:, :], root[:, :]), [q])

        kv_ready, prep_kv = norm_input(lambda kt: hh[:, kvx + kt * T:kvx + (kt + 1) * T], lambda kt: hl[:, kvx + kt * T:kvx + (kt + 1) * T],
                                       "kv_in_norm", ALL)
        ready5, prep5 = norm_input(full(xh), full(xl), "ffn1_norm1", ALL)
        swiglu("ffn2", 0, ready4, ALL, [prep_kv, prep5], factor=pool_factor, order=POOL_KT,
               each=lambda step: mean_square(step - 1) if step else None)

        kvsrc = lambda kt: (hh[:, kvx + kt * T:kvx + (kt + 1) * T], hl[:, kvx + kt * T:kvx + (kt + 1) * T])
        g, tok = gemm("ckv", 2, KT, kvsrc, T, lambda kt: kv_ready[kt])
        rs1 = rstd_of(0, rstd, ALL)
        rb = rstd[:, :].unsqueeze(1).broadcast_to([P, 2, T])
        ck = dve.do(lambda e: e.tensor_tensor(gu[:, 0, :, :], G[g][:, :, 0:T], rb, ALU.mult), [tok, rs1])
        gfree[g] = [ck]
        g, tok = gemm("krope", 1, KT, kvsrc, T, lambda kt: kv_ready[kt])
        for kt in range(KVR):
            square_in(gu[:, 0, kt, :], kt == 0, ALL, [ck])
        ka_ = dve.do(lambda e: e.tensor_tensor(tmp[0:64, 0, :], G[g][0:64, 0, 0:T], rstd[0:64, :], ALU.mult), [tok, rs1])
        gfree[g] = [ka_]
        cosT, sinT = (lambda r0, r1, c: con[r0:r1, cat["cos"] + c.start:cat["cos"] + c.stop]), (lambda r0, r1, c: con[r0:r1, cat["sin"] + c.start:cat["sin"] + c.stop])
        kb_ = dve.do(lambda e: e.tensor_tensor(krot[:, :], tmp[0:32, 0, :], cosT(0, 32, ALL), ALU.mult), [ka_])
        kc_ = dve.do(lambda e: e.tensor_tensor(tmp[0:32, 1, :], tmp[32:64, 0, :], sinT(32, 64, ALL), ALU.mult), [kb_])
        kd_ = dve.do(lambda e: e.tensor_tensor(krot[:, :], krot[:, :], tmp[0:32, 1, :], ALU.add), [kc_])
        kr_ok = dve.do(lambda e: e.tensor_copy(khead[HD:QK, :, :], krot[:, :].unsqueeze(1).broadcast_to([ROPE, MH, T])), [kd_])
        kv_done = {}

        def kv_norm():
            rk = rstd_of(1, rstd2, ALL)
            for kt in range(KVR):
                t = dve.do(lambda e: e.scalar_tensor_tensor(tmp[:, kt, :], ckvf[:, kt, :], V("kv_latent_norm", kt), rstd2[:, :],
                                                                         ALU.mult, ALU.mult), [rk, cc, kd_])
                c0 = kvx + kt * T
                kv_done[kt] = split_out(hh[:, c0:c0 + T], hl[:, c0:c0 + T], tmp[:, kt, :], [t, tok])
            return rs1

        def kv_up():
            lat = lambda kt: (hh[:, kvx + kt * T:kvx + (kt + 1) * T], hl[:, kvx + kt * T:kvx + (kt + 1) * T])
            ks = []
            for i in range(2):
                g_, tk = gemm(f"uk{i}", 2, KVR, lat, T, lambda kt: kv_done[kt])
                a_ = act.do(lambda e: e.activation(khead[0:HD, 4 * i:4 * i + 4:2, :], G[g_][0:HD, :, 0:T], ACT.Copy), [tk])
                b_ = dve.do(lambda e: e.tensor_copy(khead[0:HD, 4 * i + 1:4 * i + 4:2, :], G[g_][HD:P, :, 0:T]), [tk, a_])
                gfree[g_] = [a_, b_]
                ks += [a_, b_]
            lat_t = lambda kt, a, m_: (hh[:, kvx + kt * T + a:kvx + kt * T + a + m_], hl[:, kvx + kt * T + a:kvx + kt * T + a + m_])
            g_, tk = token_major("uv", 4 * P, KVR, lat_t, [(0, P), (P, P)], False)
            a_ = act.do(lambda e: e.activation(v2[:, 0, :], G[g_][:, 0, :], ACT.Copy), [tk])
            b_ = dve.do(lambda e: e.tensor_copy(v2[:, 1, :], G[g_][:, 1, :]), [tk])
            gfree[g_] = [a_, b_]
            g2, tk = token_major("uv", 4 * P, KVR, lat_t, [(2 * P, META)], True)
            c_ = act.do(lambda e: e.activation(v2[0:META, 2, :], G[g2][0:META, 0, :], ACT.Copy), [tk])
            gfree[g2] = [c_]
            kv_done["k"], kv_done["v"] = ks + [kr_ok], [a_, b_, c_]

        cc = pool.do(lambda e: e.tensor_copy(ckvf[:, :, :], gu[:, 0, :, :]), [ck])
        mix_ready, prep_mix = norm_input(lambda kt: xh[:, kt, COLS1], lambda kt: xl[:, kt, COLS1], "mix_norm1", COLS1)


        swiglu("ffn1", 1, ready5, COLS1, [prep_mix], kv_up, kv_norm, [cc])

        g, tok = gemm("dq0", 2, KT, src1, SEQ, lambda kt: mix_ready[kt])
        cq_ok, cq_sq, q_ok = {}, {}, {}

        def latent_out(kt, ps, tok):
            th = act.do(lambda e: e.activation(cqh[:, kt, :], ps, ACT.Identity, scale=V("q_latent_norm", kt)), [tok])
            cq_sq[kt] = act.do(lambda e: e.activation(cqf[:, kt, :], ps, ACT.Square))
            tl = dve.do(lambda e: e.scalar_tensor_tensor(cql[:, kt, :], ps, V("q_latent_norm", kt), f(cqh[:, kt, :]), ALU.mult, ALU.subtract), [cq_sq[kt]])
            cq_ok[kt] = [th, tl]
            return tl

        gfree[g] = [latent_out(kt, G[g][:, kt, 0:SEQ], tok) for kt in range(2)]
        g, tok = gemm("dq1", 1, KT, src1, SEQ, lambda kt: mix_ready[kt])
        gfree[g] = [latent_out(2, G[g][:, 0, 0:SEQ], tok)]
        mx = pe.do(lambda e: e.matmul(A[0][:, 0:SEQ], mean_ones[:, 0, :], sumsq[:, COLS1], start=True, stop=True), [sq_state["tok"]] + afree[0])
        sq_state["used"] = mx
        v = dve.do(lambda e: e.tensor_scalar(root[:, COLS1], A[0][:, 0:SEQ], EPS, EPS, ALU.add, ALU.mult), [mx])
        afree[0] = [v]

        def latent_factor():
            for kt in range(QR):
                t = pe.do(lambda e: e.matmul(A[1][:, 0:SEQ], mean_ones[:, 2, :], cqf[:, kt, :], start=kt == 0, stop=kt == QR - 1),
                          [cq_sq[kt]] + afree[1], None if kt == QR - 1 else False)
            t = dve.do(lambda e: e.tensor_tensor(root[:, COLS1], root[:, COLS1], A[1][:, 0:SEQ], ALU.add), [t, v])
            afree[1] = [t]
            t = act.do(lambda e: e.activation(root[:, COLS1], root[:, COLS1], ACT.Sqrt), [t])
            preload(ACT.Exp)
            rq = dve.do(lambda e: e.reciprocal(rstd2[:, COLS1], root[:, COLS1]), [t])
            ra = dve.do(lambda e: e.tensor_tensor(gu[:, 0, 0, 0:SEQ], rstd2[:, COLS1], cosT(0, P, COLS1), ALU.mult), [rq])
            rb_ = dve.do(lambda e: e.tensor_tensor(gu[:, 0, 1, 0:SEQ], rstd2[:, COLS1], sinT(0, P, COLS1), ALU.mult), [rq])
            return rq, ra, rb_

        cqs = lambda kt: (cqh[:, kt, :], cql[:, kt, :])
        r64 = lambda lo_: rstd2[lo_:lo_ + HD, COLS1].unsqueeze(1).broadcast_to([HD, 2, SEQ])
        turned = []
        for i in range(2):
            g, tok = gemm(f"uqn{i}", 2, QR, cqs, SEQ, lambda kt: cq_ok[kt])
            if i == 0:
                rq, ra, rb_ = latent_factor()
            a_ = dve.do(lambda e: e.tensor_tensor(qhead[0:HD, 4 * i:4 * i + 4:2, :], G[g][0:HD, :, 0:SEQ], r64(0), ALU.mult), [tok, rq])
            b_ = dve.do(lambda e: e.tensor_tensor(qhead[0:HD, 4 * i + 1:4 * i + 4:2, :], G[g][HD:P, :, 0:SEQ], r64(HD), ALU.mult), [tok, rq])
            gfree[g] = [a_, b_]
            g, tok = gemm(f"uqr{i}", 2, QR, cqs, SEQ, lambda kt: cq_ok[kt])
            c_ = dve.do(lambda e: e.tensor_tensor(gu[:, 1, :, 0:SEQ], G[g][:, :, 0:SEQ], gu[:, 0, :, 0:SEQ], ALU.mult), [tok, ra, rb_] + turned)
            gfree[g] = [c_]
            turned = []
            for n in range(4):
                t = dve.do(lambda e: e.tensor_tensor(qhead[HD:QK, 4 * i + n, :], gu[n * ROPE:(n + 1) * ROPE, 1, 0, 0:SEQ],
                                                     gu[n * ROPE:(n + 1) * ROPE, 1, 1, 0:SEQ], ALU.add), [c_])
                turned.append(t)
                q_ok[4 * i + n] = [a_ if n % 2 == 0 else b_, t]

        KW = (META + P, T)
        OFF = (T, 0)
        mask = lambda w: con[:, cat["mla_mask"] + T - w:cat["mla_mask"] + T]
        s2, e2, pt2, pv2, o2_ok, ptc = {}, {}, {}, {}, {}, {}

        def scores2(i):
            bank, b = A[i % 2], i % 3
            for n in (1, 0):
                t = pe.do(lambda e: e.matmul(bank[:, OFF[n]:OFF[n] + KW[n]], qhead[:, i, n * P:(n + 1) * P], khead[:, i, 0:KW[n]],
                                                         start=True, stop=True), q_ok[i] + kv_done["k"] + afree[i % 2], None if n == 0 else False)
            w = [t] + ([e2[i - 3]] if i >= 3 else [])
            for n in (1, 0):
                t = dve.do(lambda e: e.scalar_tensor_tensor(sc2[:, b, OFF[n]:OFF[n] + KW[n]], bank[:, OFF[n]:OFF[n] + KW[n]],
                                                                        1.0 / math.sqrt(QK), mask(KW[n]), ALU.mult, ALU.add), w)
            afree[i % 2] = [t]
            st = stat[:, i % 4, :]
            for n in (1, 0):
                t = dve.do(lambda e: e.tensor_reduce(st[:, n:n + 1], sc2[:, b, OFF[n]:OFF[n] + KW[n]], AX_X, ALU.max, negate=True), [t])
            for n in (1, 0):
                u = act.do(lambda e: e.activation(p2[:, b, OFF[n]:OFF[n] + KW[n]], sc2[:, b, OFF[n]:OFF[n] + KW[n]], ACT.Exp,
                                                              bias=st[:, n:n + 1], accum_out=st[:, 2 + n:3 + n]), [t] + ([pt2[i - 3]] if i >= 3 else []))
            e2[i] = u
            u = dve.do(lambda e: e.reciprocal(st[:, 4:6], st[:, 2:4]), [u])
            for n in (1, 0):
                s2[i] = pool.do(lambda e: e.tensor_scalar(p2[:, b, OFF[n]:OFF[n] + KW[n]], p2[:, b, OFF[n]:OFF[n] + KW[n]],
                                                                     st[:, 4 + n:5 + n], None, ALU.mult), [u])

        def transposes2(i):
            b, bp = i % 2, i % 3
            waits = [s2[i]] + afree[2] + gfree[1] + gfree[0]
            for j, c0 in enumerate((0, P, T)):
                pe.do(lambda e: e.transpose(A[2][:, j * P:(j + 1) * P], p2[:, bp, c0:c0 + P], ident), waits, False)
            for j, c0 in enumerate((2 * P, T + P)):
                t = pe.do(lambda e: e.transpose(G[1][0:META, 0, j * P:(j + 1) * P], p2[:, bp, c0:c0 + META], ident),
                          signal=None if j else False)
            pt2[i] = t
            a_ = act.do(lambda e: e.activation(pT2[:, b, :], A[2][:, 0:384], ACT.Copy), [t] + ([pv2[i - 2]] if i >= 2 else []))
            b_ = dve.do(lambda e: e.tensor_copy(pT2m[:, b, :], G[1][0:META, 0, 0:SEQ]), [t] + ([pv2[i - 2]] if i >= 2 else []))
            afree[2], gfree[1] = [a_], [b_]
            ptc[i] = [a_, b_]

        def values2(i):
            b, half = i % 2, i % 2
            vv = lambda kt, m_: v2[0:m_, kt, i * HD:(i + 1) * HD]
            o = A[3][half * HD:(half + 1) * HD, :]
            mm = lambda out, a, c, s0, s1: (lambda e: e.matmul(out, a, c, start=s0, stop=s1))
            pe.do(mm(o[:, P:SEQ], vv(0, P), pT2[:, b, 0:P], True, False), ptc[i] + kv_done["v"] + afree[3], False)
            pe.do(mm(o[:, P:SEQ], vv(1, P), pT2[:, b, P:SEQ], False, False), signal=False)
            pe.do(mm(o[:, P:SEQ], vv(2, META), pT2m[:, b, 0:P], False, True), signal=False)
            pe.do(mm(o[:, 0:P], vv(0, P), pT2[:, b, SEQ:384], True, False), signal=False)
            pv2[i] = pe.do(mm(o[:, 0:P], v2[0:META, 1, i * HD:(i + 1) * HD], pT2m[:, b, P:SEQ], False, True))
            if half:
                o2_ok[i // 2] = split_out(o2h[:, i // 2, :], o2l[:, i // 2, :], A[3][:, 0:SEQ], [pv2[i]])
                afree[3] = o2_ok[i // 2]

        for i in range(MH + 3):
            if i < MH:
                scores2(i)
            if 2 <= i < MH + 2:
                transposes2(i - 2)
            if i >= 3:
                values2(i - 3)
        afree[0] = afree[0] + afree[1]

        preload(ACT.Sqrt)
        ready6, prep = norm_input(lambda kt: xh[:, kt, COLS1], lambda kt: xl[:, kt, COLS1], "ffn2_norm1", COLS1)
        for i in range(4):
            g, tok = gemm(f"wo{i}", 2, 4, lambda kt: (o2h[:, kt, :], o2l[:, kt, :]), SEQ, lambda kt: o2_ok[kt])
            add_residual(g, tok, i, COLS1, 1.0, [prep])
        swiglu("ffn2", 1, ready6, COLS1, [])

        r = rstd_of(0, rstd, COLS1)
        for kt in range(KT):
            t = dve.do(lambda e: e.scalar_tensor_tensor(X[:, kt, COLS1], X[:, kt, COLS1], V("final_norm", kt), rstd[:, COLS1],
                                                                     ALU.mult, ALU.mult), [r, sq_state["tok"]])
            if kt % 2:
                st_ = sp.do(lambda e: e.dma_start(outT[:, kt - 1:kt + 1, :], X[:, kt - 1:kt + 1, COLS1]), [t], (stored, 16))

        nc.sync.wait_ge(stored.sem, stored.value)


def _features(v):
    return np.ascontiguousarray(np.asarray(v).reshape(-1, P).T)


def kernel(**inputs):
    import concourse.bacc as _bacc
    from concourse.bass_utils import run_bass_kernel_spmd as _run

    a = {k: np.asarray(v) for k, v in inputs.items()}
    chunks, _ = weight_plan()
    wstream = np.zeros((len(chunks), P, CH * P), np.float32)
    for c, blocks in enumerate(chunks):
        for off, (name, layer, rows, cols) in enumerate(blocks):
            w = a[name]
            if name == "pool_w_2":
                w = w[0, layer]
            elif layer is not None:
                w = w[layer]
            wstream[c, :, off * P:(off + 1) * P] = w[np.ix_(rows, cols)]
    vat, vn = vector_plan()
    parts = {
        "c": a["c"], "ada_b": a["ada_b"], "norm1_g": a["norm1_g"], "norm2_g": a["norm2_g"], "final_g": a["final_g"],
        "pool_scale": a["pool_scale_2"], "kv_in_norm": a["kv_in_norm_2"], "final_norm": a["final_norm_2"],
        "kv_latent_norm": a["kv_latent_norm_2"], "q_latent_norm": a["q_latent_norm_2"],
    }
    for n in ("ffn1_norm", "mix_norm", "ffn2_norm"):
        for l in range(2):
            parts[f"{n}{l}"] = a[n + "_2"][l]
    vecs = np.zeros((P, vn), np.float32)
    for n, v in parts.items():
        w = _features(v)
        vecs[:, vat[n]:vat[n] + w.shape[1]] = w
    vecs[:, vat["sinks"]:vat["sinks"] + SWA_HEADS] = np.broadcast_to(a["attn_sinks"].reshape(1, -1), (P, SWA_HEADS))
    bias_oh, sel = bias_constants()
    feature_major = lambda v: np.ascontiguousarray(v.T.reshape(KT, P, -1).transpose(1, 0, 2))
    arrays = {
        "in_xT": feature_major(a["x"][0]), "in_metaT": feature_major(a["meta_tokens_2"]), "in_vecs": vecs,
        "in_consts": constants(), "in_bias_oh": bias_oh,
        "in_bias_rows": np.concatenate([a["rel_bias"], sel]), "in_wstream": wstream,
    }
    nc = _bacc.Bacc("TRN2", target_bir_lowering=False, num_devices=1)
    aps = [nc.dram_tensor(n, v.shape, F32, kind="ExternalInput").ap() for n, v in arrays.items()]
    scratch = nc.dram_tensor("bias_scratch", (HEADS1, 512), F32).ap()
    out = nc.dram_tensor("out_T", (P, KT, SEQ), F32, kind="ExternalOutput").ap()
    build_program(nc, *aps, scratch, out)
    r = _run(nc, [arrays], core_ids=[0])
    got = r.results[0]["out_T"]
    return np.ascontiguousarray(got.transpose(1, 0, 2).reshape(D, SEQ).T.reshape(1, SEQ, D))
```
